# Optimizing a Trainium2 kernel written in Bass

```python
import math
import numpy as np
import jax, jax.numpy as jnp
from jax import lax

D_MODEL = 1024
BATCH = 1
SEQ = 512
DEPTH = 1

D_MIX = D_MODEL
D_PLE = 256
DA = D_MIX // 2
HA = 4
DA_V = DA // HA
DA_QK = DA_V // 2
DB = D_MIX - DA
HB = 16
DB_H = DB // HB
D_IN = 3 * DA + 3 * DB
GRID_W = 64
WIN_R = 8
WIN_C = 16
Q_COLS = 16
K_COLS = 32
ROPE_THETA = 10000.0
EPS = 1e-6
Q_BLOCK = 128
NEG = -1e30
N_GROUPS = 4
EXPERTS_PER_GROUP = 8
N_EXPERTS = N_GROUPS * EXPERTS_PER_GROUP
TOP_K = 2
D_EXPERT = 512
MOE_BLOCK = 128


def rms_norm(x, g):
    xf = x.astype(jnp.float32)
    y = xf * lax.rsqrt(jnp.mean(xf * xf, axis=-1, keepdims=True) + EPS)
    return (y * g.astype(jnp.float32)).astype(x.dtype)

def rope_tables(seq, dim):
    inv = ROPE_THETA ** (-jnp.arange(0, dim, 2, dtype=jnp.float32) / dim)
    ang = jnp.arange(seq, dtype=jnp.float32)[:, None] * inv[None, :]
    return jnp.cos(ang), jnp.sin(ang)

def apply_rope(x, cos, sin):
    s = x.shape[1]
    bshape = (s,) + (1,) * (x.ndim - 3) + (-1,)
    c = cos.reshape(bshape)
    sn = sin.reshape(bshape)
    x1, x2 = jnp.split(x.astype(jnp.float32), 2, axis=-1)
    return jnp.concatenate([x1 * c - x2 * sn, x2 * c + x1 * sn], axis=-1).astype(x.dtype)

def diff_attention(q, k, v, g_q, g_k, lam_q1, lam_k1, lam_q2, lam_k2, g_sub, lam_init):
    b, s = q.shape[:2]
    cos, sin = rope_tables(s, DA_QK)
    q = apply_rope(rms_norm(q, g_q), cos, sin)
    k = apply_rope(rms_norm(k, g_k), cos, sin)
    lam = (jnp.exp(jnp.sum(lam_q1.astype(jnp.float32) * lam_k1.astype(jnp.float32)))
           - jnp.exp(jnp.sum(lam_q2.astype(jnp.float32) * lam_k2.astype(jnp.float32)))
           + lam_init)
    scale = DA_QK ** -0.5
    qt = q.transpose(0, 2, 1, 3, 4)
    kt = k.transpose(0, 2, 1, 3, 4)
    vt = v.transpose(0, 2, 1, 3)
    k1, k2 = kt[..., 0, :], kt[..., 1, :]
    nqb = s // Q_BLOCK
    qb = qt.reshape(b, HA, nqb, Q_BLOCK, 2, DA_QK).transpose(2, 0, 1, 3, 4, 5)

    def block(qblk):
        s1 = jnp.einsum('bhqd,bhkd->bhqk', qblk[..., 0, :], k1).astype(jnp.float32) * scale
        s2 = jnp.einsum('bhqd,bhkd->bhqk', qblk[..., 1, :], k2).astype(jnp.float32) * scale
        w = (jax.nn.softmax(s1, axis=-1) - lam * jax.nn.softmax(s2, axis=-1)).astype(vt.dtype)
        return jnp.einsum('bhqk,bhkd->bhqd', w, vt)

    o = lax.map(block, qb)
    o = o.transpose(1, 0, 3, 2, 4).reshape(b, s, HA, DA_V)
    o = rms_norm(o, g_sub) * (1.0 - lam_init)
    return o.reshape(b, s, HA * DA_V)

def neighbourhood_attention(q, k, v, g_q, g_k, rpb):
    b, s, h, d = q.shape
    rows = s // GRID_W
    kr = min(WIN_R, rows)
    ncb = GRID_W // Q_COLS
    q = rms_norm(q, g_q)
    k = rms_norm(k, g_k)
    r = np.arange(rows)
    rs = np.clip(r - kr // 2, 0, rows - kr)
    key_rows = rs[:, None] + np.arange(kr)[None, :]
    row_off = (key_rows - r[:, None] + (WIN_R - 1)).astype(np.int32)
    c = np.arange(GRID_W).reshape(ncb, Q_COLS)
    cs = np.clip(c - WIN_C // 2, 0, GRID_W - WIN_C)
    kb = np.minimum(cs[:, 0], GRID_W - K_COLS)
    key_cols = kb[:, None] + np.arange(K_COLS)[None, :]
    col_valid = ((key_cols[:, None, :] >= cs[:, :, None])
                 & (key_cols[:, None, :] < cs[:, :, None] + WIN_C))
    col_off = np.clip(key_cols[:, None, :] - c[:, :, None] + (WIN_C - 1), 0, 2 * WIN_C - 2)
    key_idx = (key_rows[:, None, :, None] * GRID_W + key_cols[None, :, None, :])
    key_idx = key_idx.reshape(rows, ncb * kr * K_COLS).astype(np.int32)
    bias_cols = rpb.astype(jnp.float32)[:, :, col_off]
    bias_cols = jnp.where(col_valid, bias_cols, NEG)
    scale = d ** -0.5
    q_rows = q.reshape(b, rows, GRID_W, h, d).transpose(1, 0, 2, 3, 4)

    def row_step(args):
        q_row, idx, roff = args
        qb = q_row.reshape(b, ncb, Q_COLS, h, d)
        kg = k[:, idx].reshape(b, ncb, kr * K_COLS, h, d)
        vg = v[:, idx].reshape(b, ncb, kr * K_COLS, h, d)
        bias = bias_cols[:, roff]
        bias = bias.transpose(0, 2, 3, 1, 4).reshape(h, ncb, Q_COLS, kr * K_COLS)
        sc = jnp.einsum('bjqhd,bjkhd->bhjqk', qb, kg).astype(jnp.float32) * scale + bias
        pr = jax.nn.softmax(sc, axis=-1).astype(vg.dtype)
        o = jnp.einsum('bhjqk,bjkhd->bjqhd', pr, vg)
        return o.reshape(b, GRID_W, h, d)

    o = lax.map(row_step, (q_rows, jnp.asarray(key_idx), jnp.asarray(row_off)))
    return o.transpose(1, 0, 2, 3, 4).reshape(b, s, h * d)

def hier_moe(x, w_rg, w_re, w1, w3, w2):
    b, s, dm = x.shape
    t = b * s
    xf = x.reshape(t, dm)
    g_prob = jax.nn.softmax((xf @ w_rg).astype(jnp.float32), axis=-1)
    g_gate, g_idx = lax.top_k(g_prob, 1)
    e_logits = (xf @ w_re).astype(jnp.float32).reshape(t, N_GROUPS, EXPERTS_PER_GROUP)
    e_logits = jnp.take_along_axis(e_logits, g_idx[:, :, None], axis=1)[:, 0]
    e_w, e_i = lax.top_k(jax.nn.softmax(e_logits, axis=-1), TOP_K)
    weights = g_gate * (e_w / jnp.sum(e_w, axis=-1, keepdims=True))
    experts = (g_idx * EXPERTS_PER_GROUP + e_i).astype(jnp.int32)
    n = t * TOP_K
    slot_e = experts.reshape(n)
    slot_tok = jnp.repeat(jnp.arange(t, dtype=jnp.int32), TOP_K)
    slot_w = weights.reshape(n)
    order = jnp.argsort(slot_e)
    se = slot_e[order]
    counts = jnp.zeros((N_EXPERTS,), jnp.int32).at[slot_e].add(1)
    starts = jnp.cumsum(counts) - counts
    padded = (counts + MOE_BLOCK - 1) // MOE_BLOCK * MOE_BLOCK
    pad_end = jnp.cumsum(padded)
    pad_start = pad_end - padded
    dest = pad_start[se] + jnp.arange(n, dtype=jnp.int32) - starts[se]
    n_blocks = n // MOE_BLOCK + N_EXPERTS
    p_len = n_blocks * MOE_BLOCK
    pad_tok = jnp.full((p_len,), t, jnp.int32).at[dest].set(slot_tok[order])
    pad_w = jnp.zeros((p_len,), jnp.float32).at[dest].set(slot_w[order])
    block_e = jnp.minimum(jnp.searchsorted(pad_end, jnp.arange(n_blocks, dtype=jnp.int32) * MOE_BLOCK,
                                           side='right'), N_EXPERTS - 1).astype(jnp.int32)
    xf_pad = jnp.concatenate([xf, jnp.zeros((1, dm), xf.dtype)], axis=0)
    xs = xf_pad[pad_tok].reshape(n_blocks, MOE_BLOCK, dm)

    def expert_block(args):
        xb, e = args
        hdn = jax.nn.silu(xb @ w1[e]) * (xb @ w3[e])
        return hdn @ w2[e]

    ys = lax.map(expert_block, (xs, block_e)).reshape(p_len, dm)
    out = jnp.zeros((t + 1, dm), ys.dtype).at[pad_tok].add(ys * pad_w[:, None].astype(ys.dtype))
    return out[:t].reshape(b, s, dm).astype(x.dtype)

def first_inputs(seed: int = 0) -> dict:
    key = jax.random.key(seed)
    ks = jax.random.split(key, 25)
    f = jnp.float32

    def nrm(k, shape, scale):
        return jax.random.normal(k, shape, f) * scale

    return {
        'x': nrm(ks[0], (BATCH, SEQ, D_MODEL), 1.0),
        'p': nrm(ks[1], (DEPTH, BATCH, SEQ, D_PLE), 1.0),
        'g_mix': 1.0 + nrm(ks[2], (DEPTH, D_MODEL), 0.02),
        'w_in': nrm(ks[3], (DEPTH, D_MODEL, D_IN), D_MODEL ** -0.5),
        'g_qa': 1.0 + nrm(ks[4], (DEPTH, DA_QK), 0.02),
        'g_ka': 1.0 + nrm(ks[5], (DEPTH, DA_QK), 0.02),
        'lam_q1': nrm(ks[6], (DEPTH, DA_QK), 0.1),
        'lam_k1': nrm(ks[7], (DEPTH, DA_QK), 0.1),
        'lam_q2': nrm(ks[8], (DEPTH, DA_QK), 0.1),
        'lam_k2': nrm(ks[9], (DEPTH, DA_QK), 0.1),
        'g_sub': 1.0 + nrm(ks[10], (DEPTH, DA_V), 0.02),
        'g_qb': 1.0 + nrm(ks[11], (DEPTH, DB_H), 0.02),
        'g_kb': 1.0 + nrm(ks[12], (DEPTH, DB_H), 0.02),
        'rpb': nrm(ks[13], (DEPTH, HB, 2 * WIN_R - 1, 2 * WIN_C - 1), 0.1),
        'w_out': nrm(ks[14], (DEPTH, D_MIX, D_MODEL), D_MIX ** -0.5),
        'g_ffn': 1.0 + nrm(ks[15], (DEPTH, D_MODEL), 0.02),
        'w_rg': nrm(ks[16], (DEPTH, D_MODEL, N_GROUPS), D_MODEL ** -0.5),
        'w_re': nrm(ks[17], (DEPTH, D_MODEL, N_EXPERTS), D_MODEL ** -0.5),
        'w1': nrm(ks[18], (DEPTH, N_EXPERTS, D_MODEL, D_EXPERT), D_MODEL ** -0.5),
        'w3': nrm(ks[19], (DEPTH, N_EXPERTS, D_MODEL, D_EXPERT), D_MODEL ** -0.5),
        'w2': nrm(ks[20], (DEPTH, N_EXPERTS, D_EXPERT, D_MODEL), D_EXPERT ** -0.5),
        'g_plg': 1.0 + nrm(ks[21], (DEPTH, D_MODEL), 0.02),
        'w_plg': nrm(ks[22], (DEPTH, D_MODEL, D_MODEL), D_MODEL ** -0.5),
        'w_ple': nrm(ks[23], (DEPTH, D_PLE, D_MODEL), D_PLE ** -0.5),
        'g_ple': 1.0 + nrm(ks[24], (DEPTH, D_MODEL), 0.02),
    }

def first_block(x, p, g_mix, w_in, g_qa, g_ka, lam_q1, lam_k1, lam_q2, lam_k2, g_sub, g_qb, g_kb,
              rpb, w_out, g_ffn, w_rg, w_re, w1, w3, w2, g_plg, w_plg, w_ple, g_ple):
    b, s, _ = x.shape
    h = x
    for i in range(DEPTH):
        lam_init = 0.8 - 0.6 * math.exp(-0.3 * i)
        a = rms_norm(h, g_mix[i])
        proj = a @ w_in[i]
        qa, ka, va, qb, kb, vb = jnp.split(proj, np.cumsum([DA, DA, DA, DB, DB])[:5].tolist(), axis=-1)
        oa = diff_attention(qa.reshape(b, s, HA, 2, DA_QK), ka.reshape(b, s, HA, 2, DA_QK),
                            va.reshape(b, s, HA, DA_V), g_qa[i], g_ka[i],
                            lam_q1[i], lam_k1[i], lam_q2[i], lam_k2[i], g_sub[i], lam_init)
        ob = neighbourhood_attention(qb.reshape(b, s, HB, DB_H), kb.reshape(b, s, HB, DB_H),
                                     vb.reshape(b, s, HB, DB_H), g_qb[i], g_kb[i], rpb[i])
        h = h + jnp.concatenate([oa, ob], axis=-1) @ w_out[i]
        h = h + hier_moe(rms_norm(h, g_ffn[i]), w_rg[i], w_re[i], w1[i], w3[i], w2[i])
        h = h + rms_norm(p[i] @ w_ple[i], g_ple[i]) * jax.nn.sigmoid(rms_norm(h, g_plg[i]) @ w_plg[i])
    return h


DEPTH_2 = 2

CTX_LEN = 256
NORM_EPS = 1e-6
N_MIXERS = 2

GQA_HEADS = 16
GQA_KV_HEADS = 4
GQA_GROUP = GQA_HEADS // GQA_KV_HEADS
GQA_HEAD_DIM = 64
GQA_WIDTH = GQA_HEADS * GQA_HEAD_DIM
GQA_KV_WIDTH = GQA_KV_HEADS * GQA_HEAD_DIM
GQA_IN_COLS = 2 * GQA_KV_WIDTH + 2 * GQA_WIDTH
GQA_CTX_COLS = 2 * GQA_KV_WIDTH

MLA_HEADS = 16
MLA_NOPE = 64
MLA_ROPE = 32
MLA_V = 64
MLA_Q_LORA = 384
MLA_KV_LORA = 256
MLA_WIDTH = MLA_HEADS * MLA_V
MLA_CTX_COLS = MLA_KV_LORA + MLA_ROPE
MLA_IN_COLS = MLA_CTX_COLS + MLA_Q_LORA + MLA_WIDTH


def rms_norm_2(x, w):
    xf = x.astype(jnp.float32)
    y = xf * lax.rsqrt(jnp.mean(xf * xf, axis=-1, keepdims=True) + NORM_EPS)
    return (y * w.astype(jnp.float32)).astype(x.dtype)

def adaln_params(cond, w_mod, b_mod):
    mod = jax.nn.silu(cond) @ w_mod + b_mod
    return jnp.split(mod, 3, axis=-1)

def axial_rope_tables(n_tokens, rot_dim, dtype):
    rows = n_tokens // GRID_W
    row = jnp.repeat(jnp.arange(rows, dtype=jnp.float32), GRID_W)
    col = jnp.tile(jnp.arange(GRID_W, dtype=jnp.float32), rows)
    axis_dim = rot_dim // 2
    inv_freq = jnp.power(ROPE_THETA, -jnp.arange(0, axis_dim, 2, dtype=jnp.float32) / axis_dim)
    ang_r = row[:, None] * inv_freq[None, :]
    ang_c = col[:, None] * inv_freq[None, :]
    ang = jnp.concatenate([ang_r, ang_r, ang_c, ang_c], axis=-1)
    return jnp.cos(ang).astype(dtype), jnp.sin(ang).astype(dtype)

def apply_axial_rope(x, cos, sin):
    shape = (1, cos.shape[0]) + (1,) * (x.ndim - 3) + (cos.shape[-1],)
    cos = cos.reshape(shape)
    sin = sin.reshape(shape)
    x1, x2, x3, x4 = jnp.split(x, 4, axis=-1)
    rotated = jnp.concatenate([-x2, x1, -x4, x3], axis=-1)
    return x * cos + rotated * sin

def sweep_query_blocks(fn, *q_arrays):
    B, S = q_arrays[0].shape[:2]
    nb = S // Q_BLOCK
    blocks = tuple(jnp.moveaxis(a.reshape((B, nb, Q_BLOCK) + a.shape[2:]), 1, 0) for a in q_arrays)
    out = lax.map(lambda blk: fn(*blk), blocks)
    out = jnp.moveaxis(out, 0, 1)
    return out.reshape((B, S) + out.shape[3:])

def gqa_attend(q, k, v):
    s = jnp.einsum('bqhgd,bkhd->bhgqk', q, k).astype(jnp.float32) * (GQA_HEAD_DIM ** -0.5)
    p = jax.nn.softmax(s, axis=-1).astype(v.dtype)
    return jnp.einsum('bhgqk,bkhd->bqhgd', p, v)

def mla_attend(q_nope, q_rope, k_nope, k_rope, v):
    s = (jnp.einsum('bqhd,bkhd->bhqk', q_nope, k_nope)
         + jnp.einsum('bqhr,bkr->bhqk', q_rope, k_rope)).astype(jnp.float32) * ((MLA_NOPE + MLA_ROPE) ** -0.5)
    p = jax.nn.softmax(s, axis=-1).astype(v.dtype)
    return jnp.einsum('bhqk,bkhd->bqhd', p, v)

def gqa_mixer(h, hc, p, cos, sin, with_ctx_out):
    B, S, _ = h.shape
    L = hc.shape[1]
    cuts = [GQA_KV_WIDTH, 2 * GQA_KV_WIDTH, 2 * GQA_KV_WIDTH + GQA_WIDTH]
    k, v, q, g = jnp.split(h @ p["w_in"], cuts, axis=-1)
    q = apply_axial_rope(rms_norm_2(q.reshape(B, S, GQA_KV_HEADS, GQA_GROUP, GQA_HEAD_DIM), p["q_norm"]), cos, sin)
    k = apply_axial_rope(rms_norm_2(k.reshape(B, S, GQA_KV_HEADS, GQA_HEAD_DIM), p["k_norm"]), cos, sin)
    v = v.reshape(B, S, GQA_KV_HEADS, GQA_HEAD_DIM)
    w_ctx = p["w_in"] if with_ctx_out else p["w_in"][:, :GQA_CTX_COLS]
    proj_c = hc @ w_ctx
    kc = rms_norm_2(proj_c[..., :GQA_KV_WIDTH].reshape(B, L, GQA_KV_HEADS, GQA_HEAD_DIM), p["k_norm"])
    vc = proj_c[..., GQA_KV_WIDTH:GQA_CTX_COLS].reshape(B, L, GQA_KV_HEADS, GQA_HEAD_DIM)
    k_all = jnp.concatenate([kc, k], axis=1)
    v_all = jnp.concatenate([vc, v], axis=1)
    o = sweep_query_blocks(lambda qb: gqa_attend(qb, k_all, v_all), q).reshape(B, S, GQA_WIDTH)
    y = (o * jax.nn.silu(g)) @ p["w_out"]
    yc = None
    if with_ctx_out:
        qc = rms_norm_2(proj_c[..., GQA_CTX_COLS:GQA_CTX_COLS + GQA_WIDTH]
                      .reshape(B, L, GQA_KV_HEADS, GQA_GROUP, GQA_HEAD_DIM), p["q_norm"])
        gc = proj_c[..., GQA_CTX_COLS + GQA_WIDTH:]
        oc = gqa_attend(qc, kc, vc).reshape(B, L, GQA_WIDTH)
        yc = (oc * jax.nn.silu(gc)) @ p["w_out"]
    return y, yc

def mla_mixer(h, hc, p, cos, sin, with_ctx_out):
    B, S, _ = h.shape
    L = hc.shape[1]

    def kv_heads(kv_a, k_r, n):
        kv = (rms_norm_2(kv_a, p["kv_a_norm"]) @ p["w_kv_b"]).reshape(B, n, MLA_HEADS, MLA_NOPE + MLA_V)
        k_nope, v = jnp.split(kv, [MLA_NOPE], axis=-1)
        return rms_norm_2(k_nope, p["k_nope_norm"]), rms_norm_2(k_r, p["k_rope_norm"]), v

    def q_heads(q_a, n):
        q = (rms_norm_2(q_a, p["q_a_norm"]) @ p["w_q_b"]).reshape(B, n, MLA_HEADS, MLA_NOPE + MLA_ROPE)
        q = rms_norm_2(q, p["q_norm"])
        return jnp.split(q, [MLA_NOPE], axis=-1)

    cuts = [MLA_KV_LORA, MLA_CTX_COLS, MLA_CTX_COLS + MLA_Q_LORA]
    kv_a, k_r, q_a, g = jnp.split(h @ p["w_in"], cuts, axis=-1)
    k_nope, k_rope, v = kv_heads(kv_a, k_r, S)
    k_rope = apply_axial_rope(k_rope, cos, sin)
    q_nope, q_rope = q_heads(q_a, S)
    q_rope = apply_axial_rope(q_rope, cos, sin)
    w_ctx = p["w_in"] if with_ctx_out else p["w_in"][:, :MLA_CTX_COLS]
    proj_c = hc @ w_ctx
    kc_nope, kc_rope, vc = kv_heads(proj_c[..., :MLA_KV_LORA], proj_c[..., MLA_KV_LORA:MLA_CTX_COLS], L)
    kn_all = jnp.concatenate([kc_nope, k_nope], axis=1)
    kr_all = jnp.concatenate([kc_rope, k_rope], axis=1)
    v_all = jnp.concatenate([vc, v], axis=1)
    o = sweep_query_blocks(lambda qn, qr: mla_attend(qn, qr, kn_all, kr_all, v_all), q_nope, q_rope)
    y = (o.reshape(B, S, MLA_WIDTH) * jax.nn.silu(g)) @ p["w_out"]
    yc = None
    if with_ctx_out:
        qc_nope, qc_rope = q_heads(proj_c[..., MLA_CTX_COLS:MLA_CTX_COLS + MLA_Q_LORA], L)
        gc = proj_c[..., MLA_CTX_COLS + MLA_Q_LORA:]
        oc = mla_attend(qc_nope, qc_rope, kc_nope, kc_rope, vc).reshape(B, L, MLA_WIDTH)
        yc = (oc * jax.nn.silu(gc)) @ p["w_out"]
    return y, yc

def hybrid_layer(x, ctx, c, c_ctx, w_mod, b_mod, norm_w, mixer, mixer_params, cos, sin, with_ctx_out):
    shift, scale, gate = adaln_params(c, w_mod, b_mod)
    shift_c, scale_c, gate_c = adaln_params(c_ctx, w_mod, b_mod)
    h = rms_norm_2(x, norm_w) * (1.0 + scale[:, None, :]) + shift[:, None, :]
    hc = rms_norm_2(ctx, norm_w) * (1.0 + scale_c) + shift_c
    y, yc = mixer(h, hc, mixer_params, cos, sin, with_ctx_out)
    x = x + gate[:, None, :] * y
    if with_ctx_out:
        ctx = ctx + gate_c * yc
    return x, ctx

def _normal(key, shape, scale):
    return jax.random.normal(key, shape, dtype=jnp.float32) * scale

def _gain(key, n):
    return 1.0 + 0.01 * jax.random.normal(key, (n,), dtype=jnp.float32)

def second_inputs(seed: int = 0) -> dict:
    key = jax.random.key(seed)
    ks = jax.random.split(key, 24)
    D = D_MODEL
    return {
        "x": _normal(ks[0], (BATCH, SEQ, D), 1.0),
        "c": _normal(ks[1], (BATCH, D), 1.0),
        "ctx": _normal(ks[2], (BATCH, CTX_LEN, D), 1.0),
        "c_ctx": _normal(ks[3], (D,), 1.0),
        "l0_w_mod": _normal(ks[4], (D, 3 * D), 0.5 * D ** -0.5),
        "l0_b_mod": _normal(ks[5], (3 * D,), 0.01),
        "l0_norm": _gain(ks[6], D),
        "l0_w_in": _normal(ks[7], (D, GQA_IN_COLS), D ** -0.5),
        "l0_q_norm": _gain(ks[8], GQA_HEAD_DIM),
        "l0_k_norm": _gain(ks[9], GQA_HEAD_DIM),
        "l0_w_out": _normal(ks[10], (GQA_WIDTH, D), GQA_WIDTH ** -0.5),
        "l1_w_mod": _normal(ks[11], (D, 3 * D), 0.5 * D ** -0.5),
        "l1_b_mod": _normal(ks[12], (3 * D,), 0.01),
        "l1_norm": _gain(ks[13], D),
        "l1_w_in": _normal(ks[14], (D, MLA_IN_COLS), D ** -0.5),
        "l1_kv_a_norm": _gain(ks[15], MLA_KV_LORA),
        "l1_w_kv_b": _normal(ks[16], (MLA_KV_LORA, MLA_HEADS * (MLA_NOPE + MLA_V)), MLA_KV_LORA ** -0.5),
        "l1_q_a_norm": _gain(ks[17], MLA_Q_LORA),
        "l1_w_q_b": _normal(ks[18], (MLA_Q_LORA, MLA_HEADS * (MLA_NOPE + MLA_ROPE)), MLA_Q_LORA ** -0.5),
        "l1_q_norm": _gain(ks[19], MLA_NOPE + MLA_ROPE),
        "l1_k_nope_norm": _gain(ks[20], MLA_NOPE),
        "l1_k_rope_norm": _gain(ks[21], MLA_ROPE),
        "l1_w_out": _normal(ks[22], (MLA_WIDTH, D), MLA_WIDTH ** -0.5),
    }

def second_block(x, c, ctx, c_ctx,
              l0_w_mod, l0_b_mod, l0_norm, l0_w_in, l0_q_norm, l0_k_norm, l0_w_out,
              l1_w_mod, l1_b_mod, l1_norm, l1_w_in, l1_kv_a_norm, l1_w_kv_b, l1_q_a_norm, l1_w_q_b,
              l1_q_norm, l1_k_nope_norm, l1_k_rope_norm, l1_w_out):
    n_tokens = x.shape[1]
    cos_a, sin_a = axial_rope_tables(n_tokens, GQA_HEAD_DIM, x.dtype)
    cos_b, sin_b = axial_rope_tables(n_tokens, MLA_ROPE, x.dtype)
    gqa_params = {"w_in": l0_w_in, "q_norm": l0_q_norm, "k_norm": l0_k_norm, "w_out": l0_w_out}
    mla_params = {"w_in": l1_w_in, "kv_a_norm": l1_kv_a_norm, "w_kv_b": l1_w_kv_b,
                  "q_a_norm": l1_q_a_norm, "w_q_b": l1_w_q_b, "q_norm": l1_q_norm,
                  "k_nope_norm": l1_k_nope_norm, "k_rope_norm": l1_k_rope_norm, "w_out": l1_w_out}
    layers = [
        (l0_w_mod, l0_b_mod, l0_norm, gqa_mixer, gqa_params, cos_a, sin_a),
        (l1_w_mod, l1_b_mod, l1_norm, mla_mixer, mla_params, cos_b, sin_b),
    ]
    for i in range(DEPTH_2):
        w_mod, b_mod, norm_w, mixer, params, cos, sin = layers[i]
        x, ctx = hybrid_layer(x, ctx, c, c_ctx, w_mod, b_mod, norm_w, mixer, params, cos, sin,
                              with_ctx_out=(i < DEPTH_2 - 1))
    return x


def setup_inputs(seed=0):
    out = dict(first_inputs(seed))
    for name, value in second_inputs(seed + 1).items():
        if name != "x":
            out[name + "_2"] = value
    return out


def reference(
    x, p, g_mix, w_in, g_qa, g_ka, lam_q1, lam_k1, lam_q2, lam_k2, g_sub, g_qb, g_kb, rpb,
    w_out, g_ffn, w_rg, w_re, w1, w3, w2, g_plg, w_plg, w_ple, g_ple, c_2, ctx_2, c_ctx_2,
    l0_w_mod_2, l0_b_mod_2, l0_norm_2, l0_w_in_2, l0_q_norm_2, l0_k_norm_2, l0_w_out_2,
    l1_w_mod_2, l1_b_mod_2, l1_norm_2, l1_w_in_2, l1_kv_a_norm_2, l1_w_kv_b_2, l1_q_a_norm_2,
    l1_w_q_b_2, l1_q_norm_2, l1_k_nope_norm_2, l1_k_rope_norm_2, l1_w_out_2,
):
    x = first_block(
        x, p, g_mix, w_in, g_qa, g_ka, lam_q1, lam_k1, lam_q2, lam_k2, g_sub, g_qb, g_kb, rpb,
        w_out, g_ffn, w_rg, w_re, w1, w3, w2, g_plg, w_plg, w_ple, g_ple,
    )
    return second_block(
        x, c_2, ctx_2, c_ctx_2, l0_w_mod_2, l0_b_mod_2, l0_norm_2, l0_w_in_2, l0_q_norm_2,
        l0_k_norm_2, l0_w_out_2, l1_w_mod_2, l1_b_mod_2, l1_norm_2, l1_w_in_2, l1_kv_a_norm_2,
        l1_w_kv_b_2, l1_q_a_norm_2, l1_w_q_b_2, l1_q_norm_2, l1_k_nope_norm_2, l1_k_rope_norm_2,
        l1_w_out_2,
    )


_drawn_inputs = setup_inputs


def setup_inputs(seed=0):
    import zlib

    import numpy as np

    out = dict(_drawn_inputs(seed))
    spreads = {}
    factors = {'g_qa': 3.269,
     'g_ka': 3.58,
     'lam_k2': 8.0,
     'g_qb': 8.0,
     'g_kb': 8.0,
     'rpb': 2.919,
     'g_plg': 8.0,
     'g_ple': 6.802,
     'ctx_2': 7.205,
     'c_ctx_2': 2.834,
     'l0_b_mod_2': 8.0,
     'l0_norm_2': 8.0,
     'l0_q_norm_2': 8.0,
     'l0_k_norm_2': 8.0,
     'l1_b_mod_2': 8.0,
     'l1_norm_2': 8.0,
     'l1_kv_a_norm_2': 8.0,
     'l1_q_a_norm_2': 8.0,
     'l1_w_q_b_2': 4.831,
     'l1_q_norm_2': 8.0,
     'l1_k_nope_norm_2': 8.0,
     'l1_k_rope_norm_2': 8.0}
    for name, (base, spread) in spreads.items():
        noise = np.random.default_rng([zlib.crc32(name.encode()), seed]).standard_normal(out[name].shape)
        drawn = base * np.exp(spread * noise) if base else spread * noise
        out[name] = __import__('jax').numpy.asarray(drawn.astype(out[name].dtype))
    for name, factor in factors.items():
        out[name] = (out[name] * factor).astype(out[name].dtype)
    return out
```

```python
import math
from contextlib import ExitStack, contextmanager

import numpy as np
import concourse.bass as bass
import concourse.mybir as mybir
from concourse.alu_op_type import AluOpType as ALU

F32 = mybir.dt.float32
I32 = mybir.dt.int32
ACT = mybir.ActivationFunctionType
AX = mybir.AxisListType
ds = bass.ds

P = 128
D = 1024
DK = D // P
GRID_W, ROWS, CB = 64, 8, 16
SEQ, CTX = 512, 256
XT, CT = SEQ // P, CTX // P
AT = XT + CT
EPS = 1e-6
NEG = -1e30
LAM_INIT = 0.8 - 0.6 * math.exp(0.0)
THETA = 10000.0
N_GROUPS, PER_GROUP, D_EXPERT = 4, 8, 512
N_EXPERTS = N_GROUPS * PER_GROUP
CAP = 64
MAX_BLOCKS = 2 * SEQ // CAP + N_EXPERTS
NA_HEADS, NA_D, WIN_R, WIN_C = 16, 32, 8, 16


def token_order():
    return np.arange(SEQ).reshape(ROWS, SEQ // ROWS // CB, CB).transpose(1, 0, 2).reshape(-1)


def per_tile(table):
    n = table.shape[0] // P
    return table.reshape(n, P, -1).transpose(1, 0, 2).reshape(P, -1)


def rope_tables():
    pos = token_order().astype(np.float32)
    f = np.float32
    inv = f(THETA) ** (-np.arange(0, 64, 2, dtype=np.float32) / f(64))
    ang = pos[:, None] * inv[None, :]
    full_c = np.concatenate([np.cos(ang)] * 2, 1)
    full_s = np.concatenate([-np.sin(ang), np.sin(ang)], 1)

    def axial(rot):
        row, col = np.floor(pos / GRID_W).astype(f), (pos % GRID_W).astype(f)
        inv = f(THETA) ** (-np.arange(0, rot // 2, 2, dtype=np.float32) / f(rot // 2))
        ar, ac = row[:, None] * inv, col[:, None] * inv
        c = np.concatenate([np.cos(ar)] * 2 + [np.cos(ac)] * 2, 1)
        s = np.concatenate([-np.sin(ar), np.sin(ar), -np.sin(ac), np.sin(ac)], 1)
        c = np.concatenate([c, np.ones((CTX, rot), f)], 0)
        s = np.concatenate([s, np.zeros((CTX, rot), f)], 0)
        return c.astype(f), s.astype(f)

    return full_c.astype(f), full_s.astype(f), axial(64), axial(32)


def window_masks():
    m = np.zeros((P, 3, 3, CB), np.float32)
    for kind, g in enumerate((0, 1, 3)):
        for q in range(P):
            c = CB * g + q % CB
            start = min(max(c - WIN_C // 2, 0), GRID_W - WIN_C)
            for d in range(3):
                for k in range(CB):
                    kc = CB * (g + d - 1) + k
                    if not start <= kc < start + WIN_C:
                        m[q, kind, d, k] = NEG
    return m


def constants():
    fc, fs, (ac, as_), (mc, ms) = rope_tables()
    select = np.zeros((P, 4, P), np.float32)
    for j in range(2):
        for cond in range(2):
            select[32 * j + cond, 2 * j + cond, :] = 1.0
    fields = dict(
        ident=np.eye(P, dtype=np.float32),
        ones=np.ones((P, P), np.float32),
        before=np.triu(np.ones((P, P), np.float32), 1),
        eps=np.full((P, 1), EPS, np.float32),
        full_cos=per_tile(fc), full_sin=per_tile(fs),
        ax_cos=per_tile(ac), ax_sin=per_tile(as_),
        mla_cos=per_tile(mc), mla_sin=per_tile(ms),
        masks=window_masks().reshape(P, -1),
        select=select.reshape(P, -1),
        prio4=np.tile(np.arange(N_GROUPS, 0, -1, dtype=np.float32), (P, 1)),
        prio8=np.tile(np.arange(PER_GROUP, 0, -1, dtype=np.float32), (P, 1)),
        block_no=np.tile(np.arange(MAX_BLOCKS, dtype=np.float32), (P, 1)),
    )
    return pack(fields)


def slot_table():
    t = np.zeros((MAX_BLOCKS, CAP, 4), np.int32)
    t[:, :, 1] = 2 * (2 * SEQ + np.arange(CAP))
    return t.reshape(-1, 4)


def slot_ids():
    tok = np.arange(XT)[None, :] * P + np.arange(P)[:, None]
    out = np.zeros((P, 2, XT, 2), np.int32)
    for s in range(2):
        out[:, s, :, 0] = 2 * tok
        out[:, s, :, 1] = 2 * (s * SEQ + tok)
    return out.reshape(P, -1)


def half_ids():
    h = np.zeros((P, 2), np.int32)
    h[P // 2:] = 1
    return h


def pack(fields):
    at, n = {}, 0
    for k, v in fields.items():
        at[k] = (n, v.shape[1])
        n += v.shape[1]
    return at, np.concatenate(list(fields.values()), 1)


def columns(v):
    return np.asarray(v).reshape(-1, P).T


def spread(v):
    v = np.asarray(v).reshape(1, -1)
    return np.broadcast_to(v, (P, v.shape[1]))


def parameters(a):
    return pack(dict(
        g_mix=columns(a["g_mix"]), g_ffn=columns(a["g_ffn"]), g_plg=columns(a["g_plg"]),
        l0_norm=columns(a["l0_norm_2"]), l1_norm=columns(a["l1_norm_2"]),
        kv_a_norm=columns(a["l1_kv_a_norm_2"]), q_a_norm=columns(a["l1_q_a_norm_2"]),
        g_sub=columns(a["g_sub"]),
        cond=np.stack([columns(a["c_2"]), columns(a["c_ctx_2"])], 2).reshape(P, -1),
        l0_b=columns(a["l0_b_mod_2"]), l1_b=columns(a["l1_b_mod_2"]),
        g_qa=spread(a["g_qa"]), g_ka=spread(a["g_ka"]),
        g_qb=spread(a["g_qb"]), g_kb=spread(a["g_kb"]),
        lam=spread(np.concatenate([np.asarray(a[n]).reshape(-1) for n in ("lam_q1", "lam_k1", "lam_q2", "lam_k2")])),
        gqa_q=spread(a["l0_q_norm_2"]), gqa_k=spread(a["l0_k_norm_2"]),
        mla_q=spread(a["l1_q_norm_2"]), mla_kn=spread(a["l1_k_nope_norm_2"]), mla_kr=spread(a["l1_k_rope_norm_2"]),
    ))


def wide_parameters(a):
    return dict(l0_b_gate=spread(np.asarray(a["l0_b_mod_2"])[2 * D:]), l1_b_gate=spread(np.asarray(a["l1_b_mod_2"])[2 * D:]),
                g_ple=spread(a["g_ple"]))


@contextmanager
def stage(nc, name, start=0, software_dma=(), **sems):
    made = {k: [nc.alloc_semaphore(f"{name}_{k}{'' if n is None else i}") for i in range(n or 1)]
            for k, n in sems.items()}
    every = [x for got in made.values() for x in got]
    if start:
        for k, got in made.items():
            for x in got:
                if k not in software_dma:
                    nc.gpsimd.sem_inc(x, start)
    with nc.Block() as block:
        yield block, {k: got if sems[k] else got[0] for k, got in made.items()}
    nc.clear_and_free_semaphores(every)
    nc.all_engine_barrier(sem_only=True)


class Chain:

    def __init__(self, eng, sem, base=0):
        self.eng, self.sem, self.base, self.n = eng, sem, base, 0

    def __call__(self, ins):
        self.n += 1
        ins.then_inc(self.sem, 1)
        self.eng.wait_ge(self.sem, self.base + self.n)


def loop(eng, n, body):
    if n == 1:
        body(0)
    elif n > 1:
        with eng.Fori(0, n) as i:
            body(i)


def inverse_root(dve, chain, ss, root, n, v, out):
    chain(dve.tensor_scalar(v, ss, 0.5 / n, 0.5 * EPS, ALU.mult, ALU.add))
    chain(dve.reciprocal(out, root))
    chain(dve.tensor_tensor(v, v, out, ALU.mult))
    chain(dve.scalar_tensor_tensor(out=v, in0=root, scalar=0.5, in1=v, op0=ALU.mult, op1=ALU.add))
    return dve.reciprocal(out, v)


def copy(nc, eng, act, out, in_):
    return eng.activation(out, in_, ACT.Copy) if act else eng.tensor_copy(out, in_)


def norm_transpose(nc, name, m, src, K, T, gain, shift, out, spill=None):
    W = K * P

    def of_tile(v, t):
        v = v if len(v.shape) == 2 else v[:, ds(t, 1), :].rearrange("p a k -> p (a k)")
        return v.unsqueeze(2).to_broadcast([P, K, P])

    with ExitStack() as c:
        sb = lambda n, s: c.enter_context(nc.sbuf_tensor(f"{name}_{n}", s, F32))
        squares, xn = sb("squares", [P, W]), sb("xn", [P, 2, W])
        ss, sd, rs = sb("ss", [P, 2]), sb("sd", [P, 2]), sb("rs", [P, 2])
        half = sb("half", [P, 2])
        ps = c.enter_context(nc.psum_tensor(f"{name}_ps", [P, 2, 1024], F32))
        with stage(nc, name, start=1, act_chain=None, dve_chain=None, sd_done=2, rs_done=2, xn_done=2,
                   turned=2, out_done=2, spilled=2) as (block, s):

            @block.scalar
            def _(act):
                def body(i):
                    chain = Chain(act, s["act_chain"], 1 + 2 * i)
                    for p in range(2):
                        act.wait_ge(s["rs_done"][p], 1 + i)
                        chain(act.activation(squares[:], src(2 * i + p),
                                             ACT.Square, accum_out=ss[:, p:p + 1]))
                        act.activation(sd[:, p:p + 1], ss[:, p:p + 1], ACT.Sqrt, bias=m["eps"],
                                       scale=1.0 / W).then_inc(s["sd_done"][p], 1)
                        act.wait_ge(s["sd_done"][p], 1 + i + 1)
                loop(act, T // 2, body)

            @block.vector
            def _(dve):
                def body(i):
                    chain = Chain(dve, s["dve_chain"], 1 + (8 if shift is None else 10) * i)
                    for p in range(2):
                        dve.wait_ge(s["sd_done"][p], 1 + i + 1)
                        dve.wait_ge(s["xn_done"][p], 1 + i)
                        inverse_root(dve, chain, ss[:, p:p + 1], sd[:, p:p + 1], W, half[:, p:p + 1],
                                     rs[:, p:p + 1]).then_inc(s["rs_done"][p], 1)
                        dve.wait_ge(s["rs_done"][p], 1 + i + 1)
                        dve.wait_ge(s["turned"][p], 1 + i)
                        if spill is not None:
                            dve.wait_ge(s["spilled"][p], 1 + 16 * i)
                        dve.tensor_scalar(xn[:, p, :], src(2 * i + p),
                                          rs[:, p:p + 1], None, ALU.mult).then_inc(s["xn_done"][p], 1)
                    for p in range(2):
                        t = 2 * i + p
                        dve.wait_ge(s["turned"][p], 1 + i + 1)
                        o = out[:, :, ds(t * P, P)]
                        v = ps[:, p, 0:W].rearrange("p (k t) -> p k t", k=K)
                        if shift is None:
                            dve.tensor_tensor(o, v, of_tile(gain, t), ALU.mult).then_inc(s["out_done"][p], 1)
                        else:
                            chain(dve.tensor_tensor(o, v, of_tile(gain, t), ALU.mult))
                            dve.tensor_tensor(o, o, of_tile(shift, t), ALU.add).then_inc(s["out_done"][p], 1)
                loop(dve, T // 2, body)

            @block.tensor
            def _(pe):
                def body(i):
                    for p in range(2):
                        pe.wait_ge(s["xn_done"][p], 1 + i + 1)
                        pe.wait_ge(s["out_done"][p], 1 + i)
                        for k in range(K):
                            last = pe.transpose(ps[:, p, k * P:(k + 1) * P], xn[:, p, k * P:(k + 1) * P], m["ident"])
                        last.then_inc(s["turned"][p], 1)
                loop(pe, T // 2, body)

            if spill is not None:
                @block.sync
                def _(sp):
                    def body(i):
                        for p in range(2):
                            sp.wait_ge(s["xn_done"][p], 1 + i + 1)
                            sp.dma_start(spill[ds(2 * i + p, 1)].rearrange("a p d -> p (a d)"), xn[:, p, :]).then_inc(s["spilled"][p], 16)
                    loop(sp, T // 2, body)
                    for p in range(2):
                        sp.wait_ge(s["spilled"][p], 1 + 16 * (T // 2))


def dense(nc, name, lhs, KT, T, w, n_chunks, width, emit, both=True, col0=0, links=0):
    pairs, NB, H = n_chunks // 2, 4, T // 2
    with ExitStack() as c:
        wb = c.enter_context(nc.sbuf_tensor(f"{name}_w", [P, 2, KT, width], F32))
        tmp = c.enter_context(nc.sbuf_tensor(f"{name}_tmp", [P, 2, width], F32))
        ps = c.enter_context(nc.psum_tensor(f"{name}_ps", [P, NB, 512], F32))
        with stage(nc, name, start=1, loaded=2, mm=NB, ev=NB, dve_chain=None, act_chain=None) as (block, s):
            src = w.rearrange("(k p) n -> p k n", p=P)

            def after(cp):
                u = cp * T + T - 1
                return u % NB, u // NB + 1

            @block.sync
            def _(sp):
                def load(i, cp):
                    sp.dma_start(wb[:, cp], src[:, :, ds(col0 + (2 * i + cp) * width, width)]).then_inc(s["loaded"][cp], 16)

                load(0, 0)
                if n_chunks > 1:
                    load(0, 1)

                def refill(i, cps):
                    for cp in cps:
                        b, n = after(cp)
                        sp.wait_ge(s["mm"][b], 1 + i * H + n)
                        load(i + 1, cp)
                loop(sp, pairs - 1, lambda i: refill(i, (0, 1)))
                if n_chunks % 2 and pairs:
                    refill(pairs - 1, (0,))

            def over_chunks(eng, body):
                loop(eng, pairs, lambda i: body(i, (0, 1)))
                if n_chunks % 2:
                    body(pairs, (0,))

            @block.tensor
            def _(pe):
                def body(i, cps):
                    for cp in cps:
                        pe.wait_ge(s["loaded"][cp], 1 + 16 * (i + 1))
                        for t in range(T):
                            u = cp * T + t
                            pe.wait_ge(s["ev"][u % NB], 1 + i * H + u // NB)
                            for k in range(KT):
                                last = pe.matmul(ps[:, u % NB, 0:width], lhs(k, t), wb[:, cp, k, :],
                                                 start=(k == 0), stop=(k == KT - 1))
                            last.then_inc(s["mm"][u % NB], 1)
                over_chunks(pe, body)

            def emptying(eng, is_act, sem):
                units = [u for u in range(2 * T) if not both or u % 2 == is_act]

                def body(i, cps):
                    chain = Chain(eng, sem, 1 + i * (len(units) * links))
                    for u in units:
                        if u // T not in cps:
                            continue
                        b = u % NB
                        eng.wait_ge(s["mm"][b], 1 + i * H + u // NB + 1)
                        emit(eng, is_act, u % T, 2 * i + u // T, ps[:, b, 0:width], tmp[:, is_act], chain).then_inc(s["ev"][b], 1)
                        if links:
                            eng.wait_ge(s["ev"][b], 1 + i * H + u // NB + 1)
                return body

            @block.vector
            def _(dve):
                over_chunks(dve, emptying(dve, 0, s["dve_chain"]))

            if both:
                @block.scalar
                def _(act):
                    over_chunks(act, emptying(act, 1, s["act_chain"]))


def dense_t(nc, name, act_t, KT, tokens, w, col0, n_chunks, emit):
    pieces = [(a, min(512, tokens - a)) for a in range(0, tokens, 512)]
    NB, CW = 4, 512
    with ExitStack() as c:
        wb = c.enter_context(nc.sbuf_tensor(f"{name}_w", [P, 2, KT, CW], F32))
        ps = c.enter_context(nc.psum_tensor(f"{name}_ps", [P, NB, 512], F32))
        with stage(nc, name, start=1, loaded=2, mm=NB, ev=NB) as (block, s):
            src = w.rearrange("(k p) n -> p k n", p=P)
            units = [(cc, j, a, n) for cc in range(n_chunks) for j in range(CW // P) for a, n in pieces]
            per_chunk = len(units) // n_chunks

            @block.sync
            def _(sp):
                for cc in range(n_chunks):
                    if cc >= 2:
                        u = (cc - 1) * per_chunk - 1
                        sp.wait_ge(s["mm"][u % NB], 1 + u // NB + 1)
                    sp.dma_start(wb[:, cc % 2], src[:, :, col0 + cc * CW:col0 + (cc + 1) * CW]).then_inc(s["loaded"][cc % 2], 16)

            @block.tensor
            def _(pe):
                for u, (cc, j, a, n) in enumerate(units):
                    if u % per_chunk == 0:
                        pe.wait_ge(s["loaded"][cc % 2], 1 + 16 * (cc // 2 + 1))
                    pe.wait_ge(s["ev"][u % NB], 1 + u // NB)
                    for k in range(KT):
                        last = pe.matmul(ps[:, u % NB, 0:n], wb[:, cc % 2, k, j * P:(j + 1) * P],
                                         act_t[:, k, a:a + n], start=(k == 0), stop=(k == KT - 1))
                    last.then_inc(s["mm"][u % NB], 1)

            @block.scalar
            def _(act):
                for u, (cc, j, a, n) in enumerate(units):
                    act.wait_ge(s["mm"][u % NB], 1 + u // NB + 1)
                    emit(act, cc * (CW // P) + j, a, n, ps[:, u % NB, 0:n]).then_inc(s["ev"][u % NB], 1)


def head_norms(nc, name, m, T, jobs):
    J = len(jobs)
    with ExitStack() as c:
        sb = lambda n, s: c.enter_context(nc.sbuf_tensor(f"{name}_{n}", s, F32))
        sq = [sb(f"sq{j}", [P, H, d]) for j, (_, H, d, _, _) in enumerate(jobs)]
        tw = [sb(f"tw{j}", [P, H, max(1, 2 * r[1] * r[2])]) if r else None for j, (_, H, d, _, r) in enumerate(jobs)]
        st = [sb(f"st{j}", [P, 4, H]) for j, (_, H, _, _, _) in enumerate(jobs)]
        with stage(nc, name, start=1, squared=None, summed=None, rooted=None, scaled=None, turned=None, done=None, dve_chain=None) as (block, s):

            @block.scalar
            def _(act):
                def body(t):
                    for j, (x, H, d, _, _) in enumerate(jobs):
                        act.wait_ge(s["summed"], 1 + t * J + j)
                        act.activation(sq[j][:], x(t), ACT.Square).then_inc(s["squared"], 1)
                    for j, (x, H, d, _, _) in enumerate(jobs):
                        act.wait_ge(s["summed"], 1 + t * J + j + 1)
                        act.wait_ge(s["scaled"], 1 + t * J)
                        act.activation(st[j][:, 1, :], st[j][:, 0, :], ACT.Sqrt, bias=m["eps"], scale=1.0 / d).then_inc(s["rooted"], 1)
                loop(act, T, body)

            @block.vector
            def _(dve):
                def body(t):
                    chain = Chain(dve, s["dve_chain"], 1 + t * (5 * J + sum(1 for q in jobs if q[4])))
                    for j in range(J):
                        dve.wait_ge(s["squared"], 1 + t * J + j + 1)
                        dve.wait_ge(s["rooted"], 1 + t * J)
                        dve.tensor_reduce(st[j][:, 0, :], sq[j][:], AX.X, ALU.add).then_inc(s["summed"], 1)
                    for j, (x, H, d, cos, rot) in enumerate(jobs):
                        dve.wait_ge(s["rooted"], 1 + t * J + j + 1)
                        chain(inverse_root(dve, chain, st[j][:, 0, :], st[j][:, 1, :], d, st[j][:, 3, :], st[j][:, 2, :]))
                        dve.tensor_tensor(x(t), x(t), st[j][:, 2, :].unsqueeze(2).to_broadcast([P, H, d]), ALU.mult).then_inc(s["scaled"], 1)
                    turns = 0
                    for j, (x, H, d, cos, rot) in enumerate(jobs):
                        dve.wait_ge(s["scaled"], 1 + t * J + j + 1)
                        if rot:
                            turns += 1
                            dve.wait_ge(s["turned"], 1 + t * sum(1 for q in jobs if q[4]) + turns)
                        cc = cos(t).unsqueeze(1).to_broadcast([P, H, d])
                        if rot:
                            f0, G, w, sin = rot
                            chain(dve.tensor_tensor(x(t), x(t), cc, ALU.mult))
                            xr = x(t)[:, :, f0:f0 + 2 * G * w]
                            dve.tensor_tensor(xr, xr, tw[j][:], ALU.add).then_inc(s["done"], 1)
                        else:
                            dve.tensor_tensor(x(t), x(t), cc, ALU.mult).then_inc(s["done"], 1)
                loop(dve, T, body)

            @block.gpsimd
            def _(pool):
                def body(t):
                    for j, (x, H, d, cos, rot) in enumerate(jobs):
                        if not rot:
                            continue
                        f0, G, w, sin = rot
                        pool.wait_ge(s["scaled"], 1 + t * J + j + 1)
                        pool.wait_ge(s["done"], 1 + t * J)
                        sw = sin(t).rearrange("p (g a w) -> p g a w", g=G, a=2)
                        for g in range(G):
                            for a in range(2):
                                last = pool.tensor_tensor(
                                    tw[j][:, :, (2 * g + a) * w:(2 * g + a + 1) * w],
                                    x(t)[:, :, f0 + (2 * g + 1 - a) * w:f0 + (2 * g + 2 - a) * w],
                                    sw[:, g, a, :].unsqueeze(1).to_broadcast([P, H, w]), ALU.mult)
                        last.then_inc(s["turned"], 1)
                loop(pool, T, body)


def attention(nc, name, m, pairs, U, nh, dv, q_src, k_src, v_src, out, gate=None, split=False,
              stage_k=(True, True), combine=None, bias=None, tiles=XT, ktiles=XT):
    NU = len(U)
    R = split or P
    NS = nh if split else 1
    KT = ktiles
    heads = 1 if combine is not None else nh
    W = 1024 if KT > 4 else 512
    pieces = []
    for _, lo, hi in U:
        n = hi - lo
        cut = [list(range(lo, hi))] if n <= 3 and bias is not None else [list(range(lo, lo + (n + 1) // 2)), list(range(lo + (n + 1) // 2, hi))]
        pieces.append([x for x in cut])
    order = [(p, u, i) for p in range(2) for u in range(NU) for i in range(nh)]
    torder = [(p, u, i, n) for p in range(2) for u in range(NU) for i in range(heads) for n in range(len(pieces[u]))]
    assert len(torder) % 2 == 0
    bank_of = {x: n % 2 for n, x in enumerate(torder)}
    use_of = {x: n // 2 for n, x in enumerate(torder)}
    per_bank = len(torder) // 2
    ob = (tiles + 3) // 4
    with ExitStack() as c:
        sb = lambda n, s: c.enter_context(nc.sbuf_tensor(f"{name}_{n}", s, F32))
        qs, ks, vs = sb("qs", [P, 2, NS, tiles, R]), sb("ks", [P, 2, NS, KT, R]), sb("vs", [P, 2, KT, nh * dv if combine is None else dv])
        qT, kT = sb("qT", [P, NS, tiles * P]), sb("kT", [P, nh, KT * P])
        kw = min(KT * P, W) if bias is None else 3 * P
        pr = sb("pr", [P, 2, nh, kw])
        pT = sb("pT", [P, 2, heads, KT, P])
        nm, sm, rc = sb("nm", [P, 2, nh]), sb("sm", [P, 2, nh]), sb("rc", [P, 2, nh])
        S = c.enter_context(nc.psum_tensor(f"{name}_S", [P, 4, 512], F32))
        Tp = c.enter_context(nc.psum_tensor(f"{name}_T", [P, 2, 512], F32))
        O = c.enter_context(nc.psum_tensor(f"{name}_O", [P, 2, 512], F32))
        if bias is not None:
            E = sb("E", [P, 2, nh, WIN_R, 3 * CB])
            EM = sb("EM", [P, 2, nh, 7, WIN_R, CB])
            em_block = {(0, 1): 0, (0, 2): 1, (1, 0): 2, (1, 1): 3, (1, 2): 4, (2, 0): 5, (2, 1): 6}
        flat = S[:].rearrange("p b n -> p (b n)")

        def scores_of(i, lo, n):
            at = i * W + (lo * P if bias is None else 0)
            return flat[:, at:at + n * P]

        with stage(nc, name, start=1, staged=2, vstaged=2, zeroed=None, tq=None, tk=None, eq=None, ek=None, scored=4,
                   maxed=4, exped=4, inverted=4, weighted=4, turned=2, emptied=2, pv=2, o_done=None,
                   dve_chain=None, e_in=2, em_done=2, reload=None, lowered=4) as (block, s):

            def count(i, p, u):
                return i * (2 * NU) + p * NU + u

            def used_before(p, u, bank):
                n = p * NU + u - 2
                return sum(1 for (a, b, _, _), k in bank_of.items() if k == bank and a * NU + b <= n)

            def par(p, u):
                n = p * NU + u
                return n % 2, n // 2

            @block.gpsimd
            def _(pool):
                if not split:
                    pool.memset(kT[:], 0.0).then_inc(s["zeroed"], 1)

                def body(i):
                    if bias is not None:
                        for p in range(2):
                            pool.wait_ge(s["e_in"][p], 1 + 16 * ROWS * (i + 1))
                            for x in range(nh):
                                pool.wait_ge(s["maxed"][x], 1 + count(i, 0, 0))
                            for kind in range(3):
                                mk = m["masks"].rearrange("p (z d k) -> p z d k", z=3, d=3)[:, kind]
                                for d in range(3):
                                    if (kind, d) not in em_block:
                                        continue
                                    for x in range(nh):
                                        last = pool.tensor_tensor(
                                            EM[:, p, x, em_block[kind, d]], E[:, p, x, :, d * CB:(d + 1) * CB],
                                            mk[:, d, :].unsqueeze(1).to_broadcast([P, WIN_R, CB]), ALU.add)
                            last.then_inc(s["em_done"][p], 1)
                    for p in range(2):
                        for u, (t, lo, hi) in enumerate(U):
                            b, before = par(p, u)
                            for x in range(nh):
                                pool.wait_ge(s["inverted"][x], 1 + count(i, p, u) + 1)
                                if combine is not None and x == 0:
                                    continue
                                w = pr[:, b, x, 0:(hi - lo) * P]
                                pool.tensor_tensor(w, w, rc[:, b, x:x + 1].to_broadcast([P, (hi - lo) * P]), ALU.mult).then_inc(s["weighted"][x], 1)
                loop(pool, pairs, body)

            @block.sync
            def _(sp):
                def load(i, p):
                    for dst, src in q_src(i, p, qs[:, p]):
                        sp.dma_start(dst, src).then_inc(s["staged"][p], 16)
                    if stage_k[p]:
                        for dst, src in k_src(i, p, ks[:, p]):
                            sp.dma_start(dst, src).then_inc(s["staged"][p], 16)
                    for dst, src in v_src(i, p, vs[:, p]):
                        sp.dma_start(dst, src).then_inc(s["vstaged"][p], 16)
                    if bias is not None:
                        for r in range(ROWS):
                            sp.dma_start(E[r * CB:(r + 1) * CB, p].rearrange("q h a b -> q h (a b)"),
                                         bias[:, ds((2 * i + p) * nh, nh), (7 - r) * 48:(15 - r) * 48]).then_inc(s["e_in"][p], 16)

                def refill(i):
                    for p in range(2):
                        sp.wait_ge(s["tq"], 1 + 2 * i + p + 1)
                        sp.sem_inc(s["reload"], 1)
                        sp.wait_ge(s["tk"], 1 + sum(stage_k) * i + sum(stage_k[:p + 1]))
                        sp.sem_inc(s["reload"], 1)
                        for b in range(2):
                            sp.wait_ge(s["pv"][b], 1 + i * NU + sum(1 for y in range((p + 1) * NU) if y % 2 == b))
                            sp.sem_inc(s["reload"], 1)
                        if bias is not None:
                            sp.wait_ge(s["em_done"][p], 1 + i + 1)
                        sp.sem_inc(s["reload"], 1)
                        load(i + 1, p)
                for p in range(2):
                    load(0, p)
                loop(sp, pairs - 1, refill)

            n_staged = [sum(len(f(0, p, b[:, p])) for f, b, on in ((q_src, qs, True), (k_src, ks, stage_k[p])) if on) for p in range(2)]
            n_v = [len(v_src(0, p, vs[:, p])) for p in range(2)]

            def q_place(x, t):
                return (S, x, t * P) if split else (S, t // 4, (t % 4) * P)

            def k_place(x, t):
                if not split:
                    return (S, 2 + t // 4, (t % 4) * P)
                return (S, 2 + x, t * P) if t < 4 else (O, 0, (2 * x + t - 4) * P)

            @block.tensor
            def _(pe):
                def scores(i, p, u, x):
                    t, lo, hi = U[u]
                    pe.wait_ge(s["exped"][x] if bias is None else s["maxed"][x], 1 + count(i, p, u))
                    qq = x if split else 0
                    cuts = [(a, min(hi, a + 4 - a % 4)) for a in ([lo] + [4] * (lo < 4 < hi))] if bias is None else [(lo, hi)]
                    for a, e in cuts:
                        at = x * W + (a * P if bias is None else 0)
                        last = pe.matmul(flat[:, at:at + (e - a) * P], qT[0:R, qq, t * P:(t + 1) * P],
                                         kT[0:R, x, a * P:e * P], start=True, stop=True)
                    last.then_inc(s["scored"][x], 1)

                def turn(i, p, u, x):
                    t, lo, hi = U[u]
                    b, before = par(p, u)
                    if combine is None:
                        pe.wait_ge(s["weighted"][x], 1 + count(i, p, u) + 1)
                    else:
                        pe.wait_ge(s["weighted"][0], 1 + count(i, p, u) + 1)
                    for n, kts in enumerate(pieces[u]):
                        bank, use = bank_of[p, u, x, n], use_of[p, u, x, n]
                        pe.wait_ge(s["emptied"][bank], 1 + i * per_bank + use)
                        for z, kt in enumerate(kts):
                            last = pe.transpose(Tp[:, bank, z * P:(z + 1) * P], pr[:, b, x, (kt - lo) * P:(kt - lo + 1) * P], m["ident"])
                        last.then_inc(s["turned"][bank], 1)

                def values(i, p, u):
                    t, lo, hi = U[u]
                    b, before = par(p, u)
                    mine = [y for y in torder if y[:2] == (p, u)]
                    for bank in range(2):
                        last_use = max((use_of[y] for y in mine if bank_of[y] == bank), default=None)
                        if last_use is not None:
                            pe.wait_ge(s["emptied"][bank], 1 + i * per_bank + last_use + 1)
                    if u == 0:
                        pe.wait_ge(s["vstaged"][p], 1 + 16 * n_v[p] * (i + 1))
                        pe.wait_ge(s["o_done"], 1 + 2 * i + p)
                    for kt in range(lo, hi):
                        for x in range(heads):
                            v = vs[:, p, kt, x * dv:(x + 1) * dv]
                            last = pe.matmul(O[x * dv:(x + 1) * dv, t // 4, (t % 4) * P:(t % 4 + 1) * P], v, pT[:, b, x, kt, :],
                                             start=(kt == lo), stop=(kt == hi - 1))
                    last.then_inc(s["pv"][b], 1)

                def body(i):
                    for p in range(2):
                        pe.wait_ge(s["staged"][p], 1 + 16 * n_staged[p] * (i + 1))
                        for x in range(nh):
                            pe.wait_ge(s["exped"][x], 1 + count(i, p, 0))
                        if split:
                            pe.wait_ge(s["o_done"], 1 + 2 * i + p)
                        for x in range(NS):
                            for t in range(tiles):
                                ten, bank, at = q_place(x, t)
                                last = pe.transpose(ten[0:R, bank, at:at + P], qs[:, p, x, t, :], m["ident"])
                        last.then_inc(s["tq"], 1)
                        if stage_k[p]:
                            for x in range(NS):
                                for t in range(KT):
                                    ten, bank, at = k_place(x, t)
                                    last = pe.transpose(ten[0:R, bank, at:at + P], ks[:, p, x, t, :], m["ident"])
                            last.then_inc(s["tk"], 1)
                        pe.wait_ge(s["eq"], 1 + 2 * i + p + 1)
                        pe.wait_ge(s["ek"], 1 + sum(stage_k) * i + sum(stage_k[:p + 1]))
                        for x in range(nh):
                            scores(i, p, 0, x)
                        for u in range(NU):
                            for x in range(nh):
                                if u + 1 < NU:
                                    scores(i, p, u + 1, x)
                                if x < heads:
                                    turn(i, p, u, x)
                            values(i, p, u)
                loop(pe, pairs, body)

            def empty_weights(eng, act, i, p, u, x):
                b, before = par(p, u)
                for n, kts in enumerate(pieces[u]):
                    bank, use = bank_of[p, u, x, n], use_of[p, u, x, n]
                    if bank != act:
                        continue
                    eng.wait_ge(s["turned"][bank], 1 + i * per_bank + use + 1)
                    eng.wait_ge(s["pv"][b], 1 + i * NU + before)
                    copy(nc, eng, act, pT[:, b, x, kts[0]:kts[-1] + 1, :],
                         Tp[:, bank, 0:len(kts) * P].rearrange("p (k q) -> p k q", q=P)).then_inc(s["emptied"][bank], 1)

            def highest(dve, i, p, u, x):
                t, lo, hi = U[u]
                b, before = par(p, u)
                n = hi - lo
                dve.wait_ge(s["scored"][x], 1 + count(i, p, u) + 1)
                if bias is None:
                    dve.wait_ge(s["exped"][x], 1 + count(i, p, u))
                    dve.tensor_reduce(nm[:, b, x:x + 1], scores_of(x, lo, n), AX.X, ALU.max, negate=True).then_inc(s["maxed"][x], 1)
                else:
                    kind = min(u, 1) if u < 3 else 2
                    dve.wait_ge(s["em_done"][p], 1 + i + 1)
                    dve.wait_ge(s["exped"][x], 1 + count(i, p, u))
                    for bank in range(2):
                        dve.wait_ge(s["turned"][bank], 1 + i * per_bank + used_before(p, u, bank))
                    w = pr[:, b, x, 0:n * P].rearrange("p (d r k) -> p d r k", r=WIN_R, k=CB)
                    at = em_block[kind, lo - t + 1]
                    dve.tensor_tensor(w, scores_of(x, 0, n).rearrange("p (d r k) -> p d r k", r=WIN_R, k=CB),
                                      EM[:, p, x, at:at + n], ALU.add).then_inc(s["maxed"][x], 1)
                    dve.wait_ge(s["maxed"][x], 1 + count(i, p, u) + 1)
                    dve.tensor_reduce(nm[:, b, x:x + 1], pr[:, b, x, 0:n * P], AX.X, ALU.max, negate=True).then_inc(s["lowered"][x], 1)

            def invert(dve, i, p, u, x, chain):
                b, before = par(p, u)
                dve.wait_ge(s["exped"][x], 1 + count(i, p, u) + 1)
                if combine is not None and x == 1:
                    chain(dve.reciprocal(rc[:, b, 1:2], sm[:, b, 1:2]))
                    dve.tensor_scalar(rc[:, b, 1:2], rc[:, b, 1:2], combine, None, ALU.mult).then_inc(s["inverted"][1], 1)
                else:
                    dve.reciprocal(rc[:, b, x:x + 1], sm[:, b, x:x + 1]).then_inc(s["inverted"][x], 1)

            @block.vector
            def _(dve):
                def body(i):
                    chain = Chain(dve, s["dve_chain"], 1 + i * 2 * NU)
                    for p in range(2):
                        dve.wait_ge(s["tq"], 1 + 2 * i + p + 1)
                        for x in range(NS):
                            for bk in range(1 if split else ob):
                                n = min(4, tiles - 4 * bk) * P
                                last = dve.tensor_copy(qT[0:R, x, bk * 512:bk * 512 + n], q_place(x, 4 * bk)[0][0:R, x if split else bk, 0:n])
                        last.then_inc(s["eq"], 1)
                        for x in range(nh):
                            highest(dve, i, p, 0, x)
                        for x in range(nh):
                            invert(dve, i, p, 0, x, chain)
                        for u in range(NU):
                            if combine is not None:
                                t, lo, hi = U[u]
                                b, before = par(p, u)
                                dve.wait_ge(s["weighted"][1], 1 + count(i, p, u) + 1)
                                dve.wait_ge(s["inverted"][0], 1 + count(i, p, u) + 1)
                                w0, w1 = pr[:, b, 0, 0:(hi - lo) * P], pr[:, b, 1, 0:(hi - lo) * P]
                                dve.scalar_tensor_tensor(out=w0, in0=w0, scalar=rc[:, b, 0:1], in1=w1, op0=ALU.mult,
                                                         op1=ALU.add).then_inc(s["weighted"][0], 1)
                            for x in range(nh):
                                if u + 1 < NU:
                                    highest(dve, i, p, u + 1, x)
                                if x < heads:
                                    empty_weights(dve, 0, i, p, u, x)
                                if u + 1 < NU:
                                    invert(dve, i, p, u + 1, x, chain)
                        for b in range(2):
                            dve.wait_ge(s["pv"][b], 1 + i * NU + sum(1 for y in range((p + 1) * NU) if y % 2 == b))
                        o = out(i, p)
                        for bk in range(ob):
                            n = min(4, tiles - 4 * bk) * P
                            dst, src = o[:, bk * 512:bk * 512 + n], O[:, bk, 0:n]
                            if gate is None:
                                last = dve.tensor_copy(dst, src)
                            else:
                                last = dve.tensor_tensor(dst, src, dst, ALU.mult)
                        last.then_inc(s["o_done"], 1)
                loop(dve, pairs, body)

            @block.scalar
            def _(act):
                def exponential(i, p, u, x):
                    t, lo, hi = U[u]
                    b, before = par(p, u)
                    act.wait_ge(s["maxed"][x] if bias is None else s["lowered"][x], 1 + count(i, p, u) + 1)
                    if bias is None:
                        act.wait_ge(s["turned"][0], 1 + i * per_bank + used_before(p, u, 0))
                        act.wait_ge(s["turned"][1], 1 + i * per_bank + used_before(p, u, 1))
                        src = scores_of(x, lo, hi - lo)
                    else:
                        src = pr[:, b, x, 0:(hi - lo) * P]
                    act.activation(pr[:, b, x, 0:(hi - lo) * P], src, ACT.Exp, bias=nm[:, b, x:x + 1],
                                   accum_out=sm[:, b, x:x + 1]).then_inc(s["exped"][x], 1)

                def body(i):
                    for p in range(2):
                        if stage_k[p]:
                            act.wait_ge(s["tk"], 1 + sum(stage_k) * i + sum(stage_k[:p + 1]))
                            if not split:
                                act.wait_ge(s["zeroed"], 1 + 1)
                            for x in range(nh):
                                rows = slice(0, R) if split else slice(x * (P // nh), (x + 1) * (P // nh))
                                for a in range(0, KT, 4):
                                    n = min(4, KT - a)
                                    ten, bank, at = k_place(x, a)
                                    last = act.activation(kT[rows, x, a * P:(a + n) * P], ten[rows, bank, at:at + n * P], ACT.Copy)
                            last.then_inc(s["ek"], 1)
                        for x in range(nh):
                            exponential(i, p, 0, x)
                        for u in range(NU):
                            for x in range(nh):
                                if u + 1 < NU:
                                    exponential(i, p, u + 1, x)
                                if x < heads:
                                    empty_weights(act, 1, i, p, u, x)
                loop(act, pairs, body)


def bias_table(nc, name, m, rpb, table):
    half = NA_HEADS // 2
    q = half * (2 * WIN_R - 1)
    wide = 4 * CB - 1
    with ExitStack() as c:
        pad = c.enter_context(nc.sbuf_tensor(f"{name}_pad", [P, 2, wide], F32))
        with stage(nc, name, zero=None, loaded=None, stored=None) as (block, s):
            @block.vector
            def _(dve):
                dve.memset(pad[:], 0.0).then_inc(s["zero"], 1)

            @block.sync
            def _(sp):
                sp.wait_ge(s["zero"], 1)
                sp.dma_start(pad[0:q, :, CB:CB + 2 * WIN_C - 1], rpb.rearrange("(a h) r c -> (h r) a c", a=2)).then_inc(s["loaded"], 16)
                sp.wait_ge(s["loaded"], 16)
                for cc in range(CB):
                    sp.dma_start(table[cc].rearrange("(a h) (r c) -> (h r) a c", a=2, c=3 * CB),
                                 pad[0:q, :, CB - 1 - cc:CB - 1 - cc + 3 * CB]).then_inc(s["stored"], 16)
                sp.wait_ge(s["stored"], 16 * CB)


def scale_tables(nc, name, jobs):
    with stage(nc, name, chain=None) as (block, s):
        @block.vector
        def _(dve):
            chain = Chain(dve, s["chain"])
            for out, in_, vec, swap, factor in jobs:
                n, w = in_.shape[1], in_.shape[2]
                if swap is None:
                    chain(dve.tensor_tensor(out, in_, vec.unsqueeze(1).to_broadcast([P, n, w]), ALU.mult))
                else:
                    h = w // (2 * swap)
                    for g in range(swap):
                        for a in range(2):
                            at, of = (2 * g + a) * h, (2 * g + 1 - a) * h
                            chain(dve.tensor_tensor(out[:, :, at:at + h], in_[:, :, at:at + h],
                                                    vec[:, of:of + h].unsqueeze(1).to_broadcast([P, n, h]), ALU.mult))
                if factor != 1.0:
                    chain(dve.tensor_scalar(out, out, factor, None, ALU.mult))


def modulation(nc, name, m, w, b_cols, b_gate, norm, gain, shift, gate, conds):
    NC = 3 * D // 512
    with ExitStack() as c:
        sb = lambda n, s: c.enter_context(nc.sbuf_tensor(f"{name}_{n}", s, F32))
        wb = sb("w", [P, 2, DK, 1024])
        sc = sb("silu", [P, DK, 2])
        rows = sb("rows", [P, 2, 512])
        cols, bg = sb("cols", [P, 4, P]), sb("bg", [P, D])
        ps = c.enter_context(nc.psum_tensor(f"{name}_ps", [P, 2, 512], F32))
        pt = c.enter_context(nc.psum_tensor(f"{name}_pt", [P, 512], F32))
        pg = c.enter_context(nc.psum_tensor(f"{name}_pg", [P, 4, 512], F32))
        with stage(nc, name, loaded=2, silu=None, mm=None, zeroed=None, rows_done=None, turned=None,
                   spread=None, chain=None, bg=None) as (block, s):
            src = w.rearrange("(k p) n -> p k n", p=P)

            @block.sync
            def _(sp):
                sp.dma_start(bg[:], b_gate).then_inc(s["bg"], 16)
                for x in range(3):
                    if x == 2:
                        sp.wait_ge(s["mm"], 1)
                    sp.dma_start(wb[:, x % 2], src[:, :, x * 1024:(x + 1) * 1024]).then_inc(s["loaded"][x % 2], 16)

            @block.scalar
            def _(act):
                act.activation(sc[:], m["cond"].rearrange("p (k c) -> p k c", c=2), ACT.Silu).then_inc(s["silu"], 1)

            @block.tensor
            def _(pe):
                pe.wait_ge(s["silu"], 1)
                for x in range(3):
                    pe.wait_ge(s["loaded"][x % 2], 16 * (x // 2 + 1))
                    for k in range(DK):
                        for y in range(2):
                            j = (2 * x + y) % 4
                            last = pe.matmul(ps[32 * j:32 * j + 2, x // 2, :], sc[:, k, :], wb[:, x % 2, k, y * 512:(y + 1) * 512],
                                             start=(k == 0), stop=(k == DK - 1))
                    last.then_inc(s["mm"], 1)
                pe.wait_ge(s["rows_done"], 6)
                for b in range(4):
                    last = pe.transpose(pt[:, b * P:(b + 1) * P], rows[:, 0, b * P:(b + 1) * P], m["ident"])
                last.then_inc(s["turned"], 1)
                for j in range(2):
                    for x in range(conds):
                        last = pe.matmul(pg[:, 2 * j + x, :], m["select"].rearrange("p (j q) -> p j q", q=P)[:, 2 * j + x, :], rows[:, 1, :],
                                         start=True, stop=True)
                last.then_inc(s["spread"], 1)

            @block.vector
            def _(dve):
                chain = Chain(dve, s["chain"])
                dve.memset(rows[:], 0.0).then_inc(s["zeroed"], 1)
                dve.wait_ge(s["zeroed"], 1)
                for x in range(3):
                    dve.wait_ge(s["mm"], x + 1)
                    for y in range(2):
                        j = (2 * x + y) % 4
                        dve.tensor_copy(rows[32 * j:32 * j + 2, x // 2, :], ps[32 * j:32 * j + 2, x // 2, :]).then_inc(s["rows_done"], 1)
                dve.wait_ge(s["turned"], 1)
                chain(dve.tensor_copy(cols[:], pt[:].rearrange("p (b q) -> p b q", q=P)))
                for t in range(AT):
                    x = 0 if t < XT else 1
                    for half in range(2):
                        bb = b_cols[:, half * 4:half * 4 + 4]
                        dve.tensor_tensor(shift[:, t, half * 4:half * 4 + 4], cols[:, :, 32 * half + x], bb, ALU.add)
                        g = gain[:, t, half * 4:half * 4 + 4]
                        bb = b_cols[:, DK + half * 4:DK + half * 4 + 4]
                        chain(dve.tensor_tensor(g, cols[:, :, 32 * (2 + half) + x], bb, ALU.add))
                        chain(dve.scalar_tensor_tensor(out=g, in0=g, scalar=1.0, in1=norm[:, half * 4:half * 4 + 4], op0=ALU.add, op1=ALU.mult))
                dve.wait_ge(s["spread"], 1)
                dve.wait_ge(s["bg"], 16)
                for j in range(2):
                    for x in range(conds):
                        chain(dve.tensor_tensor(gate[:, x, j * 512:(j + 1) * 512], pg[:, 2 * j + x, :], bg[:, j * 512:(j + 1) * 512], ALU.add))


def first_of(dve, chain, out, x, top, prio, best, n):
    shape = list(x.shape)
    chain(dve.tensor_tensor(out, x, top.unsqueeze(2).to_broadcast(shape), ALU.is_equal))
    chain(dve.tensor_tensor(out, out, prio.unsqueeze(1).to_broadcast(shape), ALU.mult))
    chain(dve.tensor_reduce(best, out, AX.X, ALU.max))
    chain(dve.tensor_tensor(out, out, best.unsqueeze(2).to_broadcast(shape), ALU.is_equal))


def route(nc, name, m, act_t, w_router, slots_init, slot_ids_dram, slots, block_expert, n_pairs):
    NL = N_GROUPS + N_EXPERTS
    with ExitStack() as c:
        sb = lambda n, s, dt=F32: c.enter_context(nc.sbuf_tensor(f"{name}_{n}", s, dt))
        wr, L = sb("wr", [P, DK, NL]), sb("L", [P, XT, NL])
        top_g, best, sum_g = sb("top_g", [P, XT]), sb("best", [P, XT]), sb("sum_g", [P, XT])
        G, z = sb("G", [P, XT, N_GROUPS]), sb("z", [P, XT, N_GROUPS])
        picked = sb("picked", [P, XT, N_GROUPS, PER_GROUP])
        el = sb("el", [P, XT, PER_GROUP])
        E = sb("E", [P, 2, XT, PER_GROUP])
        top_e = sb("top_e", [P, 2, XT])
        ratio, wt = sb("ratio", [P, XT]), sb("wt", [P, 2, XT])
        O = sb("O", [P, 2, XT, N_GROUPS, PER_GROUP])
        A = sb("A", [P, XT, N_EXPERTS])
        pos, dest = sb("pos", [P, XT, N_EXPERTS]), sb("dest", [P, 2, XT])
        dest_i = sb("dest_i", [P, 2, XT], I32)
        rows = sb("rows", [P, 2, XT, 4], I32)
        ids = sb("ids", [P, 2, XT, 2], I32)
        cnt, nb, upto, start, one = (sb(x, [P, N_EXPERTS]) for x in ("cnt", "nb", "upto", "start", "one"))
        cmp, be = sb("cmp", [P, MAX_BLOCKS, N_EXPERTS]), sb("be", [P, MAX_BLOCKS])
        pl = c.enter_context(nc.psum_tensor(f"{name}_pl", [P, XT, P], F32))
        pk = c.enter_context(nc.psum_tensor(f"{name}_pk", [P, 8, N_EXPERTS], F32))
        with stage(nc, name, loaded=None, logits=None, chosen=None, ranked=None, chain=None, low=None, exped=None,
                   init=None, table=None, put=None) as (block, s):
            @block.sync
            def _(sp):
                sp.dma_start(slots, slots_init).then_inc(s["init"], 16)
                sp.dma_start(wr[:], w_router.rearrange("(k p) n -> p k n", p=P)).then_inc(s["loaded"], 16)
                sp.dma_start(ids[:].rearrange("p a b c -> p (a b c)"), slot_ids_dram).then_inc(s["loaded"], 16)

            @block.tensor
            def _(pe):
                pe.wait_ge(s["loaded"], 32)
                for t in range(XT):
                    for k in range(DK):
                        last = pe.matmul(pl[:, t, 0:NL], act_t[:, k, t * P:(t + 1) * P], wr[:, k, :], start=(k == 0), stop=(k == DK - 1))
                last.then_inc(s["logits"], 1)
                pe.wait_ge(s["chosen"], 1)
                for t in range(XT + 1):
                    for b in range(t + (t < XT)):
                        last = pe.matmul(pk[:, t, :], m["before"] if b == t else m["ones"], A[:, b, :], start=(b == 0),
                                         stop=(b == t + (t < XT) - 1))
                last.then_inc(s["ranked"], 1)

            @block.scalar
            def _(act):
                act.wait_ge(s["low"], 1)
                act.activation(z[:], z[:], ACT.Exp).then_inc(s["exped"], 1)
                act.wait_ge(s["low"], 2)
                act.activation(ratio[:], ratio[:], ACT.Exp).then_inc(s["exped"], 1)

            @block.vector
            def _(dve):
                chain = Chain(dve, s["chain"])
                dve.wait_ge(s["logits"], 1)
                chain(dve.tensor_copy(L[:], pl[:, :, 0:NL]))
                LG, LE = L[:, :, 0:N_GROUPS], L[:, :, N_GROUPS:NL].rearrange("p t (g e) -> p t g e", g=N_GROUPS)
                chain(dve.tensor_reduce(top_g[:], LG, AX.X, ALU.max))
                dve.tensor_tensor(z[:], LG, top_g[:].unsqueeze(2).to_broadcast([P, XT, N_GROUPS]), ALU.subtract).then_inc(s["low"], 1)
                first_of(dve, chain, G[:], LG, top_g[:], m["prio4"], best[:], N_GROUPS)
                chain(dve.tensor_tensor(picked[:], LE, G[:].unsqueeze(3).to_broadcast([P, XT, N_GROUPS, PER_GROUP]), ALU.mult))
                chain(dve.tensor_reduce(el[:], picked[:].rearrange("p t g e -> p t e g"), AX.X, ALU.add))
                for x in range(2):
                    chain(dve.tensor_reduce(top_e[:, x], el[:], AX.X, ALU.max))
                    first_of(dve, chain, E[:, x], el[:], top_e[:, x], m["prio8"], best[:], PER_GROUP)
                    if x == 0:
                        chain(dve.scalar_tensor_tensor(out=el[:], in0=E[:, 0], scalar=NEG, in1=el[:], op0=ALU.mult, op1=ALU.add))
                dve.tensor_tensor(ratio[:], top_e[:, 1], top_e[:, 0], ALU.subtract).then_inc(s["low"], 1)
                for x in range(2):
                    chain(dve.tensor_tensor(O[:, x], G[:].unsqueeze(3).to_broadcast([P, XT, N_GROUPS, PER_GROUP]),
                                            E[:, x].unsqueeze(2).to_broadcast([P, XT, N_GROUPS, PER_GROUP]), ALU.mult))
                flat = lambda v: v.rearrange("p t g e -> p t (g e)")
                dve.tensor_tensor(A[:], flat(O[:, 0]), flat(O[:, 1]), ALU.add).then_inc(s["chosen"], 1)
                dve.wait_ge(s["exped"], 1)
                chain(dve.tensor_reduce(sum_g[:], z[:], AX.X, ALU.add))
                dve.wait_ge(s["exped"], 2)
                chain(dve.tensor_scalar(wt[:, 1], ratio[:], 1.0, None, ALU.add))
                chain(dve.tensor_tensor(wt[:, 1], wt[:, 1], sum_g[:], ALU.mult))
                chain(dve.reciprocal(wt[:, 0], wt[:, 1]))
                chain(dve.tensor_tensor(wt[:, 1], wt[:, 0], ratio[:], ALU.mult))
                chain(dve.memset(one[:], 1.0))
                chain(dve.memset(rows[:], 0))
                chain(dve.tensor_copy(rows[:, :, :, 0:2], ids[:]))
                chain(dve.tensor_copy(rows[:].bitcast(F32)[:, :, :, 2], wt[:]))
                dve.wait_ge(s["ranked"], 1)
                chain(dve.tensor_copy(cnt[:], pk[:, XT, :]))
                chain(dve.tensor_scalar(nb[:], cnt[:], 0.0, None, ALU.is_gt))
                for b in range(1, SEQ // CAP):
                    chain(dve.scalar_tensor_tensor(out=nb[:], in0=cnt[:], scalar=float(b * CAP), in1=nb[:], op0=ALU.is_gt, op1=ALU.add))
                chain(dve.tensor_tensor_scan(upto[:], one[:], nb[:], 0.0, ALU.mult, ALU.add))
                chain(dve.tensor_tensor(start[:], upto[:], nb[:], ALU.subtract))
                chain(dve.tensor_scalar(start[:], start[:], float(CAP), None, ALU.mult))
                chain(dve.tensor_tensor(pos[:], pk[:, 0:XT, :], start[:].unsqueeze(1).to_broadcast([P, XT, N_EXPERTS]), ALU.add))
                for x in range(2):
                    chain(dve.tensor_tensor(A[:], flat(O[:, x]), pos[:], ALU.mult))
                    chain(dve.tensor_reduce(dest[:, x], A[:], AX.X, ALU.add))
                chain(dve.tensor_copy(dest_i[:], dest[:]))
                chain(dve.tensor_tensor(cmp[:], upto[:].unsqueeze(1).to_broadcast([P, MAX_BLOCKS, N_EXPERTS]),
                                        m["block_no"].unsqueeze(2).to_broadcast([P, MAX_BLOCKS, N_EXPERTS]), ALU.is_le))
                chain(dve.tensor_reduce(be[:], cmp[:], AX.X, ALU.add))
                chain(dve.tensor_scalar(be[:], be[:], float(N_EXPERTS - 1), None, ALU.min))
                chain(dve.tensor_copy(block_expert, be[0:1, :]))
                even = m["block_no"].rearrange("p (i a) -> p i a", a=2)[:, :, 0]
                total = upto[:, N_EXPERTS - 1:N_EXPERTS]
                chain(dve.tensor_tensor(be[:, 0:MAX_BLOCKS // 2], even, total.to_broadcast([P, MAX_BLOCKS // 2]), ALU.is_lt))
                chain(dve.tensor_reduce(total, be[:, 0:MAX_BLOCKS // 2], AX.X, ALU.add))
                dve.tensor_copy(n_pairs, total[0:1]).then_inc(s["table"], 1)

            @block.gpsimd
            def _(pool):
                pool.wait_ge(s["init"], 16)
                pool.wait_ge(s["table"], 1)
                for n in range(2 * XT):
                    pool.indirect_dma_start(out=slots, out_offset=bass.IndirectOffsetOnAxis(ap=dest_i[:, n // XT, n % XT:n % XT + 1], axis=0),
                                            in_=rows[:, n // XT, n % XT, :], in_offset=None).then_inc(s["put"], 16)
                    pool.wait_ge(s["put"], 16 * (n + 1))


def expert_blocks(nc, name, m, block_expert, n_pairs, slots, halves, xn, w1, w3, w2, ys):
    H2 = D_EXPERT // 2
    FK = D_EXPERT // P
    FIRST = 2
    TB = MAX_BLOCKS + 2
    with ExitStack() as c:
        sb = lambda n, s, dt=F32: c.enter_context(nc.sbuf_tensor(f"{name}_{n}", s, dt))
        w1b, w3b, w2b = sb("w1", [P, 2, DK, D_EXPERT]), sb("w3", [P, 2, DK, D_EXPERT]), sb("w2", [P, 2, FK, D])
        meta, index = sb("meta", [P, TB, 4], I32), sb("index", [P, 2, TB], I32)
        xg, xT = sb("xg", [P, 2, D // 2]), sb("xT", [P, 4, P])
        sact, hid, hT, yb = sb("silu", [P, H2]), sb("hid", [P, H2]), sb("hT", [P, 2, P]), sb("y", [P, 2, D // 2])
        hv, current = sb("halves", [P, 2], I32), sb("current", [P, 2, 2], I32)
        bank = lambda n: c.enter_context(nc.psum_tensor(f"{name}_{n}", [P, 512], F32))
        px, p1, p3, ph, py = bank("px"), bank("p1"), bank("p3"), bank("ph"), bank("py")
        x_rows = xn.rearrange("t (a d) -> (t a) d", a=2)
        y_rows = ys.rearrange("t (a d) -> (t a) d", a=2)
        with stage(nc, name, start=FIRST, software_dma=("got", "put"), halves=None, w1=2, w3=2, w2=2, idx=None,
                   got=2, x_turned=None, x_in=None, h1=None, h3=None, silu=None, hid=None, h_turned=None,
                   h_in=None, y=None, y_out=None, current=None, go=None, put=2) as (block, s):
            trips = lambda eng: eng.value_load(n_pairs, min_val=1, max_val=MAX_BLOCKS // 2)

            @block.sync
            def _(sp):
                sp.dma_start(hv[:], halves).then_inc(s["halves"], 16)
                with sp.Fori(0, trips(sp)) as i:
                    for p in range(2):
                        e = sp.value_load(block_expert[:, ds(2 * i + p, 1)], min_val=0, max_val=N_EXPERTS - 1)
                        for w, wb, got, done in ((w1, w1b, "w1", "h1"), (w3, w3b, "w3", "h3"), (w2, w2b, "w2", "y")):
                            sp.wait_ge(s[done], FIRST + 2 * i + p - 1)
                            sp.dma_start(wb[:, p], w[ds(e, 1)].rearrange("a (k p) n -> p (a k) n", p=P)).then_inc(s[got][p], 16)

            @block.gpsimd
            def _(pool):
                def indices(which, p, b):
                    pool.tensor_copy(current[:, which, p:p + 1], index[:, which, ds(b, 1)]).then_inc(s["current"], 1)

                def gather(p):
                    pool.indirect_dma_start(out=xg[:, p, :], out_offset=None, in_=x_rows,
                                            in_offset=bass.IndirectOffsetOnAxis(ap=current[:, 0, p:p + 1], axis=0)).then_inc(s["got"][p], 16)
                for h in range(2):
                    pool.dma_start(meta[h * CAP:(h + 1) * CAP], slots.rearrange("(b s) f -> s b f", s=CAP)).then_inc(s["put"][h], 16)
                pool.wait_ge(s["put"][0], 16)
                pool.wait_ge(s["put"][1], 16)
                pool.wait_ge(s["halves"], FIRST + 16)
                pool.tensor_tensor(index[:], meta[:, :, 0:2].rearrange("p b a -> p a b"), hv[:].unsqueeze(2).to_broadcast([P, 2, TB]), ALU.add).then_inc(s["idx"], 1)
                pool.wait_ge(s["idx"], FIRST + 1)
                for p in range(2):
                    indices(0, p, p)
                    pool.wait_ge(s["current"], FIRST + p + 1)
                    gather(p)
                with pool.Fori(0, trips(pool)) as i:
                    for p in range(2):
                        pool.wait_ge(s["x_turned"], FIRST + 2 * i + p + 1)
                        pool.sem_inc(s["go"], 1)
                        pool.wait_ge(s["got"][p], 16 * i + 16)
                        pool.sem_inc(s["go"], 1)
                        pool.wait_ge(s["put"][p], 16 * i + 16)
                        pool.sem_inc(s["go"], 1)
                        indices(0, p, 2 * i + p + 2)
                        indices(1, p, 2 * i + p)
                        pool.wait_ge(s["current"], FIRST + 2 + 4 * i + 2 * p + 2)
                        pool.sem_inc(s["go"], 1)
                        gather(p)
                        pool.wait_ge(s["y_out"], FIRST + 2 * i + p + 1)
                        pool.sem_inc(s["go"], 1)
                        pool.wait_ge(s["put"][1 - p], 16 * (i + p) + 16)
                        pool.sem_inc(s["go"], 1)
                        pool.indirect_dma_start(out=y_rows, out_offset=bass.IndirectOffsetOnAxis(ap=current[:, 1, p:p + 1], axis=0),
                                                in_=yb[:, p, :], in_offset=None).then_inc(s["put"][p], 16)
                pairs = trips(pool)
                for p in range(2):
                    pool.wait_ge(s["got"][p], 16 * pairs + 16)
                    pool.sem_inc(s["go"], 1)
                    pool.wait_ge(s["put"][p], 16 * pairs + 16)
                    pool.sem_inc(s["go"], 1)

            @block.tensor
            def _(pe):
                def turn_x(p, i):
                    pe.wait_ge(s["got"][p], 16 * i + 16)
                    for j in range(4):
                        last = pe.transpose(px[:, j * P:(j + 1) * P], xg[:, p, j * P:(j + 1) * P], m["ident"])
                    last.then_inc(s["x_turned"], 1)
                turn_x(0, 0)
                with pe.Fori(0, trips(pe)) as i:
                    for p in range(2):
                        b = 2 * i + p
                        pe.wait_ge(s["x_in"], FIRST + b + 1)
                        for got, wb, out, done, used in (("w1", w1b, p1, "h1", "silu"), ("w3", w3b, p3, "h3", "hid")):
                            pe.wait_ge(s[got][p], FIRST + 16 * i + 16)
                            pe.wait_ge(s[used], FIRST + b)
                            for k in range(DK):
                                x = xT[:, k % 4, (k // 4) * CAP:(k // 4 + 1) * CAP]
                                for h in range(2):
                                    last = pe.matmul(out[h * CAP:(h + 1) * CAP, 0:H2], x, wb[:, p, k, h * H2:(h + 1) * H2],
                                                     start=(k == 0), stop=(k == DK - 1))
                            last.then_inc(s[done], 1)
                        turn_x(1 - p, i + p)
                        pe.wait_ge(s["hid"], FIRST + b + 1)
                        for j in range(2):
                            last = pe.transpose(ph[:, j * P:(j + 1) * P], hid[:, j * P:(j + 1) * P], m["ident"])
                        last.then_inc(s["h_turned"], 1)
                        pe.wait_ge(s["w2"][p], FIRST + 16 * i + 16)
                        pe.wait_ge(s["h_in"], FIRST + b + 1)
                        pe.wait_ge(s["y_out"], FIRST + b)
                        for f in range(FK):
                            x = hT[:, f % 2, (f // 2) * CAP:(f // 2 + 1) * CAP]
                            for h in range(2):
                                last = pe.matmul(py[h * CAP:(h + 1) * CAP, :], x, w2b[:, p, f, h * 512:(h + 1) * 512],
                                                 start=(f == 0), stop=(f == FK - 1))
                        last.then_inc(s["y"], 1)

            @block.scalar
            def _(act):
                with act.Fori(0, trips(act)) as i:
                    for p in range(2):
                        b = 2 * i + p
                        act.wait_ge(s["h1"], FIRST + b + 1)
                        act.wait_ge(s["hid"], FIRST + b)
                        act.activation(sact[:], p1[:, 0:H2], ACT.Silu).then_inc(s["silu"], 1)
                        act.wait_ge(s["y"], FIRST + b + 1)
                        act.wait_ge(s["put"][p], 16 * i + 16)
                        act.activation(yb[:, p, :], py[:], ACT.Copy,
                                       scale=meta[:].bitcast(F32)[:, ds(b, 1), 2]).then_inc(s["y_out"], 1)

            @block.vector
            def _(dve):
                gain = m["g_ffn"].rearrange("p (h j) -> p j h", h=2).unsqueeze(3).to_broadcast([P, 4, 2, CAP])

                def take_x(b):
                    dve.wait_ge(s["x_turned"], FIRST + b + 1)
                    dve.wait_ge(s["h3"], FIRST + b)
                    dve.tensor_tensor(xT[:].rearrange("p j (h q) -> p j h q", h=2),
                                      px[:].rearrange("p (j h q) -> p j h q", j=4, h=2), gain, ALU.mult).then_inc(s["x_in"], 1)
                take_x(0)
                with dve.Fori(0, trips(dve)) as i:
                    for p in range(2):
                        b = 2 * i + p
                        dve.wait_ge(s["silu"], FIRST + b + 1)
                        dve.wait_ge(s["h3"], FIRST + b + 1)
                        dve.wait_ge(s["h_turned"], FIRST + b)
                        dve.tensor_tensor(hid[:], p3[:, 0:H2], sact[:], ALU.mult).then_inc(s["hid"], 1)
                        take_x(b + 1)
                        dve.wait_ge(s["h_turned"], FIRST + b + 1)
                        dve.wait_ge(s["y"], FIRST + b)
                        dve.tensor_copy(hT[:].rearrange("p j q -> p (j q)"), ph[:, 0:2 * P]).then_inc(s["h_in"], 1)


def add_experts(nc, name, ys, h):
    with ExitStack() as c:
        y = c.enter_context(nc.sbuf_tensor(f"{name}_y", [P, 2, XT, D], F32))
        with stage(nc, name, loaded=2, chain=None) as (block, s):
            @block.sync
            def _(sp):
                for x in range(2):
                    sp.dma_start(y[:, x], ys[x * SEQ:(x + 1) * SEQ, :].rearrange("(t p) d -> p t d", p=P)).then_inc(s["loaded"][x], 16)

            @block.vector
            def _(dve):
                chain = Chain(dve, s["chain"])
                for x in range(2):
                    dve.wait_ge(s["loaded"][x], 16)
                    chain(dve.tensor_tensor(h[:, 0:XT], h[:, 0:XT], y[:, x], ALU.add))


def load(nc, name, pairs):
    with stage(nc, name, sp_in=None, act_in=None) as (block, s):
        @block.sync
        def _(sp):
            for out, in_ in pairs[0::2]:
                sp.dma_start(out, in_).then_inc(s["sp_in"], 16)
            sp.wait_ge(s["sp_in"], 16 * len(pairs[0::2]))

        if len(pairs) > 1:
            @block.scalar
            def _(act):
                for out, in_ in pairs[1::2]:
                    act.dma_start(out, in_).then_inc(s["act_in"], 16)
                act.wait_ge(s["act_in"], 16 * len(pairs[1::2]))


def lambda_scalar(nc, name, m, neg_lam):
    with ExitStack() as c:
        prod = c.enter_context(nc.sbuf_tensor(f"{name}_prod", [P, 2, 64], F32))
        dots = c.enter_context(nc.sbuf_tensor(f"{name}_dots", [P, 2], F32))
        with stage(nc, name, chain=None, dots=None, exped=None) as (block, s):
            v = m["lam"].rearrange("p (a b d) -> p a b d", a=2, b=2)

            @block.vector
            def _(dve):
                chain = Chain(dve, s["chain"])
                chain(dve.tensor_tensor(prod[:], v[:, :, 0], v[:, :, 1], ALU.mult))
                dve.tensor_reduce(dots[:], prod[:], AX.X, ALU.add).then_inc(s["dots"], 1)
                dve.wait_ge(s["exped"], 1)
                chain(dve.tensor_tensor(neg_lam, dots[:, 1:2], dots[:, 0:1], ALU.subtract))
                chain(dve.tensor_scalar(neg_lam, neg_lam, -LAM_INIT, None, ALU.add))

            @block.scalar
            def _(act):
                act.wait_ge(s["dots"], 1)
                act.activation(dots[:], dots[:], ACT.Exp).then_inc(s["exped"], 1)


def sub_norm(nc, name, m, o, heads):
    with ExitStack() as c:
        sb = lambda n, s: c.enter_context(nc.sbuf_tensor(f"{name}_{n}", s, F32))
        half = sb("half", [P, SEQ])
        sq, root, inv, g = sb("sq", [P, heads, SEQ]), sb("root", [P, heads, SEQ]), sb("inv", [P, heads, SEQ]), sb("g", [P, 1])
        ps = c.enter_context(nc.psum_tensor(f"{name}_ps", [P, heads, SEQ], F32))
        with stage(nc, name, sq=None, summed=None, rooted=None, chain=None) as (block, s):
            @block.scalar
            def _(act):
                for h in range(heads):
                    act.activation(sq[:, h], o[:, h], ACT.Square).then_inc(s["sq"], 1)
                for h in range(heads):
                    act.wait_ge(s["summed"], h + 1)
                    act.activation(root[:, h], ps[:, h], ACT.Sqrt, bias=m["eps"], scale=1.0 / P).then_inc(s["rooted"], 1)

            @block.tensor
            def _(pe):
                for h in range(heads):
                    pe.wait_ge(s["sq"], h + 1)
                    pe.matmul(ps[:, h], m["ones"], sq[:, h], start=True, stop=True).then_inc(s["summed"], 1)

            @block.vector
            def _(dve):
                chain = Chain(dve, s["chain"])
                chain(dve.tensor_scalar(g[:], m["g_sub"], 1.0 - LAM_INIT, None, ALU.mult))
                for h in range(heads):
                    dve.wait_ge(s["rooted"], h + 1)
                    chain(inverse_root(dve, chain, ps[:, h], root[:, h], P, half[:], inv[:, h]))
                    chain(dve.scalar_tensor_tensor(out=o[:, h], in0=o[:, h], scalar=g[:], in1=inv[:, h], op0=ALU.mult, op1=ALU.mult))


def add_side(nc, name, m, g_ple, y, gate, h):
    with ExitStack() as c:
        sb = lambda n, s: c.enter_context(nc.sbuf_tensor(f"{name}_{n}", s, F32))
        sq, st, wide = sb("sq", [P, D]), sb("st", [P, 4, XT]), sb("g", [P, D])
        with stage(nc, name, chain=None, act_chain=None, rooted=None, loaded=None) as (block, s):
            @block.sync
            def _(sp):
                sp.dma_start(wide[:], g_ple).then_inc(s["loaded"], 16)

            @block.scalar
            def _(act):
                chain = Chain(act, s["act_chain"])
                for t in range(XT):
                    chain(act.activation(sq[:], y[:, t], ACT.Square, accum_out=st[:, 0, t:t + 1]))
                act.activation(st[:, 1], st[:, 0], ACT.Sqrt, bias=m["eps"], scale=1.0 / D).then_inc(s["rooted"], 1)

            @block.vector
            def _(dve):
                chain = Chain(dve, s["chain"])
                dve.wait_ge(s["loaded"], 16)
                chain(dve.tensor_tensor(gate, gate, wide[:].unsqueeze(1).to_broadcast([P, XT, D]), ALU.mult))
                dve.wait_ge(s["rooted"], 1)
                chain(inverse_root(dve, chain, st[:, 0], st[:, 1], D, st[:, 3], st[:, 2]))
                for t in range(XT):
                    chain(dve.scalar_tensor_tensor(out=gate[:, t], in0=y[:, t], scalar=st[:, 2, t:t + 1], in1=gate[:, t], op0=ALU.mult, op1=ALU.mult))
                    chain(dve.tensor_tensor(h[:, t], h[:, t], gate[:, t], ALU.add))


def store_to(nc, dst, width):
    return lambda eng, is_act, t, c, ps, tmp, chain: copy(nc, eng, is_act, dst[:, t, ds(c * width, width)], ps)


def add_to(h):
    return lambda eng, is_act, t, c, ps, tmp, chain: eng.tensor_tensor(h[:, t, ds(c * 512, 512)], h[:, t, ds(c * 512, 512)], ps, ALU.add)


def add_gated(h, gate):
    def emit(eng, is_act, t, c, ps, tmp, chain):
        chain(eng.tensor_tensor(tmp, ps, gate[:, 0 if t < XT else 1, ds(c * 512, 512)], ALU.mult))
        dst = h[:, t, ds(c * 512, 512)]
        return eng.tensor_tensor(dst, dst, tmp, ALU.add)
    return emit


def tokens_of(a):
    return lambda k, t: a[:, k, t * P:(t + 1) * P]


def build(nc, A, prm_at, const_at, stop=None, dbg=None):
    with ExitStack() as top:
        def sb(c, name, shape, dt=F32):
            return c.enter_context(nc.sbuf_tensor(name, shape, dt))

        prm = sb(top, "params", [P, sum(n for _, n in prm_at.values())])
        cst = sb(top, "consts", [P, sum(n for _, n in const_at.values())])
        m = {k: prm[:, a:a + n] for k, (a, n) in prm_at.items()}
        m.update({k: cst[:, a:a + n] for k, (a, n) in const_at.items()})
        hx = sb(top, "residual", [P, AT, D])
        rows = lambda v: v.rearrange("(t p) d -> p t d", p=P)
        tiles = lambda v, w: v.rearrange("p (t w) -> p t w", w=w)
        table = nc.dram_tensor("bias_rows", [CB, NA_HEADS, (2 * WIN_R - 1) * 3 * CB], F32).ap()
        slots = nc.dram_tensor("slots", [(MAX_BLOCKS + 2) * CAP, 4], I32).ap()
        xn = nc.dram_tensor("expert_in", [SEQ, D], F32).ap()
        ys = nc.dram_tensor("expert_out", [2 * SEQ + CAP, D], F32).ap()

        def debug(key, ap):
            if stop == key:
                load(nc, "dbg", [(dbg, ap)])
                return True

        load(nc, "load", [(prm[:], A["params"]), (cst[:], A["consts"]),
                          (hx[:, 0:XT], rows(A["x"])), (hx[:, XT:AT], rows(A["ctx"]))])
        if debug("load", hx[:, 0:XT]): return

        with ExitStack() as c:
            oT = sb(c, "mix_out", [P, DK, SEQ])
            with ExitStack() as cc:
                proj = sb(cc, "mix_proj", [P, XT, 3 * D])
                bias_table(nc, "rpb", m, A["rpb"], table)
                with ExitStack() as ca:
                    aT = sb(ca, "mix_in", [P, DK, SEQ])
                    norm_transpose(nc, "mix_norm", m, lambda t: hx[:, ds(t, 1), :].rearrange("p a d -> p (a d)"), DK, XT, m["g_mix"], None, aT)
                    if debug("aT", aT[:, :, :]): return
                    dense(nc, "mix_in_w", tokens_of(aT), DK, XT, A["w_in"], 6, 512, store_to(nc, proj, 512))
                if debug("proj", proj[:, :, 0:1024]): return
                tabs = sb(cc, "mix_tabs", [P, 4, XT, 64])
                gains = sb(cc, "mix_gains", [P, 2, 1, NA_D])
                neg_lam = sb(cc, "neg_lam", [P, 1])
                sa, sn = 64 ** -0.5, NA_D ** -0.5
                scale_tables(nc, "mix_tab", [
                    (tabs[:, 0], tiles(m["full_cos"], 64), m["g_qa"], None, sa), (tabs[:, 1], tiles(m["full_sin"], 64), m["g_qa"], 1, sa),
                    (tabs[:, 2], tiles(m["full_cos"], 64), m["g_ka"], None, 1.0), (tabs[:, 3], tiles(m["full_sin"], 64), m["g_ka"], 1, 1.0),
                    (gains[:, 0], m["ones"][:, 0:NA_D].unsqueeze(1), m["g_qb"], None, sn), (gains[:, 1], m["ones"][:, 0:NA_D].unsqueeze(1), m["g_kb"], None, 1.0)])
                lambda_scalar(nc, "lam", m, neg_lam[:])

                def part(col, n, d):
                    return lambda t: proj[:, ds(t, 1), col:col + n * d].rearrange("p a (h d) -> p (a h) d", d=d)

                def row(tab):
                    return lambda t: tab[:, ds(t, 1), :].rearrange("p a d -> p (a d)")
                head_norms(nc, "mix_hn", m, XT, [
                    (part(0, 8, 64), 8, 64, row(tabs[:, 0]), (0, 1, 32, row(tabs[:, 1]))),
                    (part(512, 8, 64), 8, 64, row(tabs[:, 2]), (0, 1, 32, row(tabs[:, 3]))),
                    (part(1536, 16, 32), 16, 32, lambda t: gains[:, 0, 0], None),
                    (part(2048, 16, 32), 16, 32, lambda t: gains[:, 1, 0], None)])
                if debug("hn", proj[:, :, 0:1024]): return
                if debug("hn2", proj[:, :, 1536:2560]): return

                def group(col):
                    return lambda i, p, dst: [(dst if len(dst.shape) == 3 else dst[:, 0], proj[:, :, ds(col + (2 * i + p) * P, P)])]
                attention(nc, "diff", m, 2, [(t, 0, XT) for t in range(XT)], 2, P, group(0), group(512), group(1024),
                          lambda i, p: oT[:, ds(2 * i + p, 1), :].rearrange("p a t -> p (a t)"), combine=neg_lam[:])
                sub_norm(nc, "subn", m, oT[:, 0:4], 4)
                if debug("diff", oT[:, 0:4]): return
                attention(nc, "near", m, 2, [(t, max(t - 1, 0), min(t + 2, XT)) for t in range(XT)], 4, NA_D,
                          group(1536), group(2048), group(2560),
                          lambda i, p: oT[:, ds(4 + 2 * i + p, 1), :].rearrange("p a t -> p (a t)"), bias=table)
                if debug("near", oT[:, 4:8]): return
            dense(nc, "mix_out_w", tokens_of(oT), DK, XT, A["w_out"], 2, 512, add_to(hx), both=False)
        if debug("h1", hx[:, 0:XT]): return

        with ExitStack() as c:
            block_expert, n_pairs = sb(c, "block_expert", [P, MAX_BLOCKS], I32), sb(c, "n_pairs", [P, 1], I32)
            with ExitStack() as cc:
                aT = sb(cc, "ffn_in", [P, DK, SEQ])
                norm_transpose(nc, "ffn_norm", m, lambda t: hx[:, ds(t, 1), :].rearrange("p a d -> p (a d)"), DK, XT, m["g_ffn"], None, aT,
                               spill=xn.rearrange("(t p) d -> t p d", p=P))
                route(nc, "route", m, aT, A["w_router"], A["slots_init"], A["slot_ids"], slots, block_expert[0:1, :], n_pairs[0:1, :])
            expert_blocks(nc, "exp", m, block_expert[0:1, :], n_pairs[0:1, :], slots, A["halves"], xn, A["w1"], A["w3"], A["w2"], ys)
        add_experts(nc, "moe_add", ys, hx)
        if debug("h2", hx[:, 0:XT]): return

        with ExitStack() as c:
            side, sg = sb(c, "side", [P, XT, D]), sb(c, "side_gate", [P, XT, D])
            with ExitStack() as cc:
                pT = sb(cc, "side_in", [P, 2, SEQ])
                load(nc, "load_p", [(pT[:], A["p_t"].rearrange("(k p) t -> p k t", p=P))])
                dense(nc, "side_w", tokens_of(pT), 2, XT, A["w_ple"], 2, 512, store_to(nc, side, 512))
                aT = sb(cc, "plg_in", [P, DK, SEQ])
                norm_transpose(nc, "plg_norm", m, lambda t: hx[:, ds(t, 1), :].rearrange("p a d -> p (a d)"), DK, XT, m["g_plg"], None, aT)
                sg_raw = lambda eng, is_act, t, cidx, ps, tmp, chain: copy(nc, eng, is_act, sg[:, t, ds(cidx * 512, 512)], ps)
                dense(nc, "plg_w", tokens_of(aT), DK, XT, A["w_plg"], 2, 512, sg_raw)
            with stage(nc, "sigm", done=None) as (block, s):
                @block.scalar
                def _(act):
                    for t in range(XT):
                        act.activation(sg[:, t], sg[:, t], ACT.Sigmoid).then_inc(s["done"], 1)
            add_side(nc, "side_add", m, A["g_ple"], side, sg[:], hx)
        if debug("h3", hx[:, 0:XT]): return

        with ExitStack() as c:
            gain, shift, gate = sb(c, "l0_gain", [P, AT, DK]), sb(c, "l0_shift", [P, AT, DK]), sb(c, "l0_gate", [P, 2, D])
            modulation(nc, "l0_mod", m, A["l0_w_mod"], m["l0_b"], A["l0_b_gate"], m["l0_norm"], gain, shift, gate, 2)
            gT = sb(c, "l0_gT", [P, DK, AT * P])
            with ExitStack() as cc:
                proj = sb(cc, "l0_proj", [P, AT, 1536])
                with ExitStack() as ca:
                    aT = sb(ca, "l0_in", [P, DK, AT * P])
                    norm_transpose(nc, "l0_n", m, lambda t: hx[:, ds(t, 1), :].rearrange("p a d -> p (a d)"), DK, AT, gain, shift, aT)
                    dense(nc, "l0_w", tokens_of(aT), DK, AT, A["l0_w_in"], 3, 512, store_to(nc, proj, 512))
                    dense_t(nc, "l0_g", aT, DK, AT * P, A["l0_w_in"], 1536, 2,
                            lambda act, n, a, w, ps: act.activation(gT[:, n, a:a + w], ps, ACT.Silu))
                tabs = sb(cc, "l0_tabs", [P, 4, AT, 64])
                s0 = 64 ** -0.5
                scale_tables(nc, "l0_tab", [
                    (tabs[:, 0], tiles(m["ax_cos"], 64), m["gqa_q"], None, s0), (tabs[:, 1], tiles(m["ax_sin"], 64), m["gqa_q"], 2, s0),
                    (tabs[:, 2], tiles(m["ax_cos"], 64), m["gqa_k"], None, 1.0), (tabs[:, 3], tiles(m["ax_sin"], 64), m["gqa_k"], 2, 1.0)])

                def part2(col, n, d):
                    return lambda t: proj[:, ds(t, 1), col:col + n * d].rearrange("p a (h d) -> p (a h) d", d=d)

                def row2(tab):
                    return lambda t: tab[:, ds(t, 1), :].rearrange("p a d -> p (a d)")
                head_norms(nc, "l0_hn", m, AT, [
                    (part2(512, 16, 64), 16, 64, row2(tabs[:, 0]), (0, 2, 16, row2(tabs[:, 1]))),
                    (part2(0, 4, 64), 4, 64, row2(tabs[:, 2]), (0, 2, 16, row2(tabs[:, 3])))])
                attention(nc, "gqa", m, 4, [(t, 0, AT) for t in range(XT)] + [(t, XT, AT) for t in range(XT, AT)], 2, 64,
                          lambda i, p, dst: [(dst[:, 0], proj[:, :, ds(512 + (2 * i + p) * P, P)])],
                          lambda i, p, dst: [(dst[:, 0, :, x * 64:(x + 1) * 64], proj[:, :, ds(i * 64, 64)]) for x in range(2)],
                          lambda i, p, dst: [(dst[:, :, x * 64:(x + 1) * 64], proj[:, :, ds(256 + i * 64, 64)]) for x in range(2)],
                          lambda i, p: gT[:, ds(2 * i + p, 1), :].rearrange("p a t -> p (a t)"), gate=True,
                          stage_k=(True, False), tiles=AT, ktiles=AT)
            dense(nc, "l0_o", tokens_of(gT), DK, AT, A["l0_w_out"], 2, 512, add_gated(hx, gate), both=False, links=1)
        if debug("h4", hx[:, 0:XT]): return

        with ExitStack() as c:
            gain, shift, gate = sb(c, "l1_gain", [P, AT, DK]), sb(c, "l1_shift", [P, AT, DK]), sb(c, "l1_gate", [P, 1, D])
            modulation(nc, "l1_mod", m, A["l1_w_mod"], m["l1_b"], A["l1_b_gate"], m["l1_norm"], gain, shift, gate, 1)
            gT = sb(c, "l1_gT", [P, DK, SEQ])
            with ExitStack() as cc:
                latent, q_low = sb(cc, "l1_latent", [P, AT, 288]), sb(cc, "l1_q_low", [P, XT, 384])
                with ExitStack() as ca:
                    aT = sb(ca, "l1_in", [P, DK, AT * P])
                    norm_transpose(nc, "l1_n", m, lambda t: hx[:, ds(t, 1), :].rearrange("p a d -> p (a d)"), DK, AT, gain, shift, aT)
                    dense(nc, "l1_wk", tokens_of(aT), DK, AT, A["l1_w_in"], 1, 288, store_to(nc, latent, 288))
                    dense(nc, "l1_wq", tokens_of(aT), DK, XT, A["l1_w_in"], 1, 384, store_to(nc, q_low, 384), col0=288)
                    dense_t(nc, "l1_g", aT, DK, SEQ, A["l1_w_in"], 672, 2,
                            lambda act, n, a, w, ps: act.activation(gT[:, n, a:a + w], ps, ACT.Silu))
                kv, q = sb(cc, "l1_kv", [P, AT, 2048]), sb(cc, "l1_q", [P, XT, 1536])
                with ExitStack() as ca:
                    kvT, qaT = sb(ca, "l1_kvT", [P, 2, AT * P]), sb(ca, "l1_qaT", [P, 3, SEQ])
                    norm_transpose(nc, "l1_nkv", m, lambda t: latent[:, ds(t, 1), 0:256].rearrange("p a d -> p (a d)"), 2, AT, m["kv_a_norm"], None, kvT)
                    norm_transpose(nc, "l1_nq", m, lambda t: q_low[:, ds(t, 1), :].rearrange("p a d -> p (a d)"), 3, XT, m["q_a_norm"], None, qaT)
                    dense(nc, "l1_kvb", tokens_of(kvT), 2, AT, A["l1_w_kv_b"], 4, 512, store_to(nc, kv, 512))
                    dense(nc, "l1_qb", tokens_of(qaT), 3, XT, A["l1_w_q_b"], 3, 512, store_to(nc, q, 512))
                tc, tsn, tk = sb(cc, "l1_tc", [P, XT, 96]), sb(cc, "l1_ts", [P, XT, 32]), sb(cc, "l1_tk", [P, 2, AT, 32])
                tkn = sb(cc, "l1_tkn", [P, 1, 64])
                s1 = 96 ** -0.5
                scale_tables(nc, "l1_tab", [
                    (tc[:, :, 0:64], m["ones"][:, 0:64].unsqueeze(1).to_broadcast([P, XT, 64]), m["mla_q"][:, 0:64], None, s1),
                    (tc[:, :, 64:96], tiles(m["mla_cos"], 32)[:, 0:XT], m["mla_q"][:, 64:96], None, s1),
                    (tsn[:], tiles(m["mla_sin"], 32)[:, 0:XT], m["mla_q"][:, 64:96], 2, s1),
                    (tk[:, 0], tiles(m["mla_cos"], 32), m["mla_kr"], None, 1.0), (tk[:, 1], tiles(m["mla_sin"], 32), m["mla_kr"], 2, 1.0),
                    (tkn[:], m["ones"][:, 0:64].unsqueeze(1), m["mla_kn"], None, 1.0)])

                def row3(tab):
                    return lambda t: tab[:, ds(t, 1), :].rearrange("p a d -> p (a d)")
                head_norms(nc, "l1_hq", m, XT, [
                    (lambda t: q[:, ds(t, 1), :].rearrange("p a (h d) -> p (a h) d", d=96), 16, 96, row3(tc), (64, 2, 8, row3(tsn)))])
                head_norms(nc, "l1_hk", m, AT, [
                    (lambda t: kv[:, ds(t, 1), :].rearrange("p a (h d) -> p (a h) d", d=128)[:, :, 0:64], 16, 64, lambda t: tkn[:, 0], None),
                    (lambda t: latent[:, ds(t, 1), 256:288], 1, 32, row3(tk[:, 0]), (0, 2, 8, row3(tk[:, 1])))])
                attention(nc, "mla", m, 4, [(t, 0, AT) for t in range(XT)], 2, 64,
                          lambda i, p, dst: [(dst[:, x], q[:, :, ds((4 * i + 2 * p + x) * 96, 96)]) for x in range(2)],
                          lambda i, p, dst: [e for x in range(2) for e in
                                             ((dst[:, x, :, 0:64], kv[:, :, ds((4 * i + 2 * p + x) * 128, 64)]), (dst[:, x, :, 64:96], latent[:, :, 256:288]))],
                          lambda i, p, dst: [(dst[:, :, x * 64:(x + 1) * 64], kv[:, :, ds((4 * i + 2 * p + x) * 128 + 64, 64)]) for x in range(2)],
                          lambda i, p: gT[:, ds(2 * i + p, 1), :].rearrange("p a t -> p (a t)"), gate=True, split=96,
                          tiles=XT, ktiles=AT)
            dense(nc, "l1_o", tokens_of(gT), DK, XT, A["l1_w_out"], 2, 512, add_gated(hx, gate), both=False, links=1)
        load(nc, "store", [(rows(A["out"]), hx[:, 0:XT])])


def arrays(a):
    order = token_order()
    f = lambda k: np.ascontiguousarray(np.asarray(a[k]))
    prm_at, prm = parameters(a)
    const_at, cst = constants()
    init = slot_table()
    ins = dict(
        params=prm, consts=cst, x=f("x")[0][order], ctx=f("ctx_2")[0], p_t=f("p")[0, 0][order].T,
        rpb=f("rpb")[0], w_in=f("w_in")[0], w_out=f("w_out")[0],
        w_router=np.concatenate([f("w_rg")[0], f("w_re")[0]], 1),
        slots_init=np.concatenate([init, init[:2 * CAP]]), slot_ids=slot_ids(), halves=half_ids(),
        **wide_parameters(a), w1=f("w1")[0], w3=f("w3")[0], w2=f("w2")[0], w_plg=f("w_plg")[0], w_ple=f("w_ple")[0],
        l0_w_mod=f("l0_w_mod_2"), l0_w_in=f("l0_w_in_2"), l0_w_out=f("l0_w_out_2"),
        l1_w_mod=f("l1_w_mod_2"), l1_w_in=f("l1_w_in_2"), l1_w_kv_b=f("l1_w_kv_b_2"), l1_w_q_b=f("l1_w_q_b_2"),
        l1_w_out=f("l1_w_out_2"),
    )
    return {k: np.ascontiguousarray(v) for k, v in ins.items()}, prm_at, const_at


def kernel(**inputs):
    import concourse.bacc as bacc
    from concourse.bass_utils import run_bass_kernel_spmd

    ins, prm_at, const_at = arrays(inputs)
    nc = bacc.Bacc("TRN2", target_bir_lowering=False, num_devices=1)
    A = {k: nc.dram_tensor(f"in_{k}", v.shape, mybir.dt.from_np(v.dtype), kind="ExternalInput").ap() for k, v in ins.items()}
    A["out"] = nc.dram_tensor("out", (SEQ, D), F32, kind="ExternalOutput").ap()
    build(nc, A, prm_at, const_at)
    r = run_bass_kernel_spmd(nc, [{f"in_{k}": v for k, v in ins.items()}], core_ids=[0])
    got = np.asarray(r.results[0]["out"])
    out = np.empty_like(got)
    out[token_order()] = got
    return out.reshape(1, SEQ, D)
```

```python
import math
from contextlib import ExitStack, contextmanager

import numpy as np
import concourse.bass as bass
import concourse.mybir as mybir
from concourse.alu_op_type import AluOpType as ALU

F32 = mybir.dt.float32
I32 = mybir.dt.int32
ACT = mybir.ActivationFunctionType
AX = mybir.AxisListType
ds = bass.ds

P = 128
D = 1024
DK = D // P
GRID_W, ROWS, CB = 64, 8, 16
SEQ, CTX = 512, 256
XT, CT = SEQ // P, CTX // P
AT = XT + CT
EPS = 1e-6
NEG = -1e30
LAM_INIT = 0.8 - 0.6 * math.exp(0.0)
THETA = 10000.0
N_GROUPS, PER_GROUP, D_EXPERT = 4, 8, 512
N_EXPERTS = N_GROUPS * PER_GROUP
CAP = 64
MAX_BLOCKS = 2 * SEQ // CAP + N_EXPERTS
NA_HEADS, NA_D, WIN_R, WIN_C = 16, 32, 8, 16


def token_order():
    return np.arange(SEQ).reshape(ROWS, SEQ // ROWS // CB, CB).transpose(1, 0, 2).reshape(-1)


def per_tile(table):
    n = table.shape[0] // P
    return table.reshape(n, P, -1).transpose(1, 0, 2).reshape(P, -1)


def rope_tables():
    pos = token_order().astype(np.float32)
    f = np.float32
    inv = f(THETA) ** (-np.arange(0, 64, 2, dtype=np.float32) / f(64))
    ang = pos[:, None] * inv[None, :]
    full_c = np.concatenate([np.cos(ang)] * 2, 1)
    full_s = np.concatenate([-np.sin(ang), np.sin(ang)], 1)

    def axial(rot):
        row, col = np.floor(pos / GRID_W).astype(f), (pos % GRID_W).astype(f)
        inv = f(THETA) ** (-np.arange(0, rot // 2, 2, dtype=np.float32) / f(rot // 2))
        ar, ac = row[:, None] * inv, col[:, None] * inv
        c = np.concatenate([np.cos(ar)] * 2 + [np.cos(ac)] * 2, 1)
        s = np.concatenate([-np.sin(ar), np.sin(ar), -np.sin(ac), np.sin(ac)], 1)
        c = np.concatenate([c, np.ones((CTX, rot), f)], 0)
        s = np.concatenate([s, np.zeros((CTX, rot), f)], 0)
        return c.astype(f), s.astype(f)

    return full_c.astype(f), full_s.astype(f), axial(64), axial(32)


def window_masks():
    m = np.zeros((P, 3, 3, CB), np.float32)
    for kind, g in enumerate((0, 1, 3)):
        for q in range(P):
            c = CB * g + q % CB
            start = min(max(c - WIN_C // 2, 0), GRID_W - WIN_C)
            for d in range(3):
                for k in range(CB):
                    kc = CB * (g + d - 1) + k
                    if not start <= kc < start + WIN_C:
                        m[q, kind, d, k] = NEG
    return m


def constants():
    fc, fs, (ac, as_), (mc, ms) = rope_tables()
    select = np.zeros((P, 4, P), np.float32)
    for j in range(2):
        for cond in range(2):
            select[32 * j + cond, 2 * j + cond, :] = 1.0
    fields = dict(
        ident=np.eye(P, dtype=np.float32),
        ones=np.ones((P, P), np.float32),
        before=np.triu(np.ones((P, P), np.float32), 1),
        eps=np.full((P, 1), EPS, np.float32),
        full_cos=per_tile(fc), full_sin=per_tile(fs),
        ax_cos=per_tile(ac), ax_sin=per_tile(as_),
        mla_cos=per_tile(mc), mla_sin=per_tile(ms),
        masks=window_masks().reshape(P, -1),
        select=select.reshape(P, -1),
        prio4=np.tile(np.arange(N_GROUPS, 0, -1, dtype=np.float32), (P, 1)),
        prio8=np.tile(np.arange(PER_GROUP, 0, -1, dtype=np.float32), (P, 1)),
        block_no=np.tile(np.arange(MAX_BLOCKS, dtype=np.float32), (P, 1)),
    )
    return pack(fields)


def slot_table():
    t = np.zeros((MAX_BLOCKS, CAP, 4), np.int32)
    t[:, :, 1] = 2 * (2 * SEQ + np.arange(CAP))
    return t.reshape(-1, 4)


def slot_ids():
    tok = np.arange(XT)[None, :] * P + np.arange(P)[:, None]
    out = np.zeros((P, 2, XT, 2), np.int32)
    for s in range(2):
        out[:, s, :, 0] = 2 * tok
        out[:, s, :, 1] = 2 * (s * SEQ + tok)
    return out.reshape(P, -1)


def half_ids():
    h = np.zeros((P, 2), np.int32)
    h[P // 2:] = 1
    return h


def pack(fields):
    at, n = {}, 0
    for k, v in fields.items():
        at[k] = (n, v.shape[1])
        n += v.shape[1]
    return at, np.concatenate(list(fields.values()), 1)


def columns(v):
    return np.asarray(v).reshape(-1, P).T


def spread(v):
    v = np.asarray(v).reshape(1, -1)
    return np.broadcast_to(v, (P, v.shape[1]))


def parameters(a):
    return pack(dict(
        g_mix=columns(a["g_mix"]), g_ffn=columns(a["g_ffn"]), g_plg=columns(a["g_plg"]),
        l0_norm=columns(a["l0_norm_2"]), l1_norm=columns(a["l1_norm_2"]),
        kv_a_norm=columns(a["l1_kv_a_norm_2"]), q_a_norm=columns(a["l1_q_a_norm_2"]),
        g_sub=columns(a["g_sub"]),
        cond=np.stack([columns(a["c_2"]), columns(a["c_ctx_2"])], 2).reshape(P, -1),
        l0_b=columns(a["l0_b_mod_2"]), l1_b=columns(a["l1_b_mod_2"]),
        g_qa=spread(a["g_qa"]), g_ka=spread(a["g_ka"]),
        g_qb=spread(a["g_qb"]), g_kb=spread(a["g_kb"]),
        lam=spread(np.concatenate([np.asarray(a[n]).reshape(-1) for n in ("lam_q1", "lam_k1", "lam_q2", "lam_k2")])),
        gqa_q=spread(a["l0_q_norm_2"]), gqa_k=spread(a["l0_k_norm_2"]),
        mla_q=spread(a["l1_q_norm_2"]), mla_kn=spread(a["l1_k_nope_norm_2"]), mla_kr=spread(a["l1_k_rope_norm_2"]),
    ))


def wide_parameters(a):
    return dict(l0_b_gate=spread(np.asarray(a["l0_b_mod_2"])[2 * D:]), l1_b_gate=spread(np.asarray(a["l1_b_mod_2"])[2 * D:]),
                g_ple=spread(a["g_ple"]))


@contextmanager
def semaphores(nc, name, start=0, software_dma=(), **sems):
    made = {k: [nc.alloc_semaphore(f"{name}_{k}{'' if n is None else i}") for i in range(n or 1)]
            for k, n in sems.items()}
    if start:
        for k, got in made.items():
            for x in got:
                if k not in software_dma:
                    nc.gpsimd.sem_inc(x, start)
    yield {k: got if sems[k] else got[0] for k, got in made.items()}
    nc.clear_and_free_semaphores([x for got in made.values() for x in got])
    nc.all_engine_barrier(sem_only=True)


@contextmanager
def stage(nc, name, **sems):
    with semaphores(nc, name, **sems) as s:
        with nc.Block() as block:
            yield block, s


class Chain:

    def __init__(self, eng, sem, base=0):
        self.eng, self.sem, self.base, self.n = eng, sem, base, 0

    def __call__(self, ins):
        self.n += 1
        ins.then_inc(self.sem, 1)
        self.eng.wait_ge(self.sem, self.base + self.n)


def loop(eng, n, body):
    if n == 1:
        body(0)
    elif n > 1:
        with eng.Fori(0, n) as i:
            body(i)


def inverse_root(dve, chain, ss, root, n, v, out):
    chain(dve.tensor_scalar(v, ss, 0.5 / n, 0.5 * EPS, ALU.mult, ALU.add))
    chain(dve.reciprocal(out, root))
    chain(dve.tensor_tensor(v, v, out, ALU.mult))
    chain(dve.scalar_tensor_tensor(out=v, in0=root, scalar=0.5, in1=v, op0=ALU.mult, op1=ALU.add))
    return dve.reciprocal(out, v)


def copy(nc, eng, act, out, in_):
    return eng.activation(out, in_, ACT.Copy) if act else eng.tensor_copy(out, in_)


def norm_transpose(nc, name, m, src, K, T, gain, shift, out, spill=None):
    W = K * P

    def of_tile(v, t):
        v = v if len(v.shape) == 2 else v[:, ds(t, 1), :].rearrange("p a k -> p (a k)")
        return v.unsqueeze(2).to_broadcast([P, K, P])

    with ExitStack() as c:
        sb = lambda n, s: c.enter_context(nc.sbuf_tensor(f"{name}_{n}", s, F32))
        squares, xn = sb("squares", [P, W]), sb("xn", [P, 2, W])
        ss, sd, rs = sb("ss", [P, 2]), sb("sd", [P, 2]), sb("rs", [P, 2])
        half = sb("half", [P, 2])
        ps = c.enter_context(nc.psum_tensor(f"{name}_ps", [P, 2, 1024], F32))
        with stage(nc, name, start=1, act_chain=None, dve_chain=None, sd_done=2, rs_done=2, xn_done=2,
                   turned=2, out_done=2, spilled=2) as (block, s):

            @block.scalar
            def _(act):
                def body(i):
                    chain = Chain(act, s["act_chain"], 1 + 2 * i)
                    for p in range(2):
                        act.wait_ge(s["rs_done"][p], 1 + i)
                        chain(act.activation(squares[:], src(2 * i + p),
                                             ACT.Square, accum_out=ss[:, p:p + 1]))
                        act.activation(sd[:, p:p + 1], ss[:, p:p + 1], ACT.Sqrt, bias=m["eps"],
                                       scale=1.0 / W).then_inc(s["sd_done"][p], 1)
                        act.wait_ge(s["sd_done"][p], 1 + i + 1)
                loop(act, T // 2, body)

            @block.vector
            def _(dve):
                def body(i):
                    chain = Chain(dve, s["dve_chain"], 1 + (8 if shift is None else 10) * i)
                    for p in range(2):
                        dve.wait_ge(s["sd_done"][p], 1 + i + 1)
                        dve.wait_ge(s["xn_done"][p], 1 + i)
                        inverse_root(dve, chain, ss[:, p:p + 1], sd[:, p:p + 1], W, half[:, p:p + 1],
                                     rs[:, p:p + 1]).then_inc(s["rs_done"][p], 1)
                        dve.wait_ge(s["rs_done"][p], 1 + i + 1)
                        dve.wait_ge(s["turned"][p], 1 + i)
                        if spill is not None:
                            dve.wait_ge(s["spilled"][p], 1 + 16 * i)
                        dve.tensor_scalar(xn[:, p, :], src(2 * i + p),
                                          rs[:, p:p + 1], None, ALU.mult).then_inc(s["xn_done"][p], 1)
                    for p in range(2):
                        t = 2 * i + p
                        dve.wait_ge(s["turned"][p], 1 + i + 1)
                        o = out[:, :, ds(t * P, P)]
                        v = ps[:, p, 0:W].rearrange("p (k t) -> p k t", k=K)
                        if shift is None:
                            dve.tensor_tensor(o, v, of_tile(gain, t), ALU.mult).then_inc(s["out_done"][p], 1)
                        else:
                            chain(dve.tensor_tensor(o, v, of_tile(gain, t), ALU.mult))
                            dve.tensor_tensor(o, o, of_tile(shift, t), ALU.add).then_inc(s["out_done"][p], 1)
                loop(dve, T // 2, body)

            @block.tensor
            def _(pe):
                def body(i):
                    for p in range(2):
                        pe.wait_ge(s["xn_done"][p], 1 + i + 1)
                        pe.wait_ge(s["out_done"][p], 1 + i)
                        for k in range(K):
                            last = pe.transpose(ps[:, p, k * P:(k + 1) * P], xn[:, p, k * P:(k + 1) * P], m["ident"])
                        last.then_inc(s["turned"][p], 1)
                loop(pe, T // 2, body)

            if spill is not None:
                @block.sync
                def _(sp):
                    def body(i):
                        for p in range(2):
                            sp.wait_ge(s["xn_done"][p], 1 + i + 1)
                            sp.dma_start(spill[ds(2 * i + p, 1)].rearrange("a p d -> p (a d)"), xn[:, p, :]).then_inc(s["spilled"][p], 16)
                    loop(sp, T // 2, body)
                    for p in range(2):
                        sp.wait_ge(s["spilled"][p], 1 + 16 * (T // 2))


def dense(nc, name, lhs, KT, T, w, n_chunks, width, emit, both=True, col0=0, links=0):
    pairs, NB, H = n_chunks // 2, 4, T // 2
    with ExitStack() as c:
        wb = c.enter_context(nc.sbuf_tensor(f"{name}_w", [P, 2, KT, width], F32))
        tmp = c.enter_context(nc.sbuf_tensor(f"{name}_tmp", [P, 2, width], F32))
        ps = c.enter_context(nc.psum_tensor(f"{name}_ps", [P, NB, 512], F32))
        with stage(nc, name, start=1, loaded=2, mm=NB, ev=NB, dve_chain=None, act_chain=None) as (block, s):
            src = w.rearrange("(k p) n -> p k n", p=P)

            def after(cp):
                u = cp * T + T - 1
                return u % NB, u // NB + 1

            @block.sync
            def _(sp):
                def load(i, cp):
                    sp.dma_start(wb[:, cp], src[:, :, ds(col0 + (2 * i + cp) * width, width)]).then_inc(s["loaded"][cp], 16)

                load(0, 0)
                if n_chunks > 1:
                    load(0, 1)

                def refill(i, cps):
                    for cp in cps:
                        b, n = after(cp)
                        sp.wait_ge(s["mm"][b], 1 + i * H + n)
                        load(i + 1, cp)
                loop(sp, pairs - 1, lambda i: refill(i, (0, 1)))
                if n_chunks % 2 and pairs:
                    refill(pairs - 1, (0,))

            def over_chunks(eng, body):
                loop(eng, pairs, lambda i: body(i, (0, 1)))
                if n_chunks % 2:
                    body(pairs, (0,))

            @block.tensor
            def _(pe):
                def body(i, cps):
                    for cp in cps:
                        pe.wait_ge(s["loaded"][cp], 1 + 16 * (i + 1))
                        for t in range(T):
                            u = cp * T + t
                            pe.wait_ge(s["ev"][u % NB], 1 + i * H + u // NB)
                            for k in range(KT):
                                last = pe.matmul(ps[:, u % NB, 0:width], lhs(k, t), wb[:, cp, k, :],
                                                 start=(k == 0), stop=(k == KT - 1))
                            last.then_inc(s["mm"][u % NB], 1)
                over_chunks(pe, body)

            def emptying(eng, is_act, sem):
                units = [u for u in range(2 * T) if not both or u % 2 == is_act]

                def body(i, cps):
                    chain = Chain(eng, sem, 1 + i * (len(units) * links))
                    for u in units:
                        if u // T not in cps:
                            continue
                        b = u % NB
                        eng.wait_ge(s["mm"][b], 1 + i * H + u // NB + 1)
                        emit(eng, is_act, u % T, 2 * i + u // T, ps[:, b, 0:width], tmp[:, is_act], chain).then_inc(s["ev"][b], 1)
                        if links:
                            eng.wait_ge(s["ev"][b], 1 + i * H + u // NB + 1)
                return body

            @block.vector
            def _(dve):
                over_chunks(dve, emptying(dve, 0, s["dve_chain"]))

            if both:
                @block.scalar
                def _(act):
                    over_chunks(act, emptying(act, 1, s["act_chain"]))


@contextmanager
def transposed_products(nc, name, act_t, KT, tokens, w, col0, n_chunks, out):
    pieces = [(a, min(512, tokens - a)) for a in range(0, tokens, 512)]
    NB, CW = 4, 512
    buffers = min(2, n_chunks)
    with ExitStack() as c:
        wb = c.enter_context(nc.sbuf_tensor(f"{name}_w", [P, buffers, KT, CW], F32))
        ps = c.enter_context(nc.psum_tensor(f"{name}_ps", [P, NB, 512], F32))
        s = c.enter_context(semaphores(nc, name, loaded=2, mm=NB, ev=NB))
        src = w.rearrange("(k p) n -> p k n", p=P)
        units = [(cc, j, a, n) for cc in range(n_chunks) for j in range(CW // P) for a, n in pieces]
        per_chunk = len(units) // n_chunks

        def sync(sp):
            for cc in range(n_chunks):
                if cc >= 2:
                    u = (cc - 1) * per_chunk - 1
                    sp.wait_ge(s["mm"][u % NB], u // NB + 1)
                sp.dma_start(wb[:, cc % 2], src[:, :, col0 + cc * CW:col0 + (cc + 1) * CW]).then_inc(s["loaded"][cc % 2], 16)

        def tensor(pe):
            for u, (cc, j, a, n) in enumerate(units):
                if u % per_chunk == 0:
                    pe.wait_ge(s["loaded"][cc % 2], 16 * (cc // 2 + 1))
                if u >= NB:
                    pe.wait_ge(s["ev"][u % NB], u // NB)
                for k in range(KT):
                    last = pe.matmul(ps[:, u % NB, 0:n], wb[:, cc % 2, k, j * P:(j + 1) * P], act_t[:, k, a:a + n],
                                     start=(k == 0), stop=(k == KT - 1))
                last.then_inc(s["mm"][u % NB], 1)

        def scalar(act, part, parts):
            for u in range(len(units) * part // parts, len(units) * (part + 1) // parts):
                cc, j, a, n = units[u]
                act.wait_ge(s["mm"][u % NB], u // NB + 1)
                act.activation(out(cc * (CW // P) + j, a, n), ps[:, u % NB, 0:n], ACT.Silu).then_inc(s["ev"][u % NB], 1)

        yield dict(sync=sync, tensor=tensor, scalar=scalar, vector=lambda dve: None)


def head_norms(nc, name, m, T, jobs, beside=None):
    J = len(jobs)
    with ExitStack() as c:
        sb = lambda n, s: c.enter_context(nc.sbuf_tensor(f"{name}_{n}", s, F32))
        sq = [sb(f"sq{j}", [P, H, d]) for j, (_, H, d, _, _) in enumerate(jobs)]
        tw = [sb(f"tw{j}", [P, H, max(1, 2 * r[1] * r[2])]) if r else None for j, (_, H, d, _, r) in enumerate(jobs)]
        st = [sb(f"st{j}", [P, 4, H]) for j, (_, H, _, _, _) in enumerate(jobs)]
        with stage(nc, name, start=1, squared=None, summed=None, rooted=None, scaled=None, turned=None, done=None, dve_chain=None) as (block, s):

            @block.scalar
            def _(act):
                def body(t):
                    for j, (x, H, d, _, _) in enumerate(jobs):
                        act.wait_ge(s["summed"], 1 + t * J + j)
                        act.activation(sq[j][:], x(t), ACT.Square).then_inc(s["squared"], 1)
                    for j, (x, H, d, _, _) in enumerate(jobs):
                        act.wait_ge(s["summed"], 1 + t * J + j + 1)
                        act.wait_ge(s["scaled"], 1 + t * J)
                        act.activation(st[j][:, 1, :], st[j][:, 0, :], ACT.Sqrt, bias=m["eps"], scale=1.0 / d).then_inc(s["rooted"], 1)
                if beside is None:
                    loop(act, T, body)
                else:
                    for t in range(T):
                        body(t)
                        beside["scalar"](act, t, T)

            @block.vector
            def _(dve):
                def body(t):
                    chain = Chain(dve, s["dve_chain"], 1 + t * (5 * J + sum(1 for q in jobs if q[4])))
                    for j in range(J):
                        dve.wait_ge(s["squared"], 1 + t * J + j + 1)
                        dve.wait_ge(s["rooted"], 1 + t * J)
                        dve.tensor_reduce(st[j][:, 0, :], sq[j][:], AX.X, ALU.add).then_inc(s["summed"], 1)
                    for j, (x, H, d, cos, rot) in enumerate(jobs):
                        dve.wait_ge(s["rooted"], 1 + t * J + j + 1)
                        chain(inverse_root(dve, chain, st[j][:, 0, :], st[j][:, 1, :], d, st[j][:, 3, :], st[j][:, 2, :]))
                        dve.tensor_tensor(x(t), x(t), st[j][:, 2, :].unsqueeze(2).to_broadcast([P, H, d]), ALU.mult).then_inc(s["scaled"], 1)
                    turns = 0
                    for j, (x, H, d, cos, rot) in enumerate(jobs):
                        dve.wait_ge(s["scaled"], 1 + t * J + j + 1)
                        if rot:
                            turns += 1
                            dve.wait_ge(s["turned"], 1 + t * sum(1 for q in jobs if q[4]) + turns)
                        cc = cos(t).unsqueeze(1).to_broadcast([P, H, d])
                        if rot:
                            f0, G, w, sin = rot
                            chain(dve.tensor_tensor(x(t), x(t), cc, ALU.mult))
                            xr = x(t)[:, :, f0:f0 + 2 * G * w]
                            dve.tensor_tensor(xr, xr, tw[j][:], ALU.add).then_inc(s["done"], 1)
                        else:
                            dve.tensor_tensor(x(t), x(t), cc, ALU.mult).then_inc(s["done"], 1)
                loop(dve, T, body)
                if beside is not None:
                    beside["vector"](dve)

            @block.gpsimd
            def _(pool):
                def body(t):
                    for j, (x, H, d, cos, rot) in enumerate(jobs):
                        if not rot:
                            continue
                        f0, G, w, sin = rot
                        pool.wait_ge(s["scaled"], 1 + t * J + j + 1)
                        pool.wait_ge(s["done"], 1 + t * J)
                        sw = sin(t).rearrange("p (g a w) -> p g a w", g=G, a=2)
                        for g in range(G):
                            for a in range(2):
                                last = pool.tensor_tensor(
                                    tw[j][:, :, (2 * g + a) * w:(2 * g + a + 1) * w],
                                    x(t)[:, :, f0 + (2 * g + 1 - a) * w:f0 + (2 * g + 2 - a) * w],
                                    sw[:, g, a, :].unsqueeze(1).to_broadcast([P, H, w]), ALU.mult)
                        last.then_inc(s["turned"], 1)
                loop(pool, T, body)

            if beside is not None:
                @block.sync
                def _(sp):
                    beside["sync"](sp)

                @block.tensor
                def _(pe):
                    beside["tensor"](pe)


def attention(nc, name, m, pairs, U, nh, dv, q_src, k_src, v_src, out, gate=None, split=False,
              combine=None, bias=None, spare=None, tiles=XT, ktiles=XT):
    FIRST = 2
    NU = len(U)
    LEAD = 2 * nh - 1 if nh == 2 else 2 * nh - 2
    TURN_AT = NU - 3
    R = split or P
    NS = nh if split else 1
    KT = ktiles
    heads = 1 if combine is not None else nh
    W = 1024 if KT > 4 else 512
    pieces = []
    for _, lo, hi in U:
        n = hi - lo
        pieces.append([list(range(lo, hi))] if n <= 3 and bias is not None else
                      [list(range(lo, lo + (n + 1) // 2)), list(range(lo + (n + 1) // 2, hi))])
    stage_pieces = [(z, x, lo, min(4, n - lo)) for x in range(NS) for z, n in ((0, tiles), (1, KT)) for lo in range(0, n, 4)]

    def bank_uses(last):
        uses = []
        for p in range(2):
            for u in range(NU):
                uses += [("weights", p, u, x, n) for x in range(heads) for n in range(len(pieces[u]))]
                if u == TURN_AT and not (last and p):
                    uses += [("turn", p, k) for k in range(len(stage_pieces))]
        return {x: (n % 2, n // 2) for n, x in enumerate(uses)}
    bank_use = [bank_uses(False), bank_uses(True)]
    per_bank = len(bank_use[0]) // 2
    BASE = FIRST + len(stage_pieces) // 2
    assert len(bank_use[0]) % 2 == 0 and len(stage_pieces) % 2 == 0
    ob = (tiles + 3) // 4
    with ExitStack() as c:
        sb = lambda n, s: c.enter_context(nc.sbuf_tensor(f"{name}_{n}", s, F32))
        qs, ks, vs = sb("qs", [P, 2, NS, tiles, R]), sb("ks", [P, 2, NS, KT, R]), sb("vs", [P, 2, KT, nh * dv if combine is None else dv])
        qT, kT = sb("qT", [P, 2, NS, tiles * P]), sb("kT", [P, 2, nh, KT * P])
        kw = min(KT * P, W) if bias is None else 3 * P
        pr = sb("pr", [P, 2, nh, kw])
        pT = sb("pT", [P, 2, heads, KT, P])
        nm, sm, rc = sb("nm", [P, 2, nh]), sb("sm", [P, 2, nh]), sb("rc", [P, 2, nh])
        S = c.enter_context(nc.psum_tensor(f"{name}_S", [P, 4, 512], F32))
        Tp = c.enter_context(nc.psum_tensor(f"{name}_T", [P, 2, 512], F32))
        O = c.enter_context(nc.psum_tensor(f"{name}_O", [P, 2, 512], F32))
        if bias is not None:
            E = [spare(p).rearrange("p (h a b) -> p h a b", h=nh, b=3 * CB) for p in range(2)]
            EM = sb("EM", [P, 2, nh, 7, WIN_R * CB])
            em_block = {(0, 1): 0, (0, 2): 1, (1, 0): 2, (1, 1): 3, (1, 2): 4, (2, 0): 5, (2, 1): 6}
        flat = S[:].rearrange("p b n -> p (b n)")

        def scores_of(i, lo, n):
            at = i * W + (lo * P if bias is None else 0)
            return flat[:, at:at + n * P]

        with stage(nc, name, start=FIRST, staged=2, vstaged=2, zeroed=None, scored=4, maxed=4, exped=4, inverted=4,
                   weighted=4, turned=2, emptied=2, pv=2, o_done=None, dve_chain=None, e_in=2, em_done=2,
                   reload=None, lowered=4) as (block, s):

            def count(i, p, u):
                return FIRST + i * (2 * NU) + p * NU + u

            def of_bank(i, last, use):
                bank, n = bank_use[last][use]
                return bank, BASE + i * per_bank + n

            def weights_turned(i, last, p, u, x, bank):
                n = p * NU + u - 2
                table, back = (bank_use[last], 0) if n >= 0 else (bank_use[0], per_bank)
                n %= 2 * NU
                got = [0] + [k + 1 for key, (bk, k) in table.items() if bk == bank and key[0] == "weights" and
                       (key[1] * NU + key[2], 0 if heads < nh else key[3]) <= (n, x)]
                return BASE + i * per_bank - back + max(got)

            def group_turned(i, p, bank):
                got = max(k + 1 for key, (bk, k) in bank_use[0].items() if bk == bank and key[:2] == ("turn", 1 - p))
                return BASE + i * per_bank - (0 if p else per_bank) + got

            def par(p, u):
                n = p * NU + u
                return n % 2, n // 2

            def values_done(i, p, b):
                return FIRST + i * NU + sum(1 for y in range((p + 1) * NU) if y % 2 == b)

            def item_behind(i, last, p, u, x, k):
                n = (p * NU + u) * nh + x + k
                if n < 2 * NU * nh:
                    return i, last, n // (NU * nh), n // nh % NU, n % nh
                n -= 2 * NU * nh
                return None if last else (i + 1, False, 0, n // nh, n % nh)

            def iterations(eng, body):
                loop(eng, pairs - 1, lambda i: body(i, False))
                body(pairs - 1, True)

            @block.gpsimd
            def _(pool):
                if not split:
                    for p in range(2):
                        pool.memset(kT[:, p], 0.0).then_inc(s["zeroed"], 1)

                def bias_blocks(i, p, some, last):
                    pool.wait_ge(s["e_in"][p], FIRST + 16 * ROWS * (i + 1))
                    pool.sem_inc(s["reload"], 1)
                    for x in range(nh if p or type(i) is not int or i else 0):
                        pool.wait_ge(s["maxed"][x], count(i, p, 0) - NU)
                        pool.sem_inc(s["reload"], 1)
                    for kind, d in some:
                        mk = m["masks"].rearrange("p (z d k) -> p z d k", z=3, d=3)[:, kind, d, :]
                        for x in range(nh):
                            ins = pool.tensor_tensor(
                                EM[:, p, x, em_block[kind, d]].rearrange("p (r k) -> p r k", r=WIN_R), E[p][:, x, :, d * CB:(d + 1) * CB],
                                mk.unsqueeze(1).to_broadcast([P, WIN_R, CB]), ALU.add)
                    if last:
                        ins.then_inc(s["em_done"][p], 1)
                blocks = list(em_block) if bias is not None else []
                parts = [blocks[0:3], blocks[3:5], blocks[5:7]]
                if bias is not None:
                    bias_blocks(0, 0, blocks, True)

                def body(i, last):
                    for p in range(2):
                        for u, (t, lo, hi) in enumerate(U):
                            b, before = par(p, u)
                            for x in range(nh):
                                pool.wait_ge(s["inverted"][x], count(i, p, u) + 1)
                                if combine is not None and x == 0:
                                    continue
                                w = pr[:, b, x, 0:(hi - lo) * P]
                                pool.tensor_tensor(w, w, rc[:, b, x:x + 1].to_broadcast([P, (hi - lo) * P]), ALU.mult).then_inc(s["weighted"][x], 1)
                            if bias is not None and u < 3 and not (last and p):
                                bias_blocks(i + p, 1 - p, parts[u], u == 2)
                iterations(pool, body)

            @block.sync
            def _(sp):
                def load_qk(i, p):
                    for dst, src in q_src(i, p, qs[:, p]) + k_src(i, p, ks[:, p]):
                        sp.dma_start(dst, src).then_inc(s["staged"][p], 16)

                def load_v(i, p):
                    for dst, src in v_src(i, p, vs[:, p]):
                        sp.dma_start(dst, src).then_inc(s["vstaged"][p], 16)
                    if bias is not None:
                        for r in range(ROWS):
                            sp.dma_start(E[p][r * CB:(r + 1) * CB].rearrange("q h a b -> q h (a b)"),
                                         bias[:, ds((2 * i + p) * nh, nh), (7 - r) * 48:(15 - r) * 48]).then_inc(s["e_in"][p], 16)

                def wait(sem, n):
                    sp.wait_ge(sem, n)
                    sp.sem_inc(s["reload"], 1)

                def refill(i, last):
                    for p in range(2):
                        if p == 0:
                            for b in range(2):
                                wait(s["turned"][b], group_turned(i, 1, b))
                            load_qk(i + 1, 1)
                        elif not last:
                            for b in range(2):
                                wait(s["turned"][b], group_turned(i + 1, 0, b))
                            load_qk(i + 2, 0)
                        for b in range(2):
                            wait(s["pv"][b], values_done(i, p, b))
                        if bias is not None:
                            wait(s["em_done"][p], FIRST + i + 1)
                        load_v(i + 1, p)
                for p in range(2):
                    load_qk(0, p)
                    load_v(0, p)
                for b in range(2):
                    sp.wait_ge(s["turned"][b], BASE)
                load_qk(1, 0)
                loop(sp, pairs - 2, lambda i: refill(i, False))
                refill(pairs - 2, True)

            n_staged = [len(q_src(0, p, qs[:, p])) + len(k_src(0, p, ks[:, p])) for p in range(2)]
            n_v = [len(v_src(0, p, vs[:, p])) for p in range(2)]

            @block.tensor
            def _(pe):
                def scores(i, last, p, u, x, first=False):
                    t, lo, hi = U[u]
                    if u == 0 and x == 0:
                        for b in range(2):
                            pe.wait_ge(s["emptied"][b], BASE if first else group_turned(i, p, b))
                    pe.wait_ge(s["exped"][x] if bias is None else s["maxed"][x], count(i, p, u))
                    qq = x if split else 0
                    cuts = [(a, min(hi, a + 4 - a % 4)) for a in ([lo] + [4] * (lo < 4 < hi))] if bias is None else [(lo, hi)]
                    for a, e in cuts:
                        at = x * W + (a * P if bias is None else 0)
                        ins = pe.matmul(flat[:, at:at + (e - a) * P], qT[0:R, p, qq, t * P:(t + 1) * P],
                                        kT[0:R, p, x, a * P:e * P], start=True, stop=True)
                    ins.then_inc(s["scored"][x], 1)

                def turn(i, last, p, u, x):
                    t, lo, hi = U[u]
                    b, before = par(p, u)
                    pe.wait_ge(s["weighted"][x], count(i, p, u) + 1)
                    for n, kts in enumerate(pieces[u]):
                        bank, n_before = of_bank(i, last, ("weights", p, u, x, n))
                        pe.wait_ge(s["emptied"][bank], n_before)
                        for z, kt in enumerate(kts):
                            ins = pe.transpose(Tp[:, bank, z * P:(z + 1) * P], pr[:, b, x, (kt - lo) * P:(kt - lo + 1) * P], m["ident"])
                        ins.then_inc(s["turned"][bank], 1)

                def turn_group(i, p, place):
                    pe.wait_ge(s["staged"][p], FIRST + 16 * n_staged[p] * (i + 1))
                    for k, (z, x, lo, n) in enumerate(stage_pieces):
                        bank, n_before = place(k)
                        pe.wait_ge(s["emptied"][bank], n_before)
                        for t in range(n):
                            ins = pe.transpose(Tp[0:R, bank, t * P:(t + 1) * P], (ks if z else qs)[:, p, x, lo + t, :], m["ident"])
                        ins.then_inc(s["turned"][bank], 1)

                def values(i, last, p, u):
                    t, lo, hi = U[u]
                    b, before = par(p, u)
                    for bank in range(2):
                        mine = [use for x in range(heads) for n in range(len(pieces[u]))
                                for bk, use in [of_bank(i, last, ("weights", p, u, x, n))] if bk == bank]
                        if mine:
                            pe.wait_ge(s["emptied"][bank], mine[-1] + 1)
                    if u == 0:
                        pe.wait_ge(s["vstaged"][p], FIRST + 16 * n_v[p] * (i + 1))
                        pe.wait_ge(s["o_done"], FIRST + 2 * i + p - (1 if ob == 1 else 0))
                    for kt in range(lo, hi):
                        for x in range(heads):
                            v = vs[:, p, kt, x * dv:(x + 1) * dv]
                            ins = pe.matmul(O[x * dv:(x + 1) * dv, p if ob == 1 else t // 4, (t % 4) * P:(t % 4 + 1) * P], v, pT[:, b, x, kt, :],
                                            start=(kt == lo), stop=(kt == hi - 1))
                    ins.then_inc(s["pv"][b], 1)

                turn_group(0, 0, lambda k: (k % 2, FIRST + k // 2))
                for k in range(LEAD):
                    scores(0, False, 0, k // nh, k % nh, first=True)

                def body(i, last):
                    for p in range(2):
                        for u in range(NU):
                            for x in range(nh):
                                if heads == nh:
                                    turn(i, last, p, u, x)
                                ahead = item_behind(i, last, p, u, x, LEAD)
                                if ahead:
                                    scores(*ahead)
                                if heads < nh and x == 0:
                                    turn(i, last, p, u, 0)
                            if u == TURN_AT and not (last and p):
                                turn_group(i + p, 1 - p, lambda k: of_bank(i, last, ("turn", p, k)))
                            values(i, last, p, u)
                iterations(pe, body)

            def empty_weights(eng, act, i, last, p, u, x):
                b, before = par(p, u)
                for n, kts in enumerate(pieces[u]):
                    bank, n_before = of_bank(i, last, ("weights", p, u, x, n))
                    if bank != act:
                        continue
                    eng.wait_ge(s["turned"][bank], n_before + 1)
                    eng.wait_ge(s["pv"][b], FIRST + i * NU + before)
                    copy(nc, eng, act, pT[:, b, x, kts[0]:kts[-1] + 1, :],
                         Tp[:, bank, 0:len(kts) * P].rearrange("p (k q) -> p k q", q=P)).then_inc(s["emptied"][bank], 1)

            def empty_group(eng, act, p, place):
                for k, (z, x, lo, n) in enumerate(stage_pieces):
                    bank, n_before = place(k)
                    if bank != act:
                        continue
                    eng.wait_ge(s["turned"][bank], n_before + 1)
                    if z and not split:
                        for h in range(nh):
                            rows = slice(h * (P // nh), (h + 1) * (P // nh))
                            ins = copy(nc, eng, act, kT[rows, p, h, lo * P:(lo + n) * P], Tp[rows, bank, 0:n * P])
                    else:
                        ins = copy(nc, eng, act, (kT if z else qT)[0:R, p, x, lo * P:(lo + n) * P], Tp[0:R, bank, 0:n * P])
                    ins.then_inc(s["emptied"][bank], 1)

            def highest(dve, i, last, p, u, x, first=False):
                t, lo, hi = U[u]
                b, before = par(p, u)
                n = hi - lo
                dve.wait_ge(s["scored"][x], count(i, p, u) + 1)
                dve.wait_ge(s["exped"][x], count(i, p, u))
                if bias is None:
                    dve.tensor_reduce(nm[:, b, x:x + 1], scores_of(x, lo, n), AX.X, ALU.max, negate=True).then_inc(s["maxed"][x], 1)
                else:
                    kind = min(u, 1) if u < 3 else 2
                    dve.wait_ge(s["em_done"][p], FIRST + i + 1)
                    if not first:
                        for bank in range(2):
                            dve.wait_ge(s["turned"][bank], weights_turned(i, last, p, u, x, bank))
                    at = em_block[kind, lo - t + 1]
                    dve.tensor_tensor(pr[:, b, x, 0:n * P], scores_of(x, 0, n),
                                      EM[:, p, x, at:at + n].rearrange("p d k -> p (d k)"), ALU.add).then_inc(s["maxed"][x], 1)
                    dve.wait_ge(s["maxed"][x], count(i, p, u) + 1)
                    dve.tensor_reduce(nm[:, b, x:x + 1], pr[:, b, x, 0:n * P], AX.X, ALU.max, negate=True).then_inc(s["lowered"][x], 1)

            def invert(dve, i, last, p, u, x, chain):
                b, before = par(p, u)
                dve.wait_ge(s["exped"][x], count(i, p, u) + 1)
                if combine is not None and x == 1:
                    chain(dve.reciprocal(rc[:, b, 1:2], sm[:, b, 1:2]))
                    dve.tensor_scalar(rc[:, b, 1:2], rc[:, b, 1:2], combine, None, ALU.mult).then_inc(s["inverted"][1], 1)
                else:
                    dve.reciprocal(rc[:, b, x:x + 1], sm[:, b, x:x + 1]).then_inc(s["inverted"][x], 1)

            @block.vector
            def _(dve):
                if not split:
                    dve.wait_ge(s["zeroed"], FIRST + 2)
                empty_group(dve, 0, 0, lambda k: (k % 2, FIRST + k // 2))
                before_loop = Chain(dve, s["dve_chain"], FIRST)
                for k in range(LEAD):
                    highest(dve, 0, False, 0, k // nh, k % nh, first=True)
                    if k > 0:
                        invert(dve, 0, False, 0, (k - 1) // nh, (k - 1) % nh, before_loop)

                def body(i, last):
                    chain = Chain(dve, s["dve_chain"], FIRST + before_loop.n + i * 2 * NU)
                    for p in range(2):
                        for u in range(NU):
                            if combine is not None:
                                t, lo, hi = U[u]
                                b, before = par(p, u)
                                dve.wait_ge(s["weighted"][1], count(i, p, u) + 1)
                                dve.wait_ge(s["inverted"][0], count(i, p, u) + 1)
                                w0, w1 = pr[:, b, 0, 0:(hi - lo) * P], pr[:, b, 1, 0:(hi - lo) * P]
                                dve.scalar_tensor_tensor(out=w0, in0=w0, scalar=rc[:, b, 0:1], in1=w1, op0=ALU.mult,
                                                         op1=ALU.add).then_inc(s["weighted"][0], 1)
                            for x in range(nh):
                                if heads == nh:
                                    empty_weights(dve, 0, i, last, p, u, x)
                                ahead = item_behind(i, last, p, u, x, LEAD)
                                if ahead:
                                    highest(dve, *ahead)
                                ahead = item_behind(i, last, p, u, x, LEAD - 1)
                                if ahead:
                                    invert(dve, *ahead, chain)
                                if heads < nh and x == 0:
                                    empty_weights(dve, 0, i, last, p, u, 0)
                            if u == TURN_AT and not (last and p):
                                empty_group(dve, 0, 1 - p, lambda k: of_bank(i, last, ("turn", p, k)))
                        for b in range(2):
                            dve.wait_ge(s["pv"][b], values_done(i, p, b))
                        o = out(i, p)
                        for bk in range(ob):
                            n = min(4, tiles - 4 * bk) * P
                            dst, src = o[:, bk * 512:bk * 512 + n], O[:, p if ob == 1 else bk, 0:n]
                            if gate is None:
                                ins = dve.tensor_copy(dst, src)
                            else:
                                ins = dve.tensor_tensor(dst, src, dst, ALU.mult)
                        ins.then_inc(s["o_done"], 1)
                iterations(dve, body)

            @block.scalar
            def _(act):
                def exponential(i, last, p, u, x, first=False):
                    t, lo, hi = U[u]
                    b, before = par(p, u)
                    act.wait_ge(s["maxed"][x] if bias is None else s["lowered"][x], count(i, p, u) + 1)
                    if bias is None:
                        if not first:
                            act.wait_ge(s["turned"][0], weights_turned(i, last, p, u, x, 0))
                            act.wait_ge(s["turned"][1], weights_turned(i, last, p, u, x, 1))
                        src = scores_of(x, lo, hi - lo)
                    else:
                        src = pr[:, b, x, 0:(hi - lo) * P]
                    act.activation(pr[:, b, x, 0:(hi - lo) * P], src, ACT.Exp, bias=nm[:, b, x:x + 1],
                                   accum_out=sm[:, b, x:x + 1]).then_inc(s["exped"][x], 1)

                if not split:
                    act.wait_ge(s["zeroed"], FIRST + 2)
                empty_group(act, 1, 0, lambda k: (k % 2, FIRST + k // 2))
                for k in range(LEAD):
                    exponential(0, False, 0, k // nh, k % nh, first=True)

                def body(i, last):
                    for p in range(2):
                        for u in range(NU):
                            for x in range(nh):
                                if heads == nh:
                                    empty_weights(act, 1, i, last, p, u, x)
                                ahead = item_behind(i, last, p, u, x, LEAD)
                                if ahead:
                                    exponential(*ahead)
                                if heads < nh and x == 0:
                                    empty_weights(act, 1, i, last, p, u, 0)
                            if u == TURN_AT and not (last and p):
                                empty_group(act, 1, 1 - p, lambda k: of_bank(i, last, ("turn", p, k)))
                iterations(act, body)


def bias_table(nc, name, m, rpb, table):
    half = NA_HEADS // 2
    q = half * (2 * WIN_R - 1)
    wide = 4 * CB - 1
    with ExitStack() as c:
        pad = c.enter_context(nc.sbuf_tensor(f"{name}_pad", [P, 2, wide], F32))
        with stage(nc, name, zero=None, loaded=None, stored=None) as (block, s):
            @block.vector
            def _(dve):
                dve.memset(pad[:], 0.0).then_inc(s["zero"], 1)

            @block.sync
            def _(sp):
                sp.wait_ge(s["zero"], 1)
                sp.dma_start(pad[0:q, :, CB:CB + 2 * WIN_C - 1], rpb.rearrange("(a h) r c -> (h r) a c", a=2)).then_inc(s["loaded"], 16)
                sp.wait_ge(s["loaded"], 16)
                for cc in range(CB):
                    sp.dma_start(table[cc].rearrange("(a h) (r c) -> (h r) a c", a=2, c=3 * CB),
                                 pad[0:q, :, CB - 1 - cc:CB - 1 - cc + 3 * CB]).then_inc(s["stored"], 16)
                sp.wait_ge(s["stored"], 16 * CB)


def scale_tables(nc, name, jobs):
    with stage(nc, name, chain=None) as (block, s):
        @block.vector
        def _(dve):
            chain = Chain(dve, s["chain"])
            for out, in_, vec, swap, factor in jobs:
                n, w = in_.shape[1], in_.shape[2]
                if swap is None:
                    chain(dve.tensor_tensor(out, in_, vec.unsqueeze(1).to_broadcast([P, n, w]), ALU.mult))
                else:
                    h = w // (2 * swap)
                    for g in range(swap):
                        for a in range(2):
                            at, of = (2 * g + a) * h, (2 * g + 1 - a) * h
                            chain(dve.tensor_tensor(out[:, :, at:at + h], in_[:, :, at:at + h],
                                                    vec[:, of:of + h].unsqueeze(1).to_broadcast([P, n, h]), ALU.mult))
                if factor != 1.0:
                    chain(dve.tensor_scalar(out, out, factor, None, ALU.mult))


@contextmanager
def modulations(nc, name, m, layers):
    NC = 3 * D // 1024
    NL = len(layers)
    with ExitStack() as c:
        sb = lambda n, s: c.enter_context(nc.sbuf_tensor(f"{name}_{n}", s, F32))
        wb = sb("w", [P, 2, DK // 2, 1024])
        sc = sb("silu", [P, DK, 2])
        rows = sb("rows", [P, 2 * NL, 512])
        cols, bg = sb("cols", [P, 4, P]), sb("bg", [P, NL, D])
        ps = c.enter_context(nc.psum_tensor(f"{name}_ps", [P, 2 * NL, 512], F32))
        pt = c.enter_context(nc.psum_tensor(f"{name}_pt", [P, 512], F32))
        pg = c.enter_context(nc.psum_tensor(f"{name}_pg", [P, 2, 512], F32))
        s = c.enter_context(semaphores(nc, name, loaded=2, silu=None, mm=None, zeroed=None, rows_done=None,
                                       turned=None, spread=None, added=None, chain=None, bg=None))

        def sync(sp):
            for l, (w, _, b_gate, *_) in enumerate(layers):
                sp.dma_start(bg[:, l], b_gate).then_inc(s["bg"], 16)
                for x in range(NC):
                    for z in range(2):
                        if l * NC + x:
                            sp.wait_ge(s["mm"], 2 * (l * NC + x) + z - 1)
                        sp.dma_start(wb[:, z], w.rearrange("(z k p) n -> p z k n", p=P, z=2)[:, z, :, x * 1024:(x + 1) * 1024]).then_inc(s["loaded"][z], 16)

        def scalar(act, part, parts):
            if part == 0:
                act.activation(sc[:], m["cond"].rearrange("p (k c) -> p k c", c=2), ACT.Silu).then_inc(s["silu"], 1)

        def tensor(pe):
            pe.wait_ge(s["silu"], 1)
            for n in range(NL * NC):
                l, x = n // NC, n % NC
                for z in range(2):
                    pe.wait_ge(s["loaded"][z], 16 * (n + 1))
                    for k in range(DK // 2):
                        for y in range(2):
                            j = (2 * x + y) % 4
                            last = pe.matmul(ps[32 * j:32 * j + 2, 2 * l + x // 2, :], sc[:, z * (DK // 2) + k, :], wb[:, z, k, y * 512:(y + 1) * 512],
                                             start=(z == 0 and k == 0), stop=(z == 1 and k == DK // 2 - 1))
                    last.then_inc(s["mm"], 1)
            adds = 0
            for l, (_, _, _, _, _, _, _, conds) in enumerate(layers):
                pe.wait_ge(s["rows_done"], 6 * NL)
                if l:
                    pe.wait_ge(s["chain"], 1)
                for b in range(4):
                    last = pe.transpose(pt[:, b * P:(b + 1) * P], rows[:, 2 * l, b * P:(b + 1) * P], m["ident"])
                last.then_inc(s["turned"], 1)
                for j in range(2):
                    if adds:
                        pe.wait_ge(s["added"], adds)
                    for x in range(conds):
                        last = pe.matmul(pg[:, x, :], m["select"].rearrange("p (j q) -> p j q", q=P)[:, 2 * j + x, :], rows[:, 2 * l + 1, :],
                                         start=True, stop=True)
                    last.then_inc(s["spread"], 1)
                    adds += conds

        def vector(dve):
            chain = Chain(dve, s["chain"])
            dve.memset(rows[:], 0.0).then_inc(s["zeroed"], 1)
            dve.wait_ge(s["zeroed"], 1)
            for n in range(NL * NC):
                l, x = n // NC, n % NC
                dve.wait_ge(s["mm"], 2 * (n + 1))
                for y in range(2):
                    j = (2 * x + y) % 4
                    dve.tensor_copy(rows[32 * j:32 * j + 2, 2 * l + x // 2, :], ps[32 * j:32 * j + 2, 2 * l + x // 2, :]).then_inc(s["rows_done"], 1)
            spreads = 0
            for l, (_, b_cols, _, norm, gain, shift, gate, conds) in enumerate(layers):
                dve.wait_ge(s["turned"], l + 1)
                chain(dve.tensor_copy(cols[:], pt[:].rearrange("p (b q) -> p b q", q=P)))
                for half in range(2):
                    for x, t, n in ((0, 0, XT), (1, XT, CT)):
                        spread = lambda v: v.unsqueeze(1).to_broadcast([P, n, 4])
                        sh, g = (v[:, t:t + n, half * 4:half * 4 + 4] for v in (shift, gain))
                        first, first_scale = cols[:, :, 32 * half + x], cols[:, :, 32 * (2 + half) + x]
                        chain(dve.tensor_tensor(sh, spread(first), spread(b_cols[:, half * 4:half * 4 + 4]), ALU.add))
                        chain(dve.tensor_tensor(g, spread(first_scale), spread(b_cols[:, DK + half * 4:DK + half * 4 + 4]), ALU.add))
                        chain(dve.scalar_tensor_tensor(out=g, in0=g, scalar=1.0, in1=spread(norm[:, half * 4:half * 4 + 4]), op0=ALU.add, op1=ALU.mult))
                dve.wait_ge(s["bg"], 16 * NL)
                for j in range(2):
                    spreads += 1
                    dve.wait_ge(s["spread"], spreads)
                    for x in range(conds):
                        dve.tensor_tensor(gate[:, x, j * 512:(j + 1) * 512], pg[:, x, :], bg[:, l, j * 512:(j + 1) * 512], ALU.add).then_inc(s["added"], 1)
            dve.wait_ge(s["added"], sum(2 * layer[-1] for layer in layers))

        yield dict(sync=sync, tensor=tensor, scalar=scalar, vector=vector)


def first_of(dve, chain, out, x, top, prio, best, n):
    shape = list(x.shape)
    chain(dve.tensor_tensor(out, x, top.unsqueeze(2).to_broadcast(shape), ALU.is_equal))
    chain(dve.tensor_tensor(out, out, prio.unsqueeze(1).to_broadcast(shape), ALU.mult))
    chain(dve.tensor_reduce(best, out, AX.X, ALU.max))
    chain(dve.tensor_tensor(out, out, best.unsqueeze(2).to_broadcast(shape), ALU.is_equal))


def route(nc, name, m, act_t, w_router, slots_init, slot_ids_dram, slots, block_expert, n_pairs):
    NL = N_GROUPS + N_EXPERTS
    with ExitStack() as c:
        sb = lambda n, s, dt=F32: c.enter_context(nc.sbuf_tensor(f"{name}_{n}", s, dt))
        wr, L = sb("wr", [P, DK, NL]), sb("L", [P, XT, NL])
        top_g, best, sum_g = sb("top_g", [P, XT]), sb("best", [P, XT]), sb("sum_g", [P, XT])
        G, z = sb("G", [P, XT, N_GROUPS]), sb("z", [P, XT, N_GROUPS])
        picked = sb("picked", [P, XT, N_GROUPS, PER_GROUP])
        el = sb("el", [P, XT, PER_GROUP])
        E = sb("E", [P, 2, XT, PER_GROUP])
        top_e = sb("top_e", [P, 2, XT])
        ratio, wt = sb("ratio", [P, XT]), sb("wt", [P, 2, XT])
        O = sb("O", [P, 2, XT, N_GROUPS, PER_GROUP])
        A = sb("A", [P, XT, N_EXPERTS])
        pos, dest = sb("pos", [P, XT, N_EXPERTS]), sb("dest", [P, 2, XT])
        dest_i = sb("dest_i", [P, 2, XT], I32)
        rows = sb("rows", [P, 2, XT, 4], I32)
        ids = sb("ids", [P, 2, XT, 2], I32)
        cnt, nb, upto, start, one = (sb(x, [P, N_EXPERTS]) for x in ("cnt", "nb", "upto", "start", "one"))
        cmp, be = sb("cmp", [P, MAX_BLOCKS, N_EXPERTS]), sb("be", [P, MAX_BLOCKS])
        pl = c.enter_context(nc.psum_tensor(f"{name}_pl", [P, XT, P], F32))
        pk = c.enter_context(nc.psum_tensor(f"{name}_pk", [P, 8, N_EXPERTS], F32))
        with stage(nc, name, loaded=None, logits=None, chosen=None, ranked=None, chain=None, low=None, exped=None,
                   init=None, table=None, put=None) as (block, s):
            @block.sync
            def _(sp):
                sp.dma_start(slots, slots_init).then_inc(s["init"], 16)
                sp.dma_start(wr[:], w_router.rearrange("(k p) n -> p k n", p=P)).then_inc(s["loaded"], 16)
                sp.dma_start(ids[:].rearrange("p a b c -> p (a b c)"), slot_ids_dram).then_inc(s["loaded"], 16)

            @block.tensor
            def _(pe):
                pe.wait_ge(s["loaded"], 32)
                for t in range(XT):
                    for k in range(DK):
                        last = pe.matmul(pl[:, t, 0:NL], act_t[:, k, t * P:(t + 1) * P], wr[:, k, :], start=(k == 0), stop=(k == DK - 1))
                last.then_inc(s["logits"], 1)
                pe.wait_ge(s["chosen"], 1)
                for t in range(XT + 1):
                    for b in range(t + (t < XT)):
                        last = pe.matmul(pk[:, t, :], m["before"] if b == t else m["ones"], A[:, b, :], start=(b == 0),
                                         stop=(b == t + (t < XT) - 1))
                last.then_inc(s["ranked"], 1)

            @block.scalar
            def _(act):
                act.wait_ge(s["low"], 1)
                act.activation(z[:], z[:], ACT.Exp).then_inc(s["exped"], 1)
                act.wait_ge(s["low"], 2)
                act.activation(ratio[:], ratio[:], ACT.Exp).then_inc(s["exped"], 1)

            @block.vector
            def _(dve):
                chain = Chain(dve, s["chain"])
                dve.wait_ge(s["logits"], 1)
                chain(dve.tensor_copy(L[:], pl[:, :, 0:NL]))
                LG, LE = L[:, :, 0:N_GROUPS], L[:, :, N_GROUPS:NL].rearrange("p t (g e) -> p t g e", g=N_GROUPS)
                chain(dve.tensor_reduce(top_g[:], LG, AX.X, ALU.max))
                dve.tensor_tensor(z[:], LG, top_g[:].unsqueeze(2).to_broadcast([P, XT, N_GROUPS]), ALU.subtract).then_inc(s["low"], 1)
                first_of(dve, chain, G[:], LG, top_g[:], m["prio4"], best[:], N_GROUPS)
                chain(dve.tensor_tensor(picked[:], LE, G[:].unsqueeze(3).to_broadcast([P, XT, N_GROUPS, PER_GROUP]), ALU.mult))
                chain(dve.tensor_reduce(el[:], picked[:].rearrange("p t g e -> p t e g"), AX.X, ALU.add))
                for x in range(2):
                    chain(dve.tensor_reduce(top_e[:, x], el[:], AX.X, ALU.max))
                    first_of(dve, chain, E[:, x], el[:], top_e[:, x], m["prio8"], best[:], PER_GROUP)
                    if x == 0:
                        chain(dve.scalar_tensor_tensor(out=el[:], in0=E[:, 0], scalar=NEG, in1=el[:], op0=ALU.mult, op1=ALU.add))
                dve.tensor_tensor(ratio[:], top_e[:, 1], top_e[:, 0], ALU.subtract).then_inc(s["low"], 1)
                for x in range(2):
                    chain(dve.tensor_tensor(O[:, x], G[:].unsqueeze(3).to_broadcast([P, XT, N_GROUPS, PER_GROUP]),
                                            E[:, x].unsqueeze(2).to_broadcast([P, XT, N_GROUPS, PER_GROUP]), ALU.mult))
                flat = lambda v: v.rearrange("p t g e -> p t (g e)")
                dve.tensor_tensor(A[:], flat(O[:, 0]), flat(O[:, 1]), ALU.add).then_inc(s["chosen"], 1)
                dve.wait_ge(s["exped"], 1)
                chain(dve.tensor_reduce(sum_g[:], z[:], AX.X, ALU.add))
                dve.wait_ge(s["exped"], 2)
                chain(dve.tensor_scalar(wt[:, 1], ratio[:], 1.0, None, ALU.add))
                chain(dve.tensor_tensor(wt[:, 1], wt[:, 1], sum_g[:], ALU.mult))
                chain(dve.reciprocal(wt[:, 0], wt[:, 1]))
                chain(dve.tensor_tensor(wt[:, 1], wt[:, 0], ratio[:], ALU.mult))
                chain(dve.memset(one[:], 1.0))
                chain(dve.memset(rows[:], 0))
                chain(dve.tensor_copy(rows[:, :, :, 0:2], ids[:]))
                chain(dve.tensor_copy(rows[:].bitcast(F32)[:, :, :, 2], wt[:]))
                dve.wait_ge(s["ranked"], 1)
                chain(dve.tensor_copy(cnt[:], pk[:, XT, :]))
                chain(dve.tensor_scalar(nb[:], cnt[:], 0.0, None, ALU.is_gt))
                for b in range(1, SEQ // CAP):
                    chain(dve.scalar_tensor_tensor(out=nb[:], in0=cnt[:], scalar=float(b * CAP), in1=nb[:], op0=ALU.is_gt, op1=ALU.add))
                chain(dve.tensor_tensor_scan(upto[:], one[:], nb[:], 0.0, ALU.mult, ALU.add))
                chain(dve.tensor_tensor(start[:], upto[:], nb[:], ALU.subtract))
                chain(dve.tensor_scalar(start[:], start[:], float(CAP), None, ALU.mult))
                chain(dve.tensor_tensor(pos[:], pk[:, 0:XT, :], start[:].unsqueeze(1).to_broadcast([P, XT, N_EXPERTS]), ALU.add))
                for x in range(2):
                    chain(dve.tensor_tensor(A[:], flat(O[:, x]), pos[:], ALU.mult))
                    chain(dve.tensor_reduce(dest[:, x], A[:], AX.X, ALU.add))
                chain(dve.tensor_copy(dest_i[:], dest[:]))
                chain(dve.tensor_tensor(cmp[:], upto[:].unsqueeze(1).to_broadcast([P, MAX_BLOCKS, N_EXPERTS]),
                                        m["block_no"].unsqueeze(2).to_broadcast([P, MAX_BLOCKS, N_EXPERTS]), ALU.is_le))
                chain(dve.tensor_reduce(be[:], cmp[:], AX.X, ALU.add))
                chain(dve.tensor_scalar(be[:], be[:], float(N_EXPERTS - 1), None, ALU.min))
                chain(dve.tensor_copy(block_expert, be[0:1, :]))
                even = m["block_no"].rearrange("p (i a) -> p i a", a=2)[:, :, 0]
                total = upto[:, N_EXPERTS - 1:N_EXPERTS]
                chain(dve.tensor_tensor(be[:, 0:MAX_BLOCKS // 2], even, total.to_broadcast([P, MAX_BLOCKS // 2]), ALU.is_lt))
                chain(dve.tensor_reduce(total, be[:, 0:MAX_BLOCKS // 2], AX.X, ALU.add))
                dve.tensor_copy(n_pairs, total[0:1]).then_inc(s["table"], 1)

            @block.gpsimd
            def _(pool):
                pool.wait_ge(s["init"], 16)
                pool.wait_ge(s["table"], 1)
                for n in range(2 * XT):
                    pool.indirect_dma_start(out=slots, out_offset=bass.IndirectOffsetOnAxis(ap=dest_i[:, n // XT, n % XT:n % XT + 1], axis=0),
                                            in_=rows[:, n // XT, n % XT, :], in_offset=None).then_inc(s["put"], 16)
                    pool.wait_ge(s["put"], 16 * (n + 1))


def expert_blocks(nc, name, m, block_expert, n_pairs, slots, halves, xn, w1, w3, w2, ys):
    H2 = D_EXPERT // 2
    FK = D_EXPERT // P
    FIRST = 2
    TB = MAX_BLOCKS + 2
    with ExitStack() as c:
        sb = lambda n, s, dt=F32: c.enter_context(nc.sbuf_tensor(f"{name}_{n}", s, dt))
        w1b, w3b, w2b = sb("w1", [P, 2, DK, D_EXPERT]), sb("w3", [P, 2, DK, D_EXPERT]), sb("w2", [P, 2, FK, D])
        meta, index = sb("meta", [P, TB, 4], I32), sb("index", [P, 2, TB], I32)
        xg, xT = sb("xg", [P, 2, D // 2]), sb("xT", [P, 4, P])
        sact, hid, hT, yb = sb("silu", [P, H2]), sb("hid", [P, H2]), sb("hT", [P, 2, P]), sb("y", [P, 2, D // 2])
        hv, current = sb("halves", [P, 2], I32), sb("current", [P, 2, 2], I32)
        bank = lambda n: c.enter_context(nc.psum_tensor(f"{name}_{n}", [P, 512], F32))
        px, p1, p3, ph, py = bank("px"), bank("p1"), bank("p3"), bank("ph"), bank("py")
        x_rows = xn.rearrange("t (a d) -> (t a) d", a=2)
        y_rows = ys.rearrange("t (a d) -> (t a) d", a=2)
        with stage(nc, name, start=FIRST, software_dma=("got", "put"), halves=None, w1=2, w3=2, w2=2, idx=None,
                   got=2, x_turned=None, x_in=None, h1=None, h3=None, silu=None, hid=None, h_turned=None,
                   h_in=None, y=None, y_out=None, current=None, go=None, put=2) as (block, s):
            trips = lambda eng: eng.value_load(n_pairs, min_val=1, max_val=MAX_BLOCKS // 2)

            @block.sync
            def _(sp):
                sp.dma_start(hv[:], halves).then_inc(s["halves"], 16)
                with sp.Fori(0, trips(sp)) as i:
                    for p in range(2):
                        e = sp.value_load(block_expert[:, ds(2 * i + p, 1)], min_val=0, max_val=N_EXPERTS - 1)
                        for w, wb, got, done in ((w1, w1b, "w1", "h1"), (w3, w3b, "w3", "h3"), (w2, w2b, "w2", "y")):
                            sp.wait_ge(s[done], FIRST + 2 * i + p - 1)
                            sp.dma_start(wb[:, p], w[ds(e, 1)].rearrange("a (k p) n -> p (a k) n", p=P)).then_inc(s[got][p], 16)

            @block.gpsimd
            def _(pool):
                def indices(which, p, b):
                    pool.tensor_copy(current[:, which, p:p + 1], index[:, which, ds(b, 1)]).then_inc(s["current"], 1)

                def gather(p):
                    pool.indirect_dma_start(out=xg[:, p, :], out_offset=None, in_=x_rows,
                                            in_offset=bass.IndirectOffsetOnAxis(ap=current[:, 0, p:p + 1], axis=0)).then_inc(s["got"][p], 16)
                for h in range(2):
                    pool.dma_start(meta[h * CAP:(h + 1) * CAP], slots.rearrange("(b s) f -> s b f", s=CAP)).then_inc(s["put"][h], 16)
                pool.wait_ge(s["put"][0], 16)
                pool.wait_ge(s["put"][1], 16)
                pool.wait_ge(s["halves"], FIRST + 16)
                pool.tensor_tensor(index[:], meta[:, :, 0:2].rearrange("p b a -> p a b"), hv[:].unsqueeze(2).to_broadcast([P, 2, TB]), ALU.add).then_inc(s["idx"], 1)
                pool.wait_ge(s["idx"], FIRST + 1)
                for p in range(2):
                    indices(0, p, p)
                    pool.wait_ge(s["current"], FIRST + p + 1)
                    gather(p)
                with pool.Fori(0, trips(pool)) as i:
                    for p in range(2):
                        pool.wait_ge(s["x_turned"], FIRST + 2 * i + p + 1)
                        pool.sem_inc(s["go"], 1)
                        pool.wait_ge(s["got"][p], 16 * i + 16)
                        pool.sem_inc(s["go"], 1)
                        pool.wait_ge(s["put"][p], 16 * i + 16)
                        pool.sem_inc(s["go"], 1)
                        indices(0, p, 2 * i + p + 2)
                        indices(1, p, 2 * i + p)
                        pool.wait_ge(s["current"], FIRST + 2 + 4 * i + 2 * p + 2)
                        pool.sem_inc(s["go"], 1)
                        gather(p)
                        pool.wait_ge(s["y_out"], FIRST + 2 * i + p + 1)
                        pool.sem_inc(s["go"], 1)
                        pool.wait_ge(s["put"][1 - p], 16 * (i + p) + 16)
                        pool.sem_inc(s["go"], 1)
                        pool.indirect_dma_start(out=y_rows, out_offset=bass.IndirectOffsetOnAxis(ap=current[:, 1, p:p + 1], axis=0),
                                                in_=yb[:, p, :], in_offset=None).then_inc(s["put"][p], 16)
                pairs = trips(pool)
                for p in range(2):
                    pool.wait_ge(s["got"][p], 16 * pairs + 16)
                    pool.sem_inc(s["go"], 1)
                    pool.wait_ge(s["put"][p], 16 * pairs + 16)
                    pool.sem_inc(s["go"], 1)

            @block.tensor
            def _(pe):
                def turn_x(p, i):
                    pe.wait_ge(s["got"][p], 16 * i + 16)
                    for j in range(4):
                        last = pe.transpose(px[:, j * P:(j + 1) * P], xg[:, p, j * P:(j + 1) * P], m["ident"])
                    last.then_inc(s["x_turned"], 1)
                turn_x(0, 0)
                with pe.Fori(0, trips(pe)) as i:
                    for p in range(2):
                        b = 2 * i + p
                        pe.wait_ge(s["x_in"], FIRST + b + 1)
                        for got, wb, out, done, used in (("w1", w1b, p1, "h1", "silu"), ("w3", w3b, p3, "h3", "hid")):
                            pe.wait_ge(s[got][p], FIRST + 16 * i + 16)
                            pe.wait_ge(s[used], FIRST + b)
                            for k in range(DK):
                                x = xT[:, k % 4, (k // 4) * CAP:(k // 4 + 1) * CAP]
                                for h in range(2):
                                    last = pe.matmul(out[h * CAP:(h + 1) * CAP, 0:H2], x, wb[:, p, k, h * H2:(h + 1) * H2],
                                                     start=(k == 0), stop=(k == DK - 1))
                            last.then_inc(s[done], 1)
                        turn_x(1 - p, i + p)
                        pe.wait_ge(s["hid"], FIRST + b + 1)
                        for j in range(2):
                            last = pe.transpose(ph[:, j * P:(j + 1) * P], hid[:, j * P:(j + 1) * P], m["ident"])
                        last.then_inc(s["h_turned"], 1)
                        pe.wait_ge(s["w2"][p], FIRST + 16 * i + 16)
                        pe.wait_ge(s["h_in"], FIRST + b + 1)
                        pe.wait_ge(s["y_out"], FIRST + b)
                        for f in range(FK):
                            x = hT[:, f % 2, (f // 2) * CAP:(f // 2 + 1) * CAP]
                            for h in range(2):
                                last = pe.matmul(py[h * CAP:(h + 1) * CAP, :], x, w2b[:, p, f, h * 512:(h + 1) * 512],
                                                 start=(f == 0), stop=(f == FK - 1))
                        last.then_inc(s["y"], 1)

            @block.scalar
            def _(act):
                with act.Fori(0, trips(act)) as i:
                    for p in range(2):
                        b = 2 * i + p
                        act.wait_ge(s["h1"], FIRST + b + 1)
                        act.wait_ge(s["hid"], FIRST + b)
                        act.activation(sact[:], p1[:, 0:H2], ACT.Silu).then_inc(s["silu"], 1)
                        act.wait_ge(s["y"], FIRST + b + 1)
                        act.wait_ge(s["put"][p], 16 * i + 16)
                        act.activation(yb[:, p, :], py[:], ACT.Copy,
                                       scale=meta[:].bitcast(F32)[:, ds(b, 1), 2]).then_inc(s["y_out"], 1)

            @block.vector
            def _(dve):
                gain = m["g_ffn"].rearrange("p (h j) -> p j h", h=2).unsqueeze(3).to_broadcast([P, 4, 2, CAP])

                def take_x(b):
                    dve.wait_ge(s["x_turned"], FIRST + b + 1)
                    dve.wait_ge(s["h3"], FIRST + b)
                    dve.tensor_tensor(xT[:].rearrange("p j (h q) -> p j h q", h=2),
                                      px[:].rearrange("p (j h q) -> p j h q", j=4, h=2), gain, ALU.mult).then_inc(s["x_in"], 1)
                take_x(0)
                with dve.Fori(0, trips(dve)) as i:
                    for p in range(2):
                        b = 2 * i + p
                        dve.wait_ge(s["silu"], FIRST + b + 1)
                        dve.wait_ge(s["h3"], FIRST + b + 1)
                        dve.wait_ge(s["h_turned"], FIRST + b)
                        dve.tensor_tensor(hid[:], p3[:, 0:H2], sact[:], ALU.mult).then_inc(s["hid"], 1)
                        take_x(b + 1)
                        dve.wait_ge(s["h_turned"], FIRST + b + 1)
                        dve.wait_ge(s["y"], FIRST + b)
                        dve.tensor_copy(hT[:].rearrange("p j q -> p (j q)"), ph[:, 0:2 * P]).then_inc(s["h_in"], 1)


def add_experts(nc, name, ys, h):
    with ExitStack() as c:
        y = c.enter_context(nc.sbuf_tensor(f"{name}_y", [P, 2, XT, D], F32))
        with stage(nc, name, loaded=2, chain=None) as (block, s):
            @block.sync
            def _(sp):
                for x in range(2):
                    sp.dma_start(y[:, x], ys[x * SEQ:(x + 1) * SEQ, :].rearrange("(t p) d -> p t d", p=P)).then_inc(s["loaded"][x], 16)

            @block.vector
            def _(dve):
                chain = Chain(dve, s["chain"])
                for x in range(2):
                    dve.wait_ge(s["loaded"][x], 16)
                    chain(dve.tensor_tensor(h[:, 0:XT], h[:, 0:XT], y[:, x], ALU.add))


def load(nc, name, pairs):
    with stage(nc, name, sp_in=None, act_in=None) as (block, s):
        @block.sync
        def _(sp):
            for out, in_ in pairs[0::2]:
                sp.dma_start(out, in_).then_inc(s["sp_in"], 16)
            sp.wait_ge(s["sp_in"], 16 * len(pairs[0::2]))

        if len(pairs) > 1:
            @block.scalar
            def _(act):
                for out, in_ in pairs[1::2]:
                    act.dma_start(out, in_).then_inc(s["act_in"], 16)
                act.wait_ge(s["act_in"], 16 * len(pairs[1::2]))


def lambda_scalar(nc, name, m, neg_lam):
    with ExitStack() as c:
        prod = c.enter_context(nc.sbuf_tensor(f"{name}_prod", [P, 2, 64], F32))
        dots = c.enter_context(nc.sbuf_tensor(f"{name}_dots", [P, 2], F32))
        with stage(nc, name, chain=None, dots=None, exped=None) as (block, s):
            v = m["lam"].rearrange("p (a b d) -> p a b d", a=2, b=2)

            @block.vector
            def _(dve):
                chain = Chain(dve, s["chain"])
                chain(dve.tensor_tensor(prod[:], v[:, :, 0], v[:, :, 1], ALU.mult))
                dve.tensor_reduce(dots[:], prod[:], AX.X, ALU.add).then_inc(s["dots"], 1)
                dve.wait_ge(s["exped"], 1)
                chain(dve.tensor_tensor(neg_lam, dots[:, 1:2], dots[:, 0:1], ALU.subtract))
                chain(dve.tensor_scalar(neg_lam, neg_lam, -LAM_INIT, None, ALU.add))

            @block.scalar
            def _(act):
                act.wait_ge(s["dots"], 1)
                act.activation(dots[:], dots[:], ACT.Exp).then_inc(s["exped"], 1)


def sub_norm(nc, name, m, o, heads):
    with ExitStack() as c:
        sb = lambda n, s: c.enter_context(nc.sbuf_tensor(f"{name}_{n}", s, F32))
        half = sb("half", [P, SEQ])
        sq, root, inv, g = sb("sq", [P, heads, SEQ]), sb("root", [P, heads, SEQ]), sb("inv", [P, heads, SEQ]), sb("g", [P, 1])
        ps = c.enter_context(nc.psum_tensor(f"{name}_ps", [P, heads, SEQ], F32))
        with stage(nc, name, sq=None, summed=None, rooted=None, chain=None) as (block, s):
            @block.scalar
            def _(act):
                for h in range(heads):
                    act.activation(sq[:, h], o[:, h], ACT.Square).then_inc(s["sq"], 1)
                for h in range(heads):
                    act.wait_ge(s["summed"], h + 1)
                    act.activation(root[:, h], ps[:, h], ACT.Sqrt, bias=m["eps"], scale=1.0 / P).then_inc(s["rooted"], 1)

            @block.tensor
            def _(pe):
                for h in range(heads):
                    pe.wait_ge(s["sq"], h + 1)
                    pe.matmul(ps[:, h], m["ones"], sq[:, h], start=True, stop=True).then_inc(s["summed"], 1)

            @block.vector
            def _(dve):
                chain = Chain(dve, s["chain"])
                chain(dve.tensor_scalar(g[:], m["g_sub"], 1.0 - LAM_INIT, None, ALU.mult))
                for h in range(heads):
                    dve.wait_ge(s["rooted"], h + 1)
                    chain(inverse_root(dve, chain, ps[:, h], root[:, h], P, half[:], inv[:, h]))
                    chain(dve.scalar_tensor_tensor(out=o[:, h], in0=o[:, h], scalar=g[:], in1=inv[:, h], op0=ALU.mult, op1=ALU.mult))


def add_side(nc, name, m, g_ple, y, gate, h):
    with ExitStack() as c:
        sb = lambda n, s: c.enter_context(nc.sbuf_tensor(f"{name}_{n}", s, F32))
        sq, st, wide = sb("sq", [P, D]), sb("st", [P, 4, XT]), sb("g", [P, D])
        with stage(nc, name, chain=None, act_chain=None, rooted=None, loaded=None) as (block, s):
            @block.sync
            def _(sp):
                sp.dma_start(wide[:], g_ple).then_inc(s["loaded"], 16)

            @block.scalar
            def _(act):
                chain = Chain(act, s["act_chain"])
                for t in range(XT):
                    chain(act.activation(sq[:], y[:, t], ACT.Square, accum_out=st[:, 0, t:t + 1]))
                act.activation(st[:, 1], st[:, 0], ACT.Sqrt, bias=m["eps"], scale=1.0 / D).then_inc(s["rooted"], 1)

            @block.vector
            def _(dve):
                chain = Chain(dve, s["chain"])
                dve.wait_ge(s["loaded"], 16)
                chain(dve.tensor_tensor(gate, gate, wide[:].unsqueeze(1).to_broadcast([P, XT, D]), ALU.mult))
                dve.wait_ge(s["rooted"], 1)
                chain(inverse_root(dve, chain, st[:, 0], st[:, 1], D, st[:, 3], st[:, 2]))
                for t in range(XT):
                    chain(dve.scalar_tensor_tensor(out=gate[:, t], in0=y[:, t], scalar=st[:, 2, t:t + 1], in1=gate[:, t], op0=ALU.mult, op1=ALU.mult))
                    chain(dve.tensor_tensor(h[:, t], h[:, t], gate[:, t], ALU.add))


def store_to(nc, dst, width):
    return lambda eng, is_act, t, c, ps, tmp, chain: copy(nc, eng, is_act, dst[:, t, ds(c * width, width)], ps)


def add_to(h):
    return lambda eng, is_act, t, c, ps, tmp, chain: eng.tensor_tensor(h[:, t, ds(c * 512, 512)], h[:, t, ds(c * 512, 512)], ps, ALU.add)


def add_gated(h, gate):
    def emit(eng, is_act, t, c, ps, tmp, chain):
        chain(eng.tensor_tensor(tmp, ps, gate[:, 0 if t < XT else 1, ds(c * 512, 512)], ALU.mult))
        dst = h[:, t, ds(c * 512, 512)]
        return eng.tensor_tensor(dst, dst, tmp, ALU.add)
    return emit


def tokens_of(a):
    return lambda k, t: a[:, k, t * P:(t + 1) * P]


def build(nc, A, prm_at, const_at, stop=None, dbg=None):
    with ExitStack() as top:
        def sb(c, name, shape, dt=F32):
            return c.enter_context(nc.sbuf_tensor(name, shape, dt))

        prm = sb(top, "params", [P, sum(n for _, n in prm_at.values())])
        cst = sb(top, "consts", [P, sum(n for _, n in const_at.values())])
        m = {k: prm[:, a:a + n] for k, (a, n) in prm_at.items()}
        m.update({k: cst[:, a:a + n] for k, (a, n) in const_at.items()})
        hx = sb(top, "residual", [P, AT, D])
        of_layer_2 = ExitStack()
        mods = [[sb(c, f"{n}_gain", [P, AT, DK]), sb(c, f"{n}_shift", [P, AT, DK]), sb(c, f"{n}_gate", [P, conds, D])]
                for c, n, conds in ((top, "l1", 1), (of_layer_2, "l0", 2))][::-1]
        rows = lambda v: v.rearrange("(t p) d -> p t d", p=P)
        tiles = lambda v, w: v.rearrange("p (t w) -> p t w", w=w)
        table = nc.dram_tensor("bias_rows", [CB, NA_HEADS, (2 * WIN_R - 1) * 3 * CB], F32).ap()
        slots = nc.dram_tensor("slots", [(MAX_BLOCKS + 2) * CAP, 4], I32).ap()
        xn = nc.dram_tensor("expert_in", [SEQ, D], F32).ap()
        ys = nc.dram_tensor("expert_out", [2 * SEQ + CAP, D], F32).ap()

        def debug(key, ap):
            if stop == key:
                load(nc, "dbg", [(dbg, ap)])
                return True

        load(nc, "load", [(prm[:], A["params"]), (cst[:], A["consts"]),
                          (hx[:, 0:XT], rows(A["x"])), (hx[:, XT:AT], rows(A["ctx"]))])
        if debug("load", hx[:, 0:XT]): return

        with ExitStack() as c:
            oT = sb(c, "mix_out", [P, DK, SEQ])
            with ExitStack() as cc:
                proj = sb(cc, "mix_proj", [P, XT, 3 * D])
                bias_table(nc, "rpb", m, A["rpb"], table)
                with ExitStack() as ca:
                    aT = sb(ca, "mix_in", [P, DK, SEQ])
                    norm_transpose(nc, "mix_norm", m, lambda t: hx[:, ds(t, 1), :].rearrange("p a d -> p (a d)"), DK, XT, m["g_mix"], None, aT)
                    if debug("aT", aT[:, :, :]): return
                    dense(nc, "mix_in_w", tokens_of(aT), DK, XT, A["w_in"], 6, 512, store_to(nc, proj, 512))
                if debug("proj", proj[:, :, 0:1024]): return
                tabs = sb(cc, "mix_tabs", [P, 4, XT, 64])
                gains = sb(cc, "mix_gains", [P, 2, 1, NA_D])
                neg_lam = sb(cc, "neg_lam", [P, 1])
                sa, sn = 64 ** -0.5, NA_D ** -0.5
                scale_tables(nc, "mix_tab", [
                    (tabs[:, 0], tiles(m["full_cos"], 64), m["g_qa"], None, sa), (tabs[:, 1], tiles(m["full_sin"], 64), m["g_qa"], 1, sa),
                    (tabs[:, 2], tiles(m["full_cos"], 64), m["g_ka"], None, 1.0), (tabs[:, 3], tiles(m["full_sin"], 64), m["g_ka"], 1, 1.0),
                    (gains[:, 0], m["ones"][:, 0:NA_D].unsqueeze(1), m["g_qb"], None, sn), (gains[:, 1], m["ones"][:, 0:NA_D].unsqueeze(1), m["g_kb"], None, 1.0)])
                lambda_scalar(nc, "lam", m, neg_lam[:])

                def part(col, n, d):
                    return lambda t: proj[:, ds(t, 1), col:col + n * d].rearrange("p a (h d) -> p (a h) d", d=d)

                def row(tab):
                    return lambda t: tab[:, ds(t, 1), :].rearrange("p a d -> p (a d)")
                adaln = modulations(nc, "mod", m, [
                    (A["l0_w_mod"], m["l0_b"], A["l0_b_gate"], m["l0_norm"], *mods[0], 2),
                    (A["l1_w_mod"], m["l1_b"], A["l1_b_gate"], m["l1_norm"], *mods[1], 1)])
                with adaln as beside:
                    head_norms(nc, "mix_hn", m, XT, [
                        (part(0, 8, 64), 8, 64, row(tabs[:, 0]), (0, 1, 32, row(tabs[:, 1]))),
                        (part(512, 8, 64), 8, 64, row(tabs[:, 2]), (0, 1, 32, row(tabs[:, 3]))),
                        (part(1536, 16, 32), 16, 32, lambda t: gains[:, 0, 0], None),
                        (part(2048, 16, 32), 16, 32, lambda t: gains[:, 1, 0], None)], beside)
                if debug("hn", proj[:, :, 0:1024]): return
                if debug("hn2", proj[:, :, 1536:2560]): return

                def group(col):
                    return lambda i, p, dst: [(dst if len(dst.shape) == 3 else dst[:, 0], proj[:, :, ds(col + (2 * i + p) * P, P)])]
                attention(nc, "diff", m, 2, [(t, 0, XT) for t in range(XT)], 2, P, group(0), group(512), group(1024),
                          lambda i, p: oT[:, ds(2 * i + p, 1), :].rearrange("p a t -> p (a t)"), combine=neg_lam[:])
                sub_norm(nc, "subn", m, oT[:, 0:4], 4)
                if debug("diff", oT[:, 0:4]): return
                attention(nc, "near", m, 2, [(t, max(t - 1, 0), min(t + 2, XT)) for t in range(XT)], 4, NA_D,
                          group(1536), group(2048), group(2560),
                          lambda i, p: oT[:, ds(4 + 2 * i + p, 1), :].rearrange("p a t -> p (a t)"), bias=table,
                          spare=lambda p: proj[:, p, 0:4 * WIN_R * 3 * CB])
                if debug("near", oT[:, 4:8]): return
            dense(nc, "mix_out_w", tokens_of(oT), DK, XT, A["w_out"], 2, 512, add_to(hx), both=False)
        if debug("h1", hx[:, 0:XT]): return

        with ExitStack() as c:
            block_expert, n_pairs = sb(c, "block_expert", [P, MAX_BLOCKS], I32), sb(c, "n_pairs", [P, 1], I32)
            with ExitStack() as cc:
                aT = sb(cc, "ffn_in", [P, DK, SEQ])
                norm_transpose(nc, "ffn_norm", m, lambda t: hx[:, ds(t, 1), :].rearrange("p a d -> p (a d)"), DK, XT, m["g_ffn"], None, aT,
                               spill=xn.rearrange("(t p) d -> t p d", p=P))
                route(nc, "route", m, aT, A["w_router"], A["slots_init"], A["slot_ids"], slots, block_expert[0:1, :], n_pairs[0:1, :])
            expert_blocks(nc, "exp", m, block_expert[0:1, :], n_pairs[0:1, :], slots, A["halves"], xn, A["w1"], A["w3"], A["w2"], ys)
        add_experts(nc, "moe_add", ys, hx)
        if debug("h2", hx[:, 0:XT]): return

        with ExitStack() as c:
            side, sg = sb(c, "side", [P, XT, D]), sb(c, "side_gate", [P, XT, D])
            with ExitStack() as cc:
                pT = sb(cc, "side_in", [P, 2, SEQ])
                load(nc, "load_p", [(pT[:], A["p_t"].rearrange("(k p) t -> p k t", p=P))])
                dense(nc, "side_w", tokens_of(pT), 2, XT, A["w_ple"], 2, 512, store_to(nc, side, 512))
                aT = sb(cc, "plg_in", [P, DK, SEQ])
                norm_transpose(nc, "plg_norm", m, lambda t: hx[:, ds(t, 1), :].rearrange("p a d -> p (a d)"), DK, XT, m["g_plg"], None, aT)
                sg_raw = lambda eng, is_act, t, cidx, ps, tmp, chain: copy(nc, eng, is_act, sg[:, t, ds(cidx * 512, 512)], ps)
                dense(nc, "plg_w", tokens_of(aT), DK, XT, A["w_plg"], 2, 512, sg_raw)
            with stage(nc, "sigm", done=None) as (block, s):
                @block.scalar
                def _(act):
                    for t in range(XT):
                        act.activation(sg[:, t], sg[:, t], ACT.Sigmoid).then_inc(s["done"], 1)
            add_side(nc, "side_add", m, A["g_ple"], side, sg[:], hx)
        if debug("h3", hx[:, 0:XT]): return

        with ExitStack() as c:
            gain, shift, gate = mods[0]
            gT = sb(c, "l0_gT", [P, DK, AT * P])
            with ExitStack() as cc:
                proj = sb(cc, "l0_proj", [P, AT, 1536])
                tabs = sb(cc, "l0_tabs", [P, 4, AT, 64])
                s0 = 64 ** -0.5
                scale_tables(nc, "l0_tab", [
                    (tabs[:, 0], tiles(m["ax_cos"], 64), m["gqa_q"], None, s0), (tabs[:, 1], tiles(m["ax_sin"], 64), m["gqa_q"], 2, s0),
                    (tabs[:, 2], tiles(m["ax_cos"], 64), m["gqa_k"], None, 1.0), (tabs[:, 3], tiles(m["ax_sin"], 64), m["gqa_k"], 2, 1.0)])

                def part2(col, n, d):
                    return lambda t: proj[:, ds(t, 1), col:col + n * d].rearrange("p a (h d) -> p (a h) d", d=d)

                def row2(tab):
                    return lambda t: tab[:, ds(t, 1), :].rearrange("p a d -> p (a d)")
                with ExitStack() as ca:
                    aT = sb(ca, "l0_in", [P, DK, AT * P])
                    norm_transpose(nc, "l0_n", m, lambda t: hx[:, ds(t, 1), :].rearrange("p a d -> p (a d)"), DK, AT, gain, shift, aT)
                    dense(nc, "l0_w", tokens_of(aT), DK, AT, A["l0_w_in"], 3, 512, store_to(nc, proj, 512))
                    with transposed_products(nc, "l0_g", aT, DK, AT * P, A["l0_w_in"], 1536, 2,
                                             lambda n, a, w: gT[:, n, a:a + w]) as beside:
                        head_norms(nc, "l0_hn", m, AT, [
                            (part2(512, 16, 64), 16, 64, row2(tabs[:, 0]), (0, 2, 16, row2(tabs[:, 1]))),
                            (part2(0, 4, 64), 4, 64, row2(tabs[:, 2]), (0, 2, 16, row2(tabs[:, 3])))], beside)
                attention(nc, "gqa", m, 4, [(t, 0, AT) for t in range(XT)] + [(t, XT, AT) for t in range(XT, AT)], 2, 64,
                          lambda i, p, dst: [(dst[:, 0], proj[:, :, ds(512 + (2 * i + p) * P, P)])],
                          lambda i, p, dst: [(dst[:, 0, :, x * 64:(x + 1) * 64], proj[:, :, ds(i * 64, 64)]) for x in range(2)],
                          lambda i, p, dst: [(dst[:, :, x * 64:(x + 1) * 64], proj[:, :, ds(256 + i * 64, 64)]) for x in range(2)],
                          lambda i, p: gT[:, ds(2 * i + p, 1), :].rearrange("p a t -> p (a t)"), gate=True,
                          tiles=AT, ktiles=AT)
            dense(nc, "l0_o", tokens_of(gT), DK, AT, A["l0_w_out"], 2, 512, add_gated(hx, gate), both=False, links=1)
        of_layer_2.close()
        if debug("h4", hx[:, 0:XT]): return

        with ExitStack() as c:
            gain, shift, gate = mods[1]
            gT = sb(c, "l1_gT", [P, DK, SEQ])
            with ExitStack() as cc:
                latent, kv, q = sb(cc, "l1_latent", [P, AT, 288]), sb(cc, "l1_kv", [P, AT, 2048]), sb(cc, "l1_q", [P, XT, 1536])
                tc, tsn, tk = sb(cc, "l1_tc", [P, XT, 96]), sb(cc, "l1_ts", [P, XT, 32]), sb(cc, "l1_tk", [P, 2, AT, 32])
                tkn = sb(cc, "l1_tkn", [P, 1, 64])
                s1 = 96 ** -0.5
                scale_tables(nc, "l1_tab", [
                    (tc[:, :, 0:64], m["ones"][:, 0:64].unsqueeze(1).to_broadcast([P, XT, 64]), m["mla_q"][:, 0:64], None, s1),
                    (tc[:, :, 64:96], tiles(m["mla_cos"], 32)[:, 0:XT], m["mla_q"][:, 64:96], None, s1),
                    (tsn[:], tiles(m["mla_sin"], 32)[:, 0:XT], m["mla_q"][:, 64:96], 2, s1),
                    (tk[:, 0], tiles(m["mla_cos"], 32), m["mla_kr"], None, 1.0), (tk[:, 1], tiles(m["mla_sin"], 32), m["mla_kr"], 2, 1.0),
                    (tkn[:], m["ones"][:, 0:64].unsqueeze(1), m["mla_kn"], None, 1.0)])

                def row3(tab):
                    return lambda t: tab[:, ds(t, 1), :].rearrange("p a d -> p (a d)")
                with ExitStack() as ca:
                    aT = sb(ca, "l1_in", [P, DK, AT * P])
                    with ExitStack() as cd:
                        q_low = sb(cd, "l1_q_low", [P, XT, 384])
                        norm_transpose(nc, "l1_n", m, lambda t: hx[:, ds(t, 1), :].rearrange("p a d -> p (a d)"), DK, AT, gain, shift, aT)
                        dense(nc, "l1_wk", tokens_of(aT), DK, AT, A["l1_w_in"], 1, 288, store_to(nc, latent, 288))
                        dense(nc, "l1_wq", tokens_of(aT), DK, XT, A["l1_w_in"], 1, 384, store_to(nc, q_low, 384), col0=288)
                        kvT, qaT = sb(cd, "l1_kvT", [P, 2, AT * P]), sb(cd, "l1_qaT", [P, 3, SEQ])
                        norm_transpose(nc, "l1_nkv", m, lambda t: latent[:, ds(t, 1), 0:256].rearrange("p a d -> p (a d)"), 2, AT, m["kv_a_norm"], None, kvT)
                        norm_transpose(nc, "l1_nq", m, lambda t: q_low[:, ds(t, 1), :].rearrange("p a d -> p (a d)"), 3, XT, m["q_a_norm"], None, qaT)
                        dense(nc, "l1_kvb", tokens_of(kvT), 2, AT, A["l1_w_kv_b"], 4, 512, store_to(nc, kv, 512))
                        dense(nc, "l1_qb", tokens_of(qaT), 3, XT, A["l1_w_q_b"], 3, 512, store_to(nc, q, 512))
                    gates = lambda z: transposed_products(nc, f"l1_g{z}", aT, DK, SEQ, A["l1_w_in"], 672 + z * 512, 1,
                                                          lambda n, a, w: gT[:, 4 * z + n, a:a + w])
                    with gates(0) as beside:
                        head_norms(nc, "l1_hq", m, XT, [
                            (lambda t: q[:, ds(t, 1), :].rearrange("p a (h d) -> p (a h) d", d=96), 16, 96, row3(tc), (64, 2, 8, row3(tsn)))], beside)
                    with gates(1) as beside:
                        head_norms(nc, "l1_hk", m, AT, [
                            (lambda t: kv[:, ds(t, 1), :].rearrange("p a (h d) -> p (a h) d", d=128)[:, :, 0:64], 16, 64, lambda t: tkn[:, 0], None),
                            (lambda t: latent[:, ds(t, 1), 256:288], 1, 32, row3(tk[:, 0]), (0, 2, 8, row3(tk[:, 1])))], beside)
                attention(nc, "mla", m, 4, [(t, 0, AT) for t in range(XT)], 2, 64,
                          lambda i, p, dst: [(dst[:, x], q[:, :, ds((4 * i + 2 * p + x) * 96, 96)]) for x in range(2)],
                          lambda i, p, dst: [e for x in range(2) for e in
                                             ((dst[:, x, :, 0:64], kv[:, :, ds((4 * i + 2 * p + x) * 128, 64)]), (dst[:, x, :, 64:96], latent[:, :, 256:288]))],
                          lambda i, p, dst: [(dst[:, :, x * 64:(x + 1) * 64], kv[:, :, ds((4 * i + 2 * p + x) * 128 + 64, 64)]) for x in range(2)],
                          lambda i, p: gT[:, ds(2 * i + p, 1), :].rearrange("p a t -> p (a t)"), gate=True, split=96,
                          tiles=XT, ktiles=AT)
            dense(nc, "l1_o", tokens_of(gT), DK, XT, A["l1_w_out"], 2, 512, add_gated(hx, gate), both=False, links=1)
        load(nc, "store", [(rows(A["out"]), hx[:, 0:XT])])


def arrays(a):
    order = token_order()
    f = lambda k: np.ascontiguousarray(np.asarray(a[k]))
    prm_at, prm = parameters(a)
    const_at, cst = constants()
    init = slot_table()
    ins = dict(
        params=prm, consts=cst, x=f("x")[0][order], ctx=f("ctx_2")[0], p_t=f("p")[0, 0][order].T,
        rpb=f("rpb")[0], w_in=f("w_in")[0], w_out=f("w_out")[0],
        w_router=np.concatenate([f("w_rg")[0], f("w_re")[0]], 1),
        slots_init=np.concatenate([init, init[:2 * CAP]]), slot_ids=slot_ids(), halves=half_ids(),
        **wide_parameters(a), w1=f("w1")[0], w3=f("w3")[0], w2=f("w2")[0], w_plg=f("w_plg")[0], w_ple=f("w_ple")[0],
        l0_w_mod=f("l0_w_mod_2"), l0_w_in=f("l0_w_in_2"), l0_w_out=f("l0_w_out_2"),
        l1_w_mod=f("l1_w_mod_2"), l1_w_in=f("l1_w_in_2"), l1_w_kv_b=f("l1_w_kv_b_2"), l1_w_q_b=f("l1_w_q_b_2"),
        l1_w_out=f("l1_w_out_2"),
    )
    return {k: np.ascontiguousarray(v) for k, v in ins.items()}, prm_at, const_at


def kernel(**inputs):
    import concourse.bacc as bacc
    from concourse.bass_utils import run_bass_kernel_spmd

    ins, prm_at, const_at = arrays(inputs)
    nc = bacc.Bacc("TRN2", target_bir_lowering=False, num_devices=1)
    A = {k: nc.dram_tensor(f"in_{k}", v.shape, mybir.dt.from_np(v.dtype), kind="ExternalInput").ap() for k, v in ins.items()}
    A["out"] = nc.dram_tensor("out", (SEQ, D), F32, kind="ExternalOutput").ap()
    build(nc, A, prm_at, const_at)
    r = run_bass_kernel_spmd(nc, [{f"in_{k}": v for k, v in ins.items()}], core_ids=[0])
    got = np.asarray(r.results[0]["out"])
    out = np.empty_like(got)
    out[token_order()] = got
    return out.reshape(1, SEQ, D)
```

```python
import math
from contextlib import ExitStack, contextmanager

import numpy as np
import concourse.bass as bass
import concourse.mybir as mybir
from concourse.alu_op_type import AluOpType as ALU

F32 = mybir.dt.float32
I32 = mybir.dt.int32
ACT = mybir.ActivationFunctionType
AX = mybir.AxisListType
ds = bass.ds

P = 128
D = 1024
DK = D // P
GRID_W, ROWS, CB = 64, 8, 16
SEQ, CTX = 512, 256
XT, CT = SEQ // P, CTX // P
AT = XT + CT
EPS = 1e-6
NEG = -1e30
LAM_INIT = 0.8 - 0.6 * math.exp(0.0)
THETA = 10000.0
N_GROUPS, PER_GROUP, D_EXPERT = 4, 8, 512
N_EXPERTS = N_GROUPS * PER_GROUP
CAP = 64
MAX_BLOCKS = 2 * SEQ // CAP + N_EXPERTS
NA_HEADS, NA_D, WIN_R, WIN_C = 16, 32, 8, 16


def token_order():
    return np.arange(SEQ).reshape(ROWS, SEQ // ROWS // CB, CB).transpose(1, 0, 2).reshape(-1)


def per_tile(table):
    n = table.shape[0] // P
    return table.reshape(n, P, -1).transpose(1, 0, 2).reshape(P, -1)


def rope_tables():
    pos = token_order().astype(np.float32)
    f = np.float32
    inv = f(THETA) ** (-np.arange(0, 64, 2, dtype=np.float32) / f(64))
    ang = pos[:, None] * inv[None, :]
    full_c = np.concatenate([np.cos(ang)] * 2, 1)
    full_s = np.concatenate([-np.sin(ang), np.sin(ang)], 1)

    def axial(rot):
        row, col = np.floor(pos / GRID_W).astype(f), (pos % GRID_W).astype(f)
        inv = f(THETA) ** (-np.arange(0, rot // 2, 2, dtype=np.float32) / f(rot // 2))
        ar, ac = row[:, None] * inv, col[:, None] * inv
        c = np.concatenate([np.cos(ar)] * 2 + [np.cos(ac)] * 2, 1)
        s = np.concatenate([-np.sin(ar), np.sin(ar), -np.sin(ac), np.sin(ac)], 1)
        c = np.concatenate([c, np.ones((CTX, rot), f)], 0)
        s = np.concatenate([s, np.zeros((CTX, rot), f)], 0)
        return c.astype(f), s.astype(f)

    return full_c.astype(f), full_s.astype(f), axial(64), axial(32)


def window_masks():
    m = np.zeros((P, 3, 3, CB), np.float32)
    for kind, g in enumerate((0, 1, 3)):
        for q in range(P):
            c = CB * g + q % CB
            start = min(max(c - WIN_C // 2, 0), GRID_W - WIN_C)
            for d in range(3):
                for k in range(CB):
                    kc = CB * (g + d - 1) + k
                    if not start <= kc < start + WIN_C:
                        m[q, kind, d, k] = NEG
    return m


def constants():
    fc, fs, (ac, as_), (mc, ms) = rope_tables()
    select = np.zeros((P, 4, P), np.float32)
    for j in range(2):
        for cond in range(2):
            select[32 * j + cond, 2 * j + cond, :] = 1.0
    fields = dict(
        ident=np.eye(P, dtype=np.float32),
        ones=np.ones((P, P), np.float32),
        before=np.triu(np.ones((P, P), np.float32), 1),
        eps=np.full((P, 1), EPS, np.float32),
        full_cos=per_tile(fc), full_sin=per_tile(fs),
        ax_cos=per_tile(ac), ax_sin=per_tile(as_),
        mla_cos=per_tile(mc), mla_sin=per_tile(ms),
        masks=window_masks().reshape(P, -1),
        select=select.reshape(P, -1),
        prio4=np.tile(np.arange(N_GROUPS, 0, -1, dtype=np.float32), (P, 1)),
        prio8=np.tile(np.arange(PER_GROUP, 0, -1, dtype=np.float32), (P, 1)),
        block_no=np.tile(np.arange(MAX_BLOCKS, dtype=np.float32), (P, 1)),
    )
    return pack(fields)


def slot_table():
    t = np.zeros((MAX_BLOCKS, CAP, 4), np.int32)
    t[:, :, 1] = 2 * (2 * SEQ + np.arange(CAP))
    return t.reshape(-1, 4)


def slot_ids():
    tok = np.arange(XT)[None, :] * P + np.arange(P)[:, None]
    out = np.zeros((P, 2, XT, 2), np.int32)
    for s in range(2):
        out[:, s, :, 0] = 2 * tok
        out[:, s, :, 1] = 2 * (s * SEQ + tok)
    return out.reshape(P, -1)


def half_ids():
    h = np.zeros((P, 2), np.int32)
    h[P // 2:] = 1
    return h


def pack(fields):
    at, n = {}, 0
    for k, v in fields.items():
        at[k] = (n, v.shape[1])
        n += v.shape[1]
    return at, np.concatenate(list(fields.values()), 1)


def columns(v):
    return np.asarray(v).reshape(-1, P).T


def spread(v):
    v = np.asarray(v).reshape(1, -1)
    return np.broadcast_to(v, (P, v.shape[1]))


def parameters(a):
    return pack(dict(
        g_mix=columns(a["g_mix"]), g_ffn=columns(a["g_ffn"]), g_plg=columns(a["g_plg"]),
        l0_norm=columns(a["l0_norm_2"]), l1_norm=columns(a["l1_norm_2"]),
        kv_a_norm=columns(a["l1_kv_a_norm_2"]), q_a_norm=columns(a["l1_q_a_norm_2"]),
        g_sub=columns(a["g_sub"]),
        cond=np.stack([columns(a["c_2"]), columns(a["c_ctx_2"])], 2).reshape(P, -1),
        l0_b=columns(a["l0_b_mod_2"]), l1_b=columns(a["l1_b_mod_2"]),
        g_qa=spread(a["g_qa"]), g_ka=spread(a["g_ka"]),
        g_qb=spread(a["g_qb"]), g_kb=spread(a["g_kb"]),
        lam=spread(np.concatenate([np.asarray(a[n]).reshape(-1) for n in ("lam_q1", "lam_k1", "lam_q2", "lam_k2")])),
        gqa_q=spread(a["l0_q_norm_2"]), gqa_k=spread(a["l0_k_norm_2"]),
        mla_q=spread(a["l1_q_norm_2"]), mla_kn=spread(a["l1_k_nope_norm_2"]), mla_kr=spread(a["l1_k_rope_norm_2"]),
    ))


def wide_parameters(a):
    return dict(l0_b_gate=spread(np.asarray(a["l0_b_mod_2"])[2 * D:]), l1_b_gate=spread(np.asarray(a["l1_b_mod_2"])[2 * D:]),
                g_ple=spread(a["g_ple"]))


@contextmanager
def semaphores(nc, name, start=0, software_dma=(), **sems):
    made = {k: [nc.alloc_semaphore(f"{name}_{k}{'' if n is None else i}") for i in range(n or 1)]
            for k, n in sems.items()}
    if start:
        for k, got in made.items():
            for x in got:
                if k not in software_dma:
                    nc.gpsimd.sem_inc(x, start)
    yield {k: got if sems[k] else got[0] for k, got in made.items()}
    nc.clear_and_free_semaphores([x for got in made.values() for x in got])
    nc.all_engine_barrier(sem_only=True)


@contextmanager
def stage(nc, name, **sems):
    with semaphores(nc, name, **sems) as s:
        with nc.Block() as block:
            yield block, s


class Chain:

    def __init__(self, eng, sem, base=0):
        self.eng, self.sem, self.base, self.n = eng, sem, base, 0

    def __call__(self, ins):
        self.n += 1
        ins.then_inc(self.sem, 1)
        self.eng.wait_ge(self.sem, self.base + self.n)


def loop(eng, n, body):
    if n == 1:
        body(0)
    elif n > 1:
        with eng.Fori(0, n) as i:
            body(i)


def inverse_root(dve, chain, ss, root, n, v, out):
    chain(dve.tensor_scalar(v, ss, 0.5 / n, 0.5 * EPS, ALU.mult, ALU.add))
    chain(dve.reciprocal(out, root))
    chain(dve.tensor_tensor(v, v, out, ALU.mult))
    chain(dve.scalar_tensor_tensor(out=v, in0=root, scalar=0.5, in1=v, op0=ALU.mult, op1=ALU.add))
    return dve.reciprocal(out, v)


def copy(eng, act, out, in_):
    return eng.activation(out, in_, ACT.Copy) if act else eng.tensor_copy(out, in_)


def norm_transpose(nc, name, m, src, K, T, gain, shift, out, spill=None):
    W = K * P
    by_dve = range(T - T // 3, T)

    def of_tile(v, t):
        v = v if len(v.shape) == 2 else v[:, t, :]
        return v.unsqueeze(2).to_broadcast([P, K, P])

    with ExitStack() as c:
        sb = lambda n, s: c.enter_context(nc.sbuf_tensor(f"{name}_{n}", s, F32))
        squares, xn = sb("squares", [P, 2, W]), sb("xn", [P, 2, W])
        ss, sd, rs, half = sb("ss", [P, T]), sb("sd", [P, T]), sb("rs", [P, T]), sb("half", [P, T])
        ps = c.enter_context(nc.psum_tensor(f"{name}_ps", [P, 2, 1024], F32))
        with stage(nc, name, act_chain=None, dve_chain=None, summed=None, sd_done=None, rs_done=None, xn_done=None,
                   turned=None, out_done=None, spilled=2) as (block, s):

            @block.scalar
            def _(act):
                chain = Chain(act, s["act_chain"])
                for t in range(T):
                    if t not in by_dve:
                        chain(act.activation(squares[:, 0], src(t), ACT.Square, accum_out=ss[:, t:t + 1]))
                act.wait_ge(s["summed"], len(by_dve))
                act.activation(sd[:], ss[:], ACT.Sqrt, bias=m["eps"], scale=1.0 / W).then_inc(s["sd_done"], 1)
                act.wait_ge(s["rs_done"], 1)
                for t in range(T):
                    if t >= 2:
                        act.wait_ge(s["turned"], t - 1)
                        if spill is not None:
                            act.wait_ge(s["spilled"][t % 2], 16 * (t // 2))
                    act.activation(xn[:, t % 2], src(t), ACT.Copy, scale=rs[:, t:t + 1]).then_inc(s["xn_done"], 1)

            @block.vector
            def _(dve):
                chain = Chain(dve, s["dve_chain"])
                for t in by_dve:
                    chain(dve.tensor_tensor(squares[:, 1], src(t), src(t), ALU.mult))
                    dve.tensor_reduce(ss[:, t:t + 1], squares[:, 1], AX.X, ALU.add).then_inc(s["summed"], 1)
                    dve.wait_ge(s["summed"], t - by_dve[0] + 1)
                dve.wait_ge(s["sd_done"], 1)
                inverse_root(dve, chain, ss[:], sd[:], W, half[:], rs[:]).then_inc(s["rs_done"], 1)
                for t in range(T):
                    dve.wait_ge(s["turned"], t + 1)
                    o = out[:, :, t * P:(t + 1) * P]
                    v = ps[:, t % 2, 0:W].rearrange("p (k t) -> p k t", k=K)
                    if shift is None:
                        dve.tensor_tensor(o, v, of_tile(gain, t), ALU.mult).then_inc(s["out_done"], 1)
                    else:
                        chain(dve.tensor_tensor(o, v, of_tile(gain, t), ALU.mult))
                        dve.tensor_tensor(o, o, of_tile(shift, t), ALU.add).then_inc(s["out_done"], 1)

            @block.tensor
            def _(pe):
                for t in range(T):
                    pe.wait_ge(s["xn_done"], t + 1)
                    if t >= 2:
                        pe.wait_ge(s["out_done"], t - 1)
                    for k in range(K):
                        last = pe.transpose(ps[:, t % 2, k * P:(k + 1) * P], xn[:, t % 2, k * P:(k + 1) * P], m["ident"])
                    last.then_inc(s["turned"], 1)

            if spill is not None:
                @block.sync
                def _(sp):
                    for t in range(T):
                        sp.wait_ge(s["xn_done"], t + 1)
                        sp.dma_start(spill[t], xn[:, t % 2]).then_inc(s["spilled"][t % 2], 16)
                    for p in range(2):
                        sp.wait_ge(s["spilled"][p], 16 * len(range(p, T, 2)))


def dense(nc, name, lhs, KT, T, w, n_chunks, width, emit, by="both", col0=0, links=0, beside=None):
    parts = 4 if KT % 4 == 0 else 1
    KP = KT // parts
    pairs, NB, H = n_chunks // 2, 4, T // 2
    with ExitStack() as c:
        wb = c.enter_context(nc.sbuf_tensor(f"{name}_w", [P, 2, KT, width], F32))
        tmp = c.enter_context(nc.sbuf_tensor(f"{name}_tmp", [P, 2, width], F32))
        ps = c.enter_context(nc.psum_tensor(f"{name}_ps", [P, NB, 512], F32))
        with stage(nc, name, start=1, loaded=2 * parts, mm=NB, ev=NB, dve_chain=None, act_chain=None) as (block, s):
            src = w.rearrange("(k p) n -> p k n", p=P)

            def after(cp):
                u = cp * T + T - 1
                return u % NB, u // NB + 1

            @block.sync
            def _(sp):
                def load(i, cp):
                    for z in range(parts):
                        sp.dma_start(wb[:, cp, z * KP:(z + 1) * KP], src[:, z * KP:(z + 1) * KP, ds(col0 + (2 * i + cp) * width, width)]).then_inc(
                            s["loaded"][cp * parts + z], 16)

                load(0, 0)
                if n_chunks > 1:
                    load(0, 1)
                if beside is not None:
                    beside["sync"](sp)

                def refill(i, cps):
                    for cp in cps:
                        b, n = after(cp)
                        sp.wait_ge(s["mm"][b], 1 + i * H + n)
                        load(i + 1, cp)
                loop(sp, pairs - 1, lambda i: refill(i, (0, 1)))
                if n_chunks % 2 and pairs:
                    refill(pairs - 1, (0,))

            def over_chunks(eng, body):
                loop(eng, pairs, lambda i: body(i, (0, 1)))
                if n_chunks % 2:
                    body(pairs, (0,))

            @block.tensor
            def _(pe):
                def body(i, cps):
                    for cp in cps:
                        for t in range(T):
                            u = cp * T + t
                            pe.wait_ge(s["ev"][u % NB], 1 + i * H + u // NB)
                            for k in range(KT):
                                if t == 0 and k % KP == 0:
                                    pe.wait_ge(s["loaded"][cp * parts + k // KP], 1 + 16 * (i + 1))
                                last = pe.matmul(ps[:, u % NB, 0:width], lhs(k, t), wb[:, cp, k, :],
                                                 start=(k == 0), stop=(k == KT - 1))
                            last.then_inc(s["mm"][u % NB], 1)
                if beside is not None and "before" in beside:
                    beside["before"](pe)
                over_chunks(pe, body)
                if beside is not None and "after" in beside:
                    beside["after"](pe)

            if beside is not None and "gpsimd" in beside:
                @block.gpsimd
                def _(pool):
                    beside["gpsimd"](pool)

            def emptying(eng, is_act, sem):
                units = [u for u in range(2 * T) if by != "both" or u % 2 == is_act]

                def body(i, cps):
                    chain = Chain(eng, sem, 1 + i * (len(units) * links))
                    for u in units:
                        if u // T not in cps:
                            continue
                        b = u % NB
                        eng.wait_ge(s["mm"][b], 1 + i * H + u // NB + 1)
                        emit(eng, is_act, u % T, 2 * i + u // T, ps[:, b, 0:width], tmp[:, is_act], chain).then_inc(s["ev"][b], 1)
                        if links:
                            eng.wait_ge(s["ev"][b], 1 + i * H + u // NB + 1)
                return body

            @block.vector
            def _(dve):
                if beside is not None:
                    beside["vector"](dve)
                if by != "act":
                    over_chunks(dve, emptying(dve, 0, s["dve_chain"]))

            if by != "dve":
                @block.scalar
                def _(act):
                    if beside is not None:
                        beside["scalar"](act)
                    over_chunks(act, emptying(act, 1, s["act_chain"]))


@contextmanager
def transposed_products(nc, name, act_t, KT, tokens, w, col0, n_chunks, out):
    pieces = [(a, min(512, tokens - a)) for a in range(0, tokens, 512)]
    NB, CW = 4, 512
    buffers = min(2, n_chunks)
    with ExitStack() as c:
        wb = c.enter_context(nc.sbuf_tensor(f"{name}_w", [P, buffers, KT, CW], F32))
        ps = c.enter_context(nc.psum_tensor(f"{name}_ps", [P, NB, 512], F32))
        s = c.enter_context(semaphores(nc, name, loaded=2, mm=NB, ev=NB))
        src = w.rearrange("(k p) n -> p k n", p=P)
        units = [(cc, j, a, n) for cc in range(n_chunks) for j in range(CW // P) for a, n in pieces]
        per_chunk = len(units) // n_chunks

        def sync(sp):
            for cc in range(n_chunks):
                if cc >= 2:
                    u = (cc - 1) * per_chunk - 1
                    sp.wait_ge(s["mm"][u % NB], u // NB + 1)
                sp.dma_start(wb[:, cc % 2], src[:, :, col0 + cc * CW:col0 + (cc + 1) * CW]).then_inc(s["loaded"][cc % 2], 16)

        def tensor(pe):
            for u, (cc, j, a, n) in enumerate(units):
                if u % per_chunk == 0:
                    pe.wait_ge(s["loaded"][cc % 2], 16 * (cc // 2 + 1))
                if u >= NB:
                    pe.wait_ge(s["ev"][u % NB], u // NB)
                for k in range(KT):
                    last = pe.matmul(ps[:, u % NB, 0:n], wb[:, cc % 2, k, j * P:(j + 1) * P], act_t[:, k, a:a + n],
                                     start=(k == 0), stop=(k == KT - 1))
                last.then_inc(s["mm"][u % NB], 1)

        def scalar(act, part, parts):
            for u in range(len(units) * part // parts, len(units) * (part + 1) // parts):
                cc, j, a, n = units[u]
                act.wait_ge(s["mm"][u % NB], u // NB + 1)
                act.activation(out(cc * (CW // P) + j, a, n), ps[:, u % NB, 0:n], ACT.Silu).then_inc(s["ev"][u % NB], 1)

        yield dict(sync=sync, tensor=tensor, scalar=scalar, vector=lambda dve: None)


def head_norms(nc, name, m, T, jobs, beside=None):
    J = len(jobs)
    with ExitStack() as c:
        sb = lambda n, s: c.enter_context(nc.sbuf_tensor(f"{name}_{n}", s, F32))
        sq = [sb(f"sq{j}", [P, H, d]) for j, (_, H, d, _, _) in enumerate(jobs)]
        tw = [sb(f"tw{j}", [P, H, max(1, 2 * r[1] * r[2])]) if r else None for j, (_, H, d, _, r) in enumerate(jobs)]
        st = [sb(f"st{j}", [P, 4, H]) for j, (_, H, _, _, _) in enumerate(jobs)]
        with stage(nc, name, start=1, squared=None, summed=None, rooted=None, scaled=None, turned=None, done=None, dve_chain=None) as (block, s):

            @block.scalar
            def _(act):
                def body(t):
                    for j, (x, H, d, _, _) in enumerate(jobs):
                        act.wait_ge(s["summed"], 1 + t * J + j)
                        act.activation(sq[j][:], x(t), ACT.Square).then_inc(s["squared"], 1)
                    for j, (x, H, d, _, _) in enumerate(jobs):
                        act.wait_ge(s["summed"], 1 + t * J + j + 1)
                        act.wait_ge(s["scaled"], 1 + t * J)
                        act.activation(st[j][:, 1, :], st[j][:, 0, :], ACT.Sqrt, bias=m["eps"], scale=1.0 / d).then_inc(s["rooted"], 1)
                if beside is None:
                    loop(act, T, body)
                else:
                    for t in range(T):
                        body(t)
                        beside["scalar"](act, t, T)

            @block.vector
            def _(dve):
                def body(t):
                    chain = Chain(dve, s["dve_chain"], 1 + t * (5 * J + sum(1 for q in jobs if q[4])))
                    for j in range(J):
                        dve.wait_ge(s["squared"], 1 + t * J + j + 1)
                        dve.wait_ge(s["rooted"], 1 + t * J)
                        dve.tensor_reduce(st[j][:, 0, :], sq[j][:], AX.X, ALU.add).then_inc(s["summed"], 1)
                    for j, (x, H, d, cos, rot) in enumerate(jobs):
                        dve.wait_ge(s["rooted"], 1 + t * J + j + 1)
                        chain(inverse_root(dve, chain, st[j][:, 0, :], st[j][:, 1, :], d, st[j][:, 3, :], st[j][:, 2, :]))
                        dve.tensor_tensor(x(t), x(t), st[j][:, 2, :].unsqueeze(2).to_broadcast([P, H, d]), ALU.mult).then_inc(s["scaled"], 1)
                    turns = 0
                    for j, (x, H, d, cos, rot) in enumerate(jobs):
                        dve.wait_ge(s["scaled"], 1 + t * J + j + 1)
                        if rot:
                            turns += 1
                            dve.wait_ge(s["turned"], 1 + t * sum(1 for q in jobs if q[4]) + turns)
                        cc = cos(t).unsqueeze(1).to_broadcast([P, H, d])
                        if rot:
                            f0, G, w, sin = rot
                            chain(dve.tensor_tensor(x(t), x(t), cc, ALU.mult))
                            xr = x(t)[:, :, f0:f0 + 2 * G * w]
                            dve.tensor_tensor(xr, xr, tw[j][:], ALU.add).then_inc(s["done"], 1)
                        else:
                            dve.tensor_tensor(x(t), x(t), cc, ALU.mult).then_inc(s["done"], 1)
                loop(dve, T, body)
                if beside is not None:
                    beside["vector"](dve)

            @block.gpsimd
            def _(pool):
                def body(t):
                    for j, (x, H, d, cos, rot) in enumerate(jobs):
                        if not rot:
                            continue
                        f0, G, w, sin = rot
                        pool.wait_ge(s["scaled"], 1 + t * J + j + 1)
                        pool.wait_ge(s["done"], 1 + t * J)
                        sw = sin(t).rearrange("p (g a w) -> p g a w", g=G, a=2)
                        for g in range(G):
                            for a in range(2):
                                last = pool.tensor_tensor(
                                    tw[j][:, :, (2 * g + a) * w:(2 * g + a + 1) * w],
                                    x(t)[:, :, f0 + (2 * g + 1 - a) * w:f0 + (2 * g + 2 - a) * w],
                                    sw[:, g, a, :].unsqueeze(1).to_broadcast([P, H, w]), ALU.mult)
                        last.then_inc(s["turned"], 1)
                loop(pool, T, body)

            if beside is not None:
                @block.sync
                def _(sp):
                    beside["sync"](sp)

                @block.tensor
                def _(pe):
                    beside["tensor"](pe)


def attention(nc, name, m, pairs, U, nh, dv, q_src, k_src, v_src, out, gate=None, split=False,
              combine=None, bias=None, spare=None, tiles=XT, ktiles=XT):
    FIRST = 2
    NU = len(U)
    LEAD = 2 * nh - 1 if nh == 2 else 2 * nh - 2
    TURN_AT = NU - 3
    R = split or P
    NS = nh if split else 1
    KT = ktiles
    heads = 1 if combine is not None else nh
    W = 1024 if KT > 4 else 512
    pieces = []
    for _, lo, hi in U:
        n = hi - lo
        pieces.append([list(range(lo, hi))] if n <= 3 and bias is not None else
                      [list(range(lo, lo + (n + 1) // 2)), list(range(lo + (n + 1) // 2, hi))])
    stage_pieces = [(z, x, lo, min(4, n - lo)) for x in range(NS) for z, n in ((0, tiles), (1, KT)) for lo in range(0, n, 4)]

    def bank_uses(last):
        uses = []
        for p in range(2):
            for u in range(NU):
                uses += [("weights", p, u, x, n) for x in range(heads) for n in range(len(pieces[u]))]
                if u == TURN_AT and not (last and p):
                    uses += [("turn", p, k) for k in range(len(stage_pieces))]
        return {x: (n % 2, n // 2) for n, x in enumerate(uses)}
    bank_use = [bank_uses(False), bank_uses(True)]
    per_bank = len(bank_use[0]) // 2
    BASE = FIRST + len(stage_pieces) // 2
    assert len(bank_use[0]) % 2 == 0 and len(stage_pieces) % 2 == 0
    ob = (tiles + 3) // 4
    with ExitStack() as c:
        sb = lambda n, s: c.enter_context(nc.sbuf_tensor(f"{name}_{n}", s, F32))
        qs, ks, vs = sb("qs", [P, 2, NS, tiles, R]), sb("ks", [P, 2, NS, KT, R]), sb("vs", [P, 2, KT, nh * dv if combine is None else dv])
        qT, kT = sb("qT", [P, 2, NS, tiles * P]), sb("kT", [P, 2, nh, KT * P])
        kw = min(KT * P, W) if bias is None else 3 * P
        pr = sb("pr", [P, 2, nh, kw]) if spare is None else spare[:, 2:4, :].rearrange("p b (h k) -> p b h k", h=nh)
        pT = sb("pT", [P, 2, heads, KT, P])
        nm, sm, rc = sb("nm", [P, 2, nh]), sb("sm", [P, 2, nh]), sb("rc", [P, 2, nh])
        S = c.enter_context(nc.psum_tensor(f"{name}_S", [P, 4, 512], F32))
        Tp = c.enter_context(nc.psum_tensor(f"{name}_T", [P, 2, 512], F32))
        O = c.enter_context(nc.psum_tensor(f"{name}_O", [P, 2, 512], F32))
        if bias is not None:
            E = [spare[:, p, :].rearrange("p (h a b) -> p h a b", h=nh, b=3 * CB) for p in range(2)]
            EM = sb("EM", [P, 2, nh, 7, WIN_R * CB])
            em_block = {(0, 1): 0, (0, 2): 1, (1, 0): 2, (1, 1): 3, (1, 2): 4, (2, 0): 5, (2, 1): 6}
        flat = S[:].rearrange("p b n -> p (b n)")

        def scores_of(i, lo, n):
            at = i * W + (lo * P if bias is None else 0)
            return flat[:, at:at + n * P]

        with stage(nc, name, start=FIRST, staged=2, vstaged=2, zeroed=None, scored=4, maxed=4, exped=4, inverted=4,
                   weighted=4, turned=2, emptied=2, pv=2, o_done=None, dve_chain=None, e_in=2, em_done=2,
                   reload=None, lowered=4) as (block, s):

            def count(i, p, u):
                return FIRST + i * (2 * NU) + p * NU + u

            def of_bank(i, last, use):
                bank, n = bank_use[last][use]
                return bank, BASE + i * per_bank + n

            def weights_turned(i, last, p, u, x, bank):
                n = p * NU + u - 2
                table, back = (bank_use[last], 0) if n >= 0 else (bank_use[0], per_bank)
                n %= 2 * NU
                got = [0] + [k + 1 for key, (bk, k) in table.items() if bk == bank and key[0] == "weights" and
                       (key[1] * NU + key[2], 0 if heads < nh else key[3]) <= (n, x)]
                return BASE + i * per_bank - back + max(got)

            def group_turned(i, p, bank):
                got = max(k + 1 for key, (bk, k) in bank_use[0].items() if bk == bank and key[:2] == ("turn", 1 - p))
                return BASE + i * per_bank - (0 if p else per_bank) + got

            def par(p, u):
                n = p * NU + u
                return n % 2, n // 2

            def values_done(i, p, b):
                return FIRST + i * NU + sum(1 for y in range((p + 1) * NU) if y % 2 == b)

            def item_behind(i, last, p, u, x, k):
                n = (p * NU + u) * nh + x + k
                if n < 2 * NU * nh:
                    return i, last, n // (NU * nh), n // nh % NU, n % nh
                n -= 2 * NU * nh
                return None if last else (i + 1, False, 0, n // nh, n % nh)

            def iterations(eng, body):
                loop(eng, pairs - 1, lambda i: body(i, False))
                body(pairs - 1, True)

            @block.gpsimd
            def _(pool):
                if not split:
                    for p in range(2):
                        pool.memset(kT[:, p], 0.0).then_inc(s["zeroed"], 1)

                def bias_blocks(i, p, some, last):
                    pool.wait_ge(s["e_in"][p], FIRST + 16 * ROWS * (i + 1))
                    pool.sem_inc(s["reload"], 1)
                    for x in range(nh if p or type(i) is not int or i else 0):
                        pool.wait_ge(s["maxed"][x], count(i, p, 0) - NU)
                        pool.sem_inc(s["reload"], 1)
                    for kind, d in some:
                        mk = m["masks"].rearrange("p (z d k) -> p z d k", z=3, d=3)[:, kind, d, :]
                        for x in range(nh):
                            ins = pool.tensor_tensor(
                                EM[:, p, x, em_block[kind, d]].rearrange("p (r k) -> p r k", r=WIN_R), E[p][:, x, :, d * CB:(d + 1) * CB],
                                mk.unsqueeze(1).to_broadcast([P, WIN_R, CB]), ALU.add)
                    if last:
                        ins.then_inc(s["em_done"][p], 1)
                blocks = list(em_block) if bias is not None else []
                parts = [blocks[0:3], blocks[3:5], blocks[5:7]]
                if bias is not None:
                    bias_blocks(0, 0, blocks, True)

                def body(i, last):
                    for p in range(2):
                        for u, (t, lo, hi) in enumerate(U):
                            b, before = par(p, u)
                            for x in range(nh):
                                pool.wait_ge(s["inverted"][x], count(i, p, u) + 1)
                                if combine is not None and x == 0:
                                    continue
                                w = pr[:, b, x, 0:(hi - lo) * P]
                                pool.tensor_tensor(w, w, rc[:, b, x:x + 1].to_broadcast([P, (hi - lo) * P]), ALU.mult).then_inc(s["weighted"][x], 1)
                            if bias is not None and u < 3 and not (last and p):
                                bias_blocks(i + p, 1 - p, parts[u], u == 2)
                iterations(pool, body)

            @block.sync
            def _(sp):
                def load_qk(i, p):
                    for dst, src in q_src(i, p, qs[:, p]) + k_src(i, p, ks[:, p]):
                        sp.dma_start(dst, src).then_inc(s["staged"][p], 16)

                def load_v(i, p):
                    for dst, src in v_src(i, p, vs[:, p]):
                        sp.dma_start(dst, src).then_inc(s["vstaged"][p], 16)
                    if bias is not None:
                        for r in range(ROWS):
                            sp.dma_start(E[p][r * CB:(r + 1) * CB].rearrange("q h a b -> q h (a b)"),
                                         bias[:, ds((2 * i + p) * nh, nh), (7 - r) * 48:(15 - r) * 48]).then_inc(s["e_in"][p], 16)

                def wait(sem, n):
                    sp.wait_ge(sem, n)
                    sp.sem_inc(s["reload"], 1)

                def refill(i, last):
                    for p in range(2):
                        if p == 0:
                            for b in range(2):
                                wait(s["turned"][b], group_turned(i, 1, b))
                            load_qk(i + 1, 1)
                        elif not last:
                            for b in range(2):
                                wait(s["turned"][b], group_turned(i + 1, 0, b))
                            load_qk(i + 2, 0)
                        for b in range(2):
                            wait(s["pv"][b], values_done(i, p, b))
                        if bias is not None:
                            wait(s["em_done"][p], FIRST + i + 1)
                        load_v(i + 1, p)
                for p in range(2):
                    load_qk(0, p)
                    load_v(0, p)
                for b in range(2):
                    sp.wait_ge(s["turned"][b], BASE)
                load_qk(1, 0)
                loop(sp, pairs - 2, lambda i: refill(i, False))
                refill(pairs - 2, True)

            n_staged = [len(q_src(0, p, qs[:, p])) + len(k_src(0, p, ks[:, p])) for p in range(2)]
            n_v = [len(v_src(0, p, vs[:, p])) for p in range(2)]

            @block.tensor
            def _(pe):
                def scores(i, last, p, u, x, first=False):
                    t, lo, hi = U[u]
                    if u == 0 and x == 0:
                        for b in range(2):
                            pe.wait_ge(s["emptied"][b], BASE if first else group_turned(i, p, b))
                    pe.wait_ge(s["exped"][x] if bias is None else s["maxed"][x], count(i, p, u))
                    qq = x if split else 0
                    cuts = [(a, min(hi, a + 4 - a % 4)) for a in ([lo] + [4] * (lo < 4 < hi))] if bias is None else [(lo, hi)]
                    for a, e in cuts:
                        at = x * W + (a * P if bias is None else 0)
                        ins = pe.matmul(flat[:, at:at + (e - a) * P], qT[0:R, p, qq, t * P:(t + 1) * P],
                                        kT[0:R, p, x, a * P:e * P], start=True, stop=True)
                    ins.then_inc(s["scored"][x], 1)

                def turn(i, last, p, u, x):
                    t, lo, hi = U[u]
                    b, before = par(p, u)
                    pe.wait_ge(s["weighted"][x], count(i, p, u) + 1)
                    for n, kts in enumerate(pieces[u]):
                        bank, n_before = of_bank(i, last, ("weights", p, u, x, n))
                        pe.wait_ge(s["emptied"][bank], n_before)
                        for z, kt in enumerate(kts):
                            ins = pe.transpose(Tp[:, bank, z * P:(z + 1) * P], pr[:, b, x, (kt - lo) * P:(kt - lo + 1) * P], m["ident"])
                        ins.then_inc(s["turned"][bank], 1)

                def turn_group(i, p, place):
                    pe.wait_ge(s["staged"][p], FIRST + 16 * n_staged[p] * (i + 1))
                    for k, (z, x, lo, n) in enumerate(stage_pieces):
                        bank, n_before = place(k)
                        pe.wait_ge(s["emptied"][bank], n_before)
                        for t in range(n):
                            ins = pe.transpose(Tp[0:R, bank, t * P:(t + 1) * P], (ks if z else qs)[:, p, x, lo + t, :], m["ident"])
                        ins.then_inc(s["turned"][bank], 1)

                def values(i, last, p, u):
                    t, lo, hi = U[u]
                    b, before = par(p, u)
                    for bank in range(2):
                        mine = [use for x in range(heads) for n in range(len(pieces[u]))
                                for bk, use in [of_bank(i, last, ("weights", p, u, x, n))] if bk == bank]
                        if mine:
                            pe.wait_ge(s["emptied"][bank], mine[-1] + 1)
                    if u == 0:
                        pe.wait_ge(s["vstaged"][p], FIRST + 16 * n_v[p] * (i + 1))
                        pe.wait_ge(s["o_done"], FIRST + 2 * i + p - (1 if ob == 1 else 0))
                    for kt in range(lo, hi):
                        for x in range(heads):
                            v = vs[:, p, kt, x * dv:(x + 1) * dv]
                            ins = pe.matmul(O[x * dv:(x + 1) * dv, p if ob == 1 else t // 4, (t % 4) * P:(t % 4 + 1) * P], v, pT[:, b, x, kt, :],
                                            start=(kt == lo), stop=(kt == hi - 1))
                    ins.then_inc(s["pv"][b], 1)

                turn_group(0, 0, lambda k: (k % 2, FIRST + k // 2))
                for k in range(LEAD):
                    scores(0, False, 0, k // nh, k % nh, first=True)

                def body(i, last):
                    for p in range(2):
                        for u in range(NU):
                            for x in range(nh):
                                if heads == nh:
                                    turn(i, last, p, u, x)
                                ahead = item_behind(i, last, p, u, x, LEAD)
                                if ahead:
                                    scores(*ahead)
                                if heads < nh and x == 0:
                                    turn(i, last, p, u, 0)
                            if u == TURN_AT and not (last and p):
                                turn_group(i + p, 1 - p, lambda k: of_bank(i, last, ("turn", p, k)))
                            values(i, last, p, u)
                iterations(pe, body)

            def empty_weights(eng, act, i, last, p, u, x):
                b, before = par(p, u)
                for n, kts in enumerate(pieces[u]):
                    bank, n_before = of_bank(i, last, ("weights", p, u, x, n))
                    if bank != act:
                        continue
                    eng.wait_ge(s["turned"][bank], n_before + 1)
                    eng.wait_ge(s["pv"][b], FIRST + i * NU + before)
                    copy(eng, act, pT[:, b, x, kts[0]:kts[-1] + 1, :],
                         Tp[:, bank, 0:len(kts) * P].rearrange("p (k q) -> p k q", q=P)).then_inc(s["emptied"][bank], 1)

            def empty_group(eng, act, p, place):
                for k, (z, x, lo, n) in enumerate(stage_pieces):
                    bank, n_before = place(k)
                    if bank != act:
                        continue
                    eng.wait_ge(s["turned"][bank], n_before + 1)
                    if z and not split:
                        for h in range(nh):
                            rows = slice(h * (P // nh), (h + 1) * (P // nh))
                            ins = copy(eng, act, kT[rows, p, h, lo * P:(lo + n) * P], Tp[rows, bank, 0:n * P])
                    else:
                        ins = copy(eng, act, (kT if z else qT)[0:R, p, x, lo * P:(lo + n) * P], Tp[0:R, bank, 0:n * P])
                    ins.then_inc(s["emptied"][bank], 1)

            def highest(dve, i, last, p, u, x, first=False):
                t, lo, hi = U[u]
                b, before = par(p, u)
                n = hi - lo
                dve.wait_ge(s["scored"][x], count(i, p, u) + 1)
                dve.wait_ge(s["exped"][x], count(i, p, u))
                if bias is None:
                    dve.tensor_reduce(nm[:, b, x:x + 1], scores_of(x, lo, n), AX.X, ALU.max, negate=True).then_inc(s["maxed"][x], 1)
                else:
                    kind = min(u, 1) if u < 3 else 2
                    dve.wait_ge(s["em_done"][p], FIRST + i + 1)
                    if not first:
                        for bank in range(2):
                            dve.wait_ge(s["turned"][bank], weights_turned(i, last, p, u, x, bank))
                    at = em_block[kind, lo - t + 1]
                    dve.tensor_tensor(pr[:, b, x, 0:n * P], scores_of(x, 0, n),
                                      EM[:, p, x, at:at + n].rearrange("p d k -> p (d k)"), ALU.add).then_inc(s["maxed"][x], 1)
                    dve.wait_ge(s["maxed"][x], count(i, p, u) + 1)
                    dve.tensor_reduce(nm[:, b, x:x + 1], pr[:, b, x, 0:n * P], AX.X, ALU.max, negate=True).then_inc(s["lowered"][x], 1)

            def invert(dve, i, last, p, u, x, chain):
                b, before = par(p, u)
                dve.wait_ge(s["exped"][x], count(i, p, u) + 1)
                if combine is not None and x == 1:
                    chain(dve.reciprocal(rc[:, b, 1:2], sm[:, b, 1:2]))
                    dve.tensor_scalar(rc[:, b, 1:2], rc[:, b, 1:2], combine, None, ALU.mult).then_inc(s["inverted"][1], 1)
                else:
                    dve.reciprocal(rc[:, b, x:x + 1], sm[:, b, x:x + 1]).then_inc(s["inverted"][x], 1)

            @block.vector
            def _(dve):
                if not split:
                    dve.wait_ge(s["zeroed"], FIRST + 2)
                empty_group(dve, 0, 0, lambda k: (k % 2, FIRST + k // 2))
                before_loop = Chain(dve, s["dve_chain"], FIRST)
                for k in range(LEAD):
                    highest(dve, 0, False, 0, k // nh, k % nh, first=True)
                    if k > 0:
                        invert(dve, 0, False, 0, (k - 1) // nh, (k - 1) % nh, before_loop)

                def body(i, last):
                    chain = Chain(dve, s["dve_chain"], FIRST + before_loop.n + i * 2 * NU)
                    for p in range(2):
                        for u in range(NU):
                            if combine is not None:
                                t, lo, hi = U[u]
                                b, before = par(p, u)
                                dve.wait_ge(s["weighted"][1], count(i, p, u) + 1)
                                dve.wait_ge(s["inverted"][0], count(i, p, u) + 1)
                                w0, w1 = pr[:, b, 0, 0:(hi - lo) * P], pr[:, b, 1, 0:(hi - lo) * P]
                                dve.scalar_tensor_tensor(out=w0, in0=w0, scalar=rc[:, b, 0:1], in1=w1, op0=ALU.mult,
                                                         op1=ALU.add).then_inc(s["weighted"][0], 1)
                            for x in range(nh):
                                if heads == nh:
                                    empty_weights(dve, 0, i, last, p, u, x)
                                ahead = item_behind(i, last, p, u, x, LEAD)
                                if ahead:
                                    highest(dve, *ahead)
                                ahead = item_behind(i, last, p, u, x, LEAD - 1)
                                if ahead:
                                    invert(dve, *ahead, chain)
                                if heads < nh and x == 0:
                                    empty_weights(dve, 0, i, last, p, u, 0)
                            if u == TURN_AT and not (last and p):
                                empty_group(dve, 0, 1 - p, lambda k: of_bank(i, last, ("turn", p, k)))
                        for b in range(2):
                            dve.wait_ge(s["pv"][b], values_done(i, p, b))
                        o = out(i, p)
                        for bk in range(ob):
                            n = min(4, tiles - 4 * bk) * P
                            dst, src = o[:, bk * 512:bk * 512 + n], O[:, p if ob == 1 else bk, 0:n]
                            if gate is None:
                                ins = dve.tensor_copy(dst, src)
                            else:
                                ins = dve.tensor_tensor(dst, src, dst, ALU.mult)
                        ins.then_inc(s["o_done"], 1)
                iterations(dve, body)

            @block.scalar
            def _(act):
                def exponential(i, last, p, u, x, first=False):
                    t, lo, hi = U[u]
                    b, before = par(p, u)
                    act.wait_ge(s["maxed"][x] if bias is None else s["lowered"][x], count(i, p, u) + 1)
                    if bias is None:
                        if not first:
                            act.wait_ge(s["turned"][0], weights_turned(i, last, p, u, x, 0))
                            act.wait_ge(s["turned"][1], weights_turned(i, last, p, u, x, 1))
                        src = scores_of(x, lo, hi - lo)
                    else:
                        src = pr[:, b, x, 0:(hi - lo) * P]
                    act.activation(pr[:, b, x, 0:(hi - lo) * P], src, ACT.Exp, bias=nm[:, b, x:x + 1],
                                   accum_out=sm[:, b, x:x + 1]).then_inc(s["exped"][x], 1)

                if not split:
                    act.wait_ge(s["zeroed"], FIRST + 2)
                empty_group(act, 1, 0, lambda k: (k % 2, FIRST + k // 2))
                for k in range(LEAD):
                    exponential(0, False, 0, k // nh, k % nh, first=True)

                def body(i, last):
                    for p in range(2):
                        for u in range(NU):
                            for x in range(nh):
                                if heads == nh:
                                    empty_weights(act, 1, i, last, p, u, x)
                                ahead = item_behind(i, last, p, u, x, LEAD)
                                if ahead:
                                    exponential(*ahead)
                                if heads < nh and x == 0:
                                    empty_weights(act, 1, i, last, p, u, 0)
                            if u == TURN_AT and not (last and p):
                                empty_group(act, 1, 1 - p, lambda k: of_bank(i, last, ("turn", p, k)))
                iterations(act, body)


@contextmanager
def preparations(nc, name, m, rpb, table, neg_lam, jobs):
    half = NA_HEADS // 2
    q = half * (2 * WIN_R - 1)
    wide = 4 * CB - 1
    with ExitStack() as c:
        pad = c.enter_context(nc.sbuf_tensor(f"{name}_pad", [P, 2, wide], F32))
        prod = c.enter_context(nc.sbuf_tensor(f"{name}_prod", [P, 2, 64], F32))
        dots = c.enter_context(nc.sbuf_tensor(f"{name}_dots", [P, 2], F32))
        s = c.enter_context(semaphores(nc, name, zero=None, loaded=None, stored=None, dots=None, exped=None, chain=None))

        def sync(sp):
            sp.wait_ge(s["zero"], 1)
            sp.dma_start(pad[0:q, :, CB:CB + 2 * WIN_C - 1], rpb.rearrange("(a h) r c -> (h r) a c", a=2)).then_inc(s["loaded"], 16)
            sp.wait_ge(s["loaded"], 16)
            for cc in range(CB):
                sp.dma_start(table[cc].rearrange("(a h) (r c) -> (h r) a c", a=2, c=3 * CB),
                             pad[0:q, :, CB - 1 - cc:CB - 1 - cc + 3 * CB]).then_inc(s["stored"], 16)
            sp.wait_ge(s["stored"], 16 * CB)

        def scalar(act):
            act.wait_ge(s["dots"], 1)
            act.activation(dots[:], dots[:], ACT.Exp).then_inc(s["exped"], 1)

        def vector(dve):
            dve.memset(pad[:], 0.0).then_inc(s["zero"], 1)
            chain = Chain(dve, s["chain"])
            v = m["lam"].rearrange("p (a b d) -> p a b d", a=2, b=2)
            chain(dve.tensor_tensor(prod[:], v[:, :, 0], v[:, :, 1], ALU.mult))
            dve.tensor_reduce(dots[:], prod[:], AX.X, ALU.add).then_inc(s["dots"], 1)
            for out, in_, vec, swap, factor in jobs:
                n, w = in_.shape[1], in_.shape[2]
                if swap is None:
                    chain(dve.tensor_tensor(out, in_, vec.unsqueeze(1).to_broadcast([P, n, w]), ALU.mult))
                else:
                    h = w // (2 * swap)
                    for g in range(swap):
                        for a in range(2):
                            at, of = (2 * g + a) * h, (2 * g + 1 - a) * h
                            chain(dve.tensor_tensor(out[:, :, at:at + h], in_[:, :, at:at + h],
                                                    vec[:, of:of + h].unsqueeze(1).to_broadcast([P, n, h]), ALU.mult))
                if factor != 1.0:
                    chain(dve.tensor_scalar(out, out, factor, None, ALU.mult))
            dve.wait_ge(s["exped"], 1)
            chain(dve.tensor_tensor(neg_lam, dots[:, 1:2], dots[:, 0:1], ALU.subtract))
            chain(dve.tensor_scalar(neg_lam, neg_lam, -LAM_INIT, None, ALU.add))

        yield dict(sync=sync, scalar=scalar, vector=vector)


@contextmanager
def modulations(nc, name, m, layers):
    NC = 3 * D // 1024
    NL = len(layers)
    with ExitStack() as c:
        sb = lambda n, s: c.enter_context(nc.sbuf_tensor(f"{name}_{n}", s, F32))
        wb = sb("w", [P, 2, DK // 2, 1024])
        sc = sb("silu", [P, DK, 2])
        rows = sb("rows", [P, 2 * NL, 512])
        cols, bg = sb("cols", [P, 4, P]), sb("bg", [P, NL, D])
        ps = c.enter_context(nc.psum_tensor(f"{name}_ps", [P, 2 * NL, 512], F32))
        pt = c.enter_context(nc.psum_tensor(f"{name}_pt", [P, 512], F32))
        pg = c.enter_context(nc.psum_tensor(f"{name}_pg", [P, 2, 512], F32))
        s = c.enter_context(semaphores(nc, name, loaded=2, silu=None, mm=None, zeroed=None, rows_done=None,
                                       turned=None, spread=None, added=None, chain=None, bg=None))

        def sync(sp):
            for l, (w, _, b_gate, *_) in enumerate(layers):
                sp.dma_start(bg[:, l], b_gate).then_inc(s["bg"], 16)
                for x in range(NC):
                    for z in range(2):
                        if l * NC + x:
                            sp.wait_ge(s["mm"], 2 * (l * NC + x) + z - 1)
                        sp.dma_start(wb[:, z], w.rearrange("(z k p) n -> p z k n", p=P, z=2)[:, z, :, x * 1024:(x + 1) * 1024]).then_inc(s["loaded"][z], 16)

        def scalar(act, part, parts):
            if part == 0:
                act.activation(sc[:], m["cond"].rearrange("p (k c) -> p k c", c=2), ACT.Silu).then_inc(s["silu"], 1)

        def tensor(pe):
            pe.wait_ge(s["silu"], 1)
            for n in range(NL * NC):
                l, x = n // NC, n % NC
                for z in range(2):
                    pe.wait_ge(s["loaded"][z], 16 * (n + 1))
                    for k in range(DK // 2):
                        for y in range(2):
                            j = (2 * x + y) % 4
                            last = pe.matmul(ps[32 * j:32 * j + 2, 2 * l + x // 2, :], sc[:, z * (DK // 2) + k, :], wb[:, z, k, y * 512:(y + 1) * 512],
                                             start=(z == 0 and k == 0), stop=(z == 1 and k == DK // 2 - 1))
                    last.then_inc(s["mm"], 1)
            adds = 0
            for l, (_, _, _, _, _, _, _, conds) in enumerate(layers):
                pe.wait_ge(s["rows_done"], 6 * NL)
                if l:
                    pe.wait_ge(s["chain"], 1)
                for b in range(4):
                    last = pe.transpose(pt[:, b * P:(b + 1) * P], rows[:, 2 * l, b * P:(b + 1) * P], m["ident"])
                last.then_inc(s["turned"], 1)
                for j in range(2):
                    if adds:
                        pe.wait_ge(s["added"], adds)
                    for x in range(conds):
                        last = pe.matmul(pg[:, x, :], m["select"].rearrange("p (j q) -> p j q", q=P)[:, 2 * j + x, :], rows[:, 2 * l + 1, :],
                                         start=True, stop=True)
                    last.then_inc(s["spread"], 1)
                    adds += conds

        def vector(dve):
            chain = Chain(dve, s["chain"])
            dve.memset(rows[:], 0.0).then_inc(s["zeroed"], 1)
            dve.wait_ge(s["zeroed"], 1)
            for n in range(NL * NC):
                l, x = n // NC, n % NC
                dve.wait_ge(s["mm"], 2 * (n + 1))
                for y in range(2):
                    j = (2 * x + y) % 4
                    dve.tensor_copy(rows[32 * j:32 * j + 2, 2 * l + x // 2, :], ps[32 * j:32 * j + 2, 2 * l + x // 2, :]).then_inc(s["rows_done"], 1)
            spreads = 0
            for l, (_, b_cols, _, norm, gain, shift, gate, conds) in enumerate(layers):
                dve.wait_ge(s["turned"], l + 1)
                chain(dve.tensor_copy(cols[:], pt[:].rearrange("p (b q) -> p b q", q=P)))
                for half in range(2):
                    for x, t, n in ((0, 0, XT), (1, XT, CT)):
                        spread = lambda v: v.unsqueeze(1).to_broadcast([P, n, 4])
                        sh, g = (v[:, t:t + n, half * 4:half * 4 + 4] for v in (shift, gain))
                        first, first_scale = cols[:, :, 32 * half + x], cols[:, :, 32 * (2 + half) + x]
                        chain(dve.tensor_tensor(sh, spread(first), spread(b_cols[:, half * 4:half * 4 + 4]), ALU.add))
                        chain(dve.tensor_tensor(g, spread(first_scale), spread(b_cols[:, DK + half * 4:DK + half * 4 + 4]), ALU.add))
                        chain(dve.scalar_tensor_tensor(out=g, in0=g, scalar=1.0, in1=spread(norm[:, half * 4:half * 4 + 4]), op0=ALU.add, op1=ALU.mult))
                dve.wait_ge(s["bg"], 16 * NL)
                for j in range(2):
                    spreads += 1
                    dve.wait_ge(s["spread"], spreads)
                    for x in range(conds):
                        dve.tensor_tensor(gate[:, x, j * 512:(j + 1) * 512], pg[:, x, :], bg[:, l, j * 512:(j + 1) * 512], ALU.add).then_inc(s["added"], 1)
            dve.wait_ge(s["added"], sum(2 * layer[-1] for layer in layers))

        yield dict(sync=sync, tensor=tensor, scalar=scalar, vector=vector)


def first_of(dve, chain, out, x, top, prio, best):
    shape = list(x.shape)
    chain(dve.tensor_tensor(out, x, top.unsqueeze(2).to_broadcast(shape), ALU.is_equal))
    chain(dve.tensor_tensor(out, out, prio.unsqueeze(1).to_broadcast(shape), ALU.mult))
    chain(dve.tensor_reduce(best, out, AX.X, ALU.max))
    chain(dve.tensor_tensor(out, out, best.unsqueeze(2).to_broadcast(shape), ALU.is_equal))


@contextmanager
def route(nc, name, m, act_t, w_router, slots_init, slot_ids_dram, slots, block_expert, n_pairs, also):
    NL = N_GROUPS + N_EXPERTS
    with ExitStack() as c:
        sb = lambda n, s, dt=F32: c.enter_context(nc.sbuf_tensor(f"{name}_{n}", s, dt))
        wr, L = sb("wr", [P, DK, NL]), sb("L", [P, XT, NL])
        top_g, best, sum_g = sb("top_g", [P, XT]), sb("best", [P, XT]), sb("sum_g", [P, XT])
        G, z = sb("G", [P, XT, N_GROUPS]), sb("z", [P, XT, N_GROUPS])
        picked = sb("picked", [P, XT, N_GROUPS, PER_GROUP])
        el = sb("el", [P, XT, PER_GROUP])
        E = sb("E", [P, 2, XT, PER_GROUP])
        top_e = sb("top_e", [P, 2, XT])
        ratio, wt = sb("ratio", [P, XT]), sb("wt", [P, 2, XT])
        O = sb("O", [P, 2, XT, N_GROUPS, PER_GROUP])
        A = sb("A", [P, XT, N_EXPERTS])
        pos, dest = sb("pos", [P, XT, N_EXPERTS]), sb("dest", [P, 2, XT])
        dest_i = sb("dest_i", [P, 2, XT], I32)
        rows = sb("rows", [P, 2, XT, 4], I32)
        ids = sb("ids", [P, 2, XT, 2], I32)
        cnt, nb, upto, start, one = (sb(x, [P, N_EXPERTS]) for x in ("cnt", "nb", "upto", "start", "one"))
        cmp, be = sb("cmp", [P, MAX_BLOCKS, N_EXPERTS]), sb("be", [P, MAX_BLOCKS])
        pl = c.enter_context(nc.psum_tensor(f"{name}_pl", [P, XT, P], F32))
        pk = c.enter_context(nc.psum_tensor(f"{name}_pk", [P, 8, N_EXPERTS], F32))
        with semaphores(nc, name, loaded=None, also=None, logits=None, chosen=None, ranked=None, chain=None, low=None, exped=None,
                   init=None, table=None, put=None) as s:
            def sync(sp):
                sp.dma_start(*also).then_inc(s["also"], 16)
                sp.dma_start(slots, slots_init).then_inc(s["init"], 16)
                sp.dma_start(wr[:], w_router.rearrange("(k p) n -> p k n", p=P)).then_inc(s["loaded"], 16)
                sp.dma_start(ids[:].rearrange("p a b c -> p (a b c)"), slot_ids_dram).then_inc(s["loaded"], 16)

            def before(pe):
                pe.wait_ge(s["loaded"], 32)
                for t in range(XT):
                    for k in range(DK):
                        last = pe.matmul(pl[:, t, 0:NL], act_t[:, k, t * P:(t + 1) * P], wr[:, k, :], start=(k == 0), stop=(k == DK - 1))
                last.then_inc(s["logits"], 1)
                pe.wait_ge(s["also"], 16)

            def after(pe):
                pe.wait_ge(s["chosen"], 1)
                for t in range(XT + 1):
                    for b in range(t + (t < XT)):
                        last = pe.matmul(pk[:, t, :], m["before"] if b == t else m["ones"], A[:, b, :], start=(b == 0),
                                         stop=(b == t + (t < XT) - 1))
                last.then_inc(s["ranked"], 1)

            def scalar(act):
                act.wait_ge(s["low"], 1)
                act.activation(z[:], z[:], ACT.Exp).then_inc(s["exped"], 1)
                act.wait_ge(s["low"], 2)
                act.activation(ratio[:], ratio[:], ACT.Exp).then_inc(s["exped"], 1)

            def vector(dve):
                chain = Chain(dve, s["chain"])
                dve.wait_ge(s["logits"], 1)
                chain(dve.tensor_copy(L[:], pl[:, :, 0:NL]))
                LG, LE = L[:, :, 0:N_GROUPS], L[:, :, N_GROUPS:NL].rearrange("p t (g e) -> p t g e", g=N_GROUPS)
                chain(dve.tensor_reduce(top_g[:], LG, AX.X, ALU.max))
                dve.tensor_tensor(z[:], LG, top_g[:].unsqueeze(2).to_broadcast([P, XT, N_GROUPS]), ALU.subtract).then_inc(s["low"], 1)
                first_of(dve, chain, G[:], LG, top_g[:], m["prio4"], best[:])
                chain(dve.tensor_tensor(picked[:], LE, G[:].unsqueeze(3).to_broadcast([P, XT, N_GROUPS, PER_GROUP]), ALU.mult))
                chain(dve.tensor_reduce(el[:], picked[:].rearrange("p t g e -> p t e g"), AX.X, ALU.add))
                for x in range(2):
                    chain(dve.tensor_reduce(top_e[:, x], el[:], AX.X, ALU.max))
                    first_of(dve, chain, E[:, x], el[:], top_e[:, x], m["prio8"], best[:])
                    if x == 0:
                        chain(dve.scalar_tensor_tensor(out=el[:], in0=E[:, 0], scalar=NEG, in1=el[:], op0=ALU.mult, op1=ALU.add))
                dve.tensor_tensor(ratio[:], top_e[:, 1], top_e[:, 0], ALU.subtract).then_inc(s["low"], 1)
                for x in range(2):
                    chain(dve.tensor_tensor(O[:, x], G[:].unsqueeze(3).to_broadcast([P, XT, N_GROUPS, PER_GROUP]),
                                            E[:, x].unsqueeze(2).to_broadcast([P, XT, N_GROUPS, PER_GROUP]), ALU.mult))
                flat = lambda v: v.rearrange("p t g e -> p t (g e)")
                dve.tensor_tensor(A[:], flat(O[:, 0]), flat(O[:, 1]), ALU.add).then_inc(s["chosen"], 1)
                dve.wait_ge(s["exped"], 1)
                chain(dve.tensor_reduce(sum_g[:], z[:], AX.X, ALU.add))
                dve.wait_ge(s["exped"], 2)
                chain(dve.tensor_scalar(wt[:, 1], ratio[:], 1.0, None, ALU.add))
                chain(dve.tensor_tensor(wt[:, 1], wt[:, 1], sum_g[:], ALU.mult))
                chain(dve.reciprocal(wt[:, 0], wt[:, 1]))
                chain(dve.tensor_tensor(wt[:, 1], wt[:, 0], ratio[:], ALU.mult))
                chain(dve.memset(one[:], 1.0))
                chain(dve.memset(rows[:], 0))
                chain(dve.tensor_copy(rows[:, :, :, 0:2], ids[:]))
                chain(dve.tensor_copy(rows[:].bitcast(F32)[:, :, :, 2], wt[:]))
                dve.wait_ge(s["ranked"], 1)
                chain(dve.tensor_copy(cnt[:], pk[:, XT, :]))
                chain(dve.tensor_scalar(nb[:], cnt[:], 0.0, None, ALU.is_gt))
                for b in range(1, SEQ // CAP):
                    chain(dve.scalar_tensor_tensor(out=nb[:], in0=cnt[:], scalar=float(b * CAP), in1=nb[:], op0=ALU.is_gt, op1=ALU.add))
                chain(dve.tensor_tensor_scan(upto[:], one[:], nb[:], 0.0, ALU.mult, ALU.add))
                chain(dve.tensor_tensor(start[:], upto[:], nb[:], ALU.subtract))
                chain(dve.tensor_scalar(start[:], start[:], float(CAP), None, ALU.mult))
                chain(dve.tensor_tensor(pos[:], pk[:, 0:XT, :], start[:].unsqueeze(1).to_broadcast([P, XT, N_EXPERTS]), ALU.add))
                for x in range(2):
                    chain(dve.tensor_tensor(A[:], flat(O[:, x]), pos[:], ALU.mult))
                    chain(dve.tensor_reduce(dest[:, x], A[:], AX.X, ALU.add))
                chain(dve.tensor_copy(dest_i[:], dest[:]))
                chain(dve.tensor_tensor(cmp[:], upto[:].unsqueeze(1).to_broadcast([P, MAX_BLOCKS, N_EXPERTS]),
                                        m["block_no"].unsqueeze(2).to_broadcast([P, MAX_BLOCKS, N_EXPERTS]), ALU.is_le))
                chain(dve.tensor_reduce(be[:], cmp[:], AX.X, ALU.add))
                chain(dve.tensor_scalar(be[:], be[:], float(N_EXPERTS - 1), None, ALU.min))
                chain(dve.tensor_copy(block_expert, be[0:1, :]))
                even = m["block_no"].rearrange("p (i a) -> p i a", a=2)[:, :, 0]
                total = upto[:, N_EXPERTS - 1:N_EXPERTS]
                chain(dve.tensor_tensor(be[:, 0:MAX_BLOCKS // 2], even, total.to_broadcast([P, MAX_BLOCKS // 2]), ALU.is_lt))
                chain(dve.tensor_reduce(total, be[:, 0:MAX_BLOCKS // 2], AX.X, ALU.add))
                dve.tensor_copy(n_pairs, total[0:1]).then_inc(s["table"], 1)

            def gpsimd(pool):
                pool.wait_ge(s["init"], 16)
                pool.wait_ge(s["table"], 1)
                for n in range(2 * XT):
                    pool.indirect_dma_start(out=slots, out_offset=bass.IndirectOffsetOnAxis(ap=dest_i[:, n // XT, n % XT:n % XT + 1], axis=0),
                                            in_=rows[:, n // XT, n % XT, :], in_offset=None).then_inc(s["put"], 16)
                    pool.wait_ge(s["put"], 16 * (n + 1))

            yield dict(sync=sync, before=before, after=after, scalar=scalar, vector=vector, gpsimd=gpsimd)


def expert_blocks(nc, name, m, block_expert, n_pairs, slots, halves, xn, w1, w3, w2, ys):
    H2 = D_EXPERT // 2
    FK = D_EXPERT // P
    FIRST = 2
    TB = MAX_BLOCKS + 2
    with ExitStack() as c:
        sb = lambda n, s, dt=F32: c.enter_context(nc.sbuf_tensor(f"{name}_{n}", s, dt))
        w1b, w3b, w2b = sb("w1", [P, 2, DK, D_EXPERT]), sb("w3", [P, 2, DK, D_EXPERT]), sb("w2", [P, 2, FK, D])
        meta, index = sb("meta", [P, TB, 4], I32), sb("index", [P, 2, TB], I32)
        xg, xT = sb("xg", [P, 2, D // 2]), sb("xT", [P, 4, P])
        sact, hid, hT, yb = sb("silu", [P, H2]), sb("hid", [P, H2]), sb("hT", [P, 2, P]), sb("y", [P, 2, D // 2])
        hv, current = sb("halves", [P, 2], I32), sb("current", [P, 2, 2], I32)
        bank = lambda n: c.enter_context(nc.psum_tensor(f"{name}_{n}", [P, 512], F32))
        px, p1, p3, ph, py = bank("px"), bank("p1"), bank("p3"), bank("ph"), bank("py")
        x_rows = xn.rearrange("t (a d) -> (t a) d", a=2)
        y_rows = ys.rearrange("t (a d) -> (t a) d", a=2)
        with stage(nc, name, start=FIRST, software_dma=("got", "put"), halves=None, w1=2, w3=2, w2=2, idx=None,
                   got=2, x_turned=None, x_in=None, h1=None, h3=None, silu=None, hid=None, h_turned=None,
                   h_in=None, y=None, y_out=None, current=None, go=None, put=2) as (block, s):
            trips = lambda eng: eng.value_load(n_pairs, min_val=1, max_val=MAX_BLOCKS // 2)

            @block.sync
            def _(sp):
                sp.dma_start(hv[:], halves).then_inc(s["halves"], 16)
                with sp.Fori(0, trips(sp)) as i:
                    for p in range(2):
                        e = sp.value_load(block_expert[:, ds(2 * i + p, 1)], min_val=0, max_val=N_EXPERTS - 1)
                        for w, wb, got, done in ((w1, w1b, "w1", "h1"), (w3, w3b, "w3", "h3"), (w2, w2b, "w2", "y")):
                            sp.wait_ge(s[done], FIRST + 2 * i + p - 1)
                            sp.dma_start(wb[:, p], w[ds(e, 1)].rearrange("a (k p) n -> p (a k) n", p=P)).then_inc(s[got][p], 16)

            @block.gpsimd
            def _(pool):
                def indices(which, p, b):
                    pool.tensor_copy(current[:, which, p:p + 1], index[:, which, ds(b, 1)]).then_inc(s["current"], 1)

                def gather(p):
                    pool.indirect_dma_start(out=xg[:, p, :], out_offset=None, in_=x_rows,
                                            in_offset=bass.IndirectOffsetOnAxis(ap=current[:, 0, p:p + 1], axis=0)).then_inc(s["got"][p], 16)
                for h in range(2):
                    pool.dma_start(meta[h * CAP:(h + 1) * CAP], slots.rearrange("(b s) f -> s b f", s=CAP)).then_inc(s["put"][h], 16)
                pool.wait_ge(s["put"][0], 16)
                pool.wait_ge(s["put"][1], 16)
                pool.wait_ge(s["halves"], FIRST + 16)
                pool.tensor_tensor(index[:], meta[:, :, 0:2].rearrange("p b a -> p a b"), hv[:].unsqueeze(2).to_broadcast([P, 2, TB]), ALU.add).then_inc(s["idx"], 1)
                pool.wait_ge(s["idx"], FIRST + 1)
                for p in range(2):
                    indices(0, p, p)
                    pool.wait_ge(s["current"], FIRST + p + 1)
                    gather(p)
                with pool.Fori(0, trips(pool)) as i:
                    for p in range(2):
                        pool.wait_ge(s["x_turned"], FIRST + 2 * i + p + 1)
                        pool.sem_inc(s["go"], 1)
                        pool.wait_ge(s["got"][p], 16 * i + 16)
                        pool.sem_inc(s["go"], 1)
                        pool.wait_ge(s["put"][p], 16 * i + 16)
                        pool.sem_inc(s["go"], 1)
                        indices(0, p, 2 * i + p + 2)
                        indices(1, p, 2 * i + p)
                        pool.wait_ge(s["current"], FIRST + 2 + 4 * i + 2 * p + 2)
                        pool.sem_inc(s["go"], 1)
                        gather(p)
                        pool.wait_ge(s["y_out"], FIRST + 2 * i + p + 1)
                        pool.sem_inc(s["go"], 1)
                        pool.wait_ge(s["put"][1 - p], 16 * (i + p) + 16)
                        pool.sem_inc(s["go"], 1)
                        pool.indirect_dma_start(out=y_rows, out_offset=bass.IndirectOffsetOnAxis(ap=current[:, 1, p:p + 1], axis=0),
                                                in_=yb[:, p, :], in_offset=None).then_inc(s["put"][p], 16)
                pairs = trips(pool)
                for p in range(2):
                    pool.wait_ge(s["got"][p], 16 * pairs + 16)
                    pool.sem_inc(s["go"], 1)
                    pool.wait_ge(s["put"][p], 16 * pairs + 16)
                    pool.sem_inc(s["go"], 1)

            @block.tensor
            def _(pe):
                def turn_x(p, i):
                    pe.wait_ge(s["got"][p], 16 * i + 16)
                    for j in range(4):
                        last = pe.transpose(px[:, j * P:(j + 1) * P], xg[:, p, j * P:(j + 1) * P], m["ident"])
                    last.then_inc(s["x_turned"], 1)
                turn_x(0, 0)
                with pe.Fori(0, trips(pe)) as i:
                    for p in range(2):
                        b = 2 * i + p
                        pe.wait_ge(s["x_in"], FIRST + b + 1)
                        for got, wb, out, done, used in (("w1", w1b, p1, "h1", "silu"), ("w3", w3b, p3, "h3", "hid")):
                            pe.wait_ge(s[got][p], FIRST + 16 * i + 16)
                            pe.wait_ge(s[used], FIRST + b)
                            for k in range(DK):
                                x = xT[:, k % 4, (k // 4) * CAP:(k // 4 + 1) * CAP]
                                for h in range(2):
                                    last = pe.matmul(out[h * CAP:(h + 1) * CAP, 0:H2], x, wb[:, p, k, h * H2:(h + 1) * H2],
                                                     start=(k == 0), stop=(k == DK - 1))
                            last.then_inc(s[done], 1)
                        turn_x(1 - p, i + p)
                        pe.wait_ge(s["hid"], FIRST + b + 1)
                        for j in range(2):
                            last = pe.transpose(ph[:, j * P:(j + 1) * P], hid[:, j * P:(j + 1) * P], m["ident"])
                        last.then_inc(s["h_turned"], 1)
                        pe.wait_ge(s["w2"][p], FIRST + 16 * i + 16)
                        pe.wait_ge(s["h_in"], FIRST + b + 1)
                        pe.wait_ge(s["y_out"], FIRST + b)
                        for f in range(FK):
                            x = hT[:, f % 2, (f // 2) * CAP:(f // 2 + 1) * CAP]
                            for h in range(2):
                                last = pe.matmul(py[h * CAP:(h + 1) * CAP, :], x, w2b[:, p, f, h * 512:(h + 1) * 512],
                                                 start=(f == 0), stop=(f == FK - 1))
                        last.then_inc(s["y"], 1)

            @block.scalar
            def _(act):
                with act.Fori(0, trips(act)) as i:
                    for p in range(2):
                        b = 2 * i + p
                        act.wait_ge(s["h1"], FIRST + b + 1)
                        act.wait_ge(s["hid"], FIRST + b)
                        act.activation(sact[:], p1[:, 0:H2], ACT.Silu).then_inc(s["silu"], 1)
                        act.wait_ge(s["y"], FIRST + b + 1)
                        act.wait_ge(s["put"][p], 16 * i + 16)
                        act.activation(yb[:, p, :], py[:], ACT.Copy,
                                       scale=meta[:].bitcast(F32)[:, ds(b, 1), 2]).then_inc(s["y_out"], 1)

            @block.vector
            def _(dve):
                gain = m["g_ffn"].rearrange("p (h j) -> p j h", h=2).unsqueeze(3).to_broadcast([P, 4, 2, CAP])

                def take_x(b):
                    dve.wait_ge(s["x_turned"], FIRST + b + 1)
                    dve.wait_ge(s["h3"], FIRST + b)
                    dve.tensor_tensor(xT[:].rearrange("p j (h q) -> p j h q", h=2),
                                      px[:].rearrange("p (j h q) -> p j h q", j=4, h=2), gain, ALU.mult).then_inc(s["x_in"], 1)
                take_x(0)
                with dve.Fori(0, trips(dve)) as i:
                    for p in range(2):
                        b = 2 * i + p
                        dve.wait_ge(s["silu"], FIRST + b + 1)
                        dve.wait_ge(s["h3"], FIRST + b + 1)
                        dve.wait_ge(s["h_turned"], FIRST + b)
                        dve.tensor_tensor(hid[:], p3[:, 0:H2], sact[:], ALU.mult).then_inc(s["hid"], 1)
                        take_x(b + 1)
                        dve.wait_ge(s["h_turned"], FIRST + b + 1)
                        dve.wait_ge(s["y"], FIRST + b)
                        dve.tensor_copy(hT[:].rearrange("p j q -> p (j q)"), ph[:, 0:2 * P]).then_inc(s["h_in"], 1)


def add_experts(nc, name, ys, h):
    with ExitStack() as c:
        y = c.enter_context(nc.sbuf_tensor(f"{name}_y", [P, XT, 2, D], F32))
        with stage(nc, name, loaded=XT, chain=None) as (block, s):
            @block.sync
            def _(sp):
                for t in range(XT):
                    sp.dma_start(y[:, t], ys[0:2 * SEQ, :].rearrange("(x t p) d -> t p x d", p=P, x=2)[t]).then_inc(s["loaded"][t], 16)

            @block.vector
            def _(dve):
                chain = Chain(dve, s["chain"])
                for t in range(XT):
                    dve.wait_ge(s["loaded"][t], 16)
                    for x in range(2):
                        chain(dve.tensor_tensor(h[:, t], h[:, t], y[:, t, x], ALU.add))


def load(nc, name, pairs):
    with stage(nc, name, sp_in=None, act_in=None) as (block, s):
        @block.sync
        def _(sp):
            for out, in_ in pairs[0::2]:
                sp.dma_start(out, in_).then_inc(s["sp_in"], 16)
            sp.wait_ge(s["sp_in"], 16 * len(pairs[0::2]))

        if len(pairs) > 1:
            @block.scalar
            def _(act):
                for out, in_ in pairs[1::2]:
                    act.dma_start(out, in_).then_inc(s["act_in"], 16)
                act.wait_ge(s["act_in"], 16 * len(pairs[1::2]))


def sub_norm(nc, name, m, o, heads):
    with ExitStack() as c:
        sb = lambda n, s: c.enter_context(nc.sbuf_tensor(f"{name}_{n}", s, F32))
        half, root, inv, sq, g = sb("half", [P, SEQ]), sb("root", [P, SEQ]), sb("inv", [P, SEQ]), sb("sq", [P, heads, SEQ]), sb("g", [P, 1])
        sums = c.enter_context(nc.psum_tensor(f"{name}_sums", [P, SEQ], F32))
        wide = c.enter_context(nc.psum_tensor(f"{name}_wide", [P, heads, SEQ], F32))
        R = P // heads
        with stage(nc, name, sq=None, summed=None, rooted=None, inverted=None, spread=None, chain=None) as (block, s):
            @block.scalar
            def _(act):
                for h in range(heads):
                    act.activation(sq[:, h], o[:, h], ACT.Square).then_inc(s["sq"], 1)
                act.wait_ge(s["summed"], heads)
                act.activation(root[:], sums[:], ACT.Sqrt, bias=m["eps"], scale=1.0 / P).then_inc(s["rooted"], 1)

            @block.tensor
            def _(pe):
                for h in range(heads):
                    pe.wait_ge(s["sq"], h + 1)
                    pe.matmul(sums[h * R:(h + 1) * R], m["ones"][:, 0:R], sq[:, h], start=True, stop=True).then_inc(s["summed"], 1)
                pe.wait_ge(s["inverted"], 1)
                for h in range(heads):
                    pe.matmul(wide[:, h], m["ident"][:, R * h:R * h + 1].to_broadcast([P, P]), inv[:], start=True, stop=True).then_inc(s["spread"], 1)

            @block.vector
            def _(dve):
                chain = Chain(dve, s["chain"])
                chain(dve.tensor_scalar(g[:], m["g_sub"], 1.0 - LAM_INIT, None, ALU.mult))
                dve.wait_ge(s["rooted"], 1)
                inverse_root(dve, chain, sums[:], root[:], P, half[:], inv[:]).then_inc(s["inverted"], 1)
                for h in range(heads):
                    dve.wait_ge(s["spread"], h + 1)
                    chain(dve.scalar_tensor_tensor(out=o[:, h], in0=o[:, h], scalar=g[:], in1=wide[:, h], op0=ALU.mult, op1=ALU.mult))


def add_side(nc, name, m, g_ple, y, gate, h):
    with ExitStack() as c:
        sb = lambda n, s: c.enter_context(nc.sbuf_tensor(f"{name}_{n}", s, F32))
        sq, st, wide = sb("sq", [P, D]), sb("st", [P, 4, XT]), sb("g", [P, D])
        with stage(nc, name, chain=None, act_chain=None, rooted=None, loaded=None) as (block, s):
            @block.sync
            def _(sp):
                sp.dma_start(wide[:], g_ple).then_inc(s["loaded"], 16)

            @block.scalar
            def _(act):
                chain = Chain(act, s["act_chain"])
                for t in range(XT):
                    chain(act.activation(sq[:], y[:, t], ACT.Square, accum_out=st[:, 0, t:t + 1]))
                act.activation(st[:, 1], st[:, 0], ACT.Sqrt, bias=m["eps"], scale=1.0 / D).then_inc(s["rooted"], 1)

            @block.vector
            def _(dve):
                chain = Chain(dve, s["chain"])
                dve.wait_ge(s["loaded"], 16)
                chain(dve.tensor_tensor(gate, gate, wide[:].unsqueeze(1).to_broadcast([P, XT, D]), ALU.mult))
                dve.wait_ge(s["rooted"], 1)
                chain(inverse_root(dve, chain, st[:, 0], st[:, 1], D, st[:, 3], st[:, 2]))
                for t in range(XT):
                    chain(dve.scalar_tensor_tensor(out=gate[:, t], in0=y[:, t], scalar=st[:, 2, t:t + 1], in1=gate[:, t], op0=ALU.mult, op1=ALU.mult))
                    chain(dve.tensor_tensor(h[:, t], h[:, t], gate[:, t], ALU.add))


def store_to(dst, width):
    return lambda eng, is_act, t, c, ps, tmp, chain: copy(eng, is_act, dst[:, t, ds(c * width, width)], ps)


def add_to(h):
    return lambda eng, is_act, t, c, ps, tmp, chain: eng.tensor_tensor(h[:, t, ds(c * 512, 512)], h[:, t, ds(c * 512, 512)], ps, ALU.add)


def add_gated(h, gate):
    def emit(eng, is_act, t, c, ps, tmp, chain):
        chain(eng.tensor_tensor(tmp, ps, gate[:, 0 if t < XT else 1, ds(c * 512, 512)], ALU.mult))
        dst = h[:, t, ds(c * 512, 512)]
        return eng.tensor_tensor(dst, dst, tmp, ALU.add)
    return emit


def tokens_of(a):
    return lambda k, t: a[:, k, t * P:(t + 1) * P]


def build(nc, A, prm_at, const_at):
    with ExitStack() as top:
        def sb(c, name, shape, dt=F32):
            return c.enter_context(nc.sbuf_tensor(name, shape, dt))

        prm = sb(top, "params", [P, sum(n for _, n in prm_at.values())])
        cst = sb(top, "consts", [P, sum(n for _, n in const_at.values())])
        m = {k: prm[:, a:a + n] for k, (a, n) in prm_at.items()}
        m.update({k: cst[:, a:a + n] for k, (a, n) in const_at.items()})
        hx = sb(top, "residual", [P, AT, D])
        tc, tsn, tk = sb(top, "l1_tc", [P, XT, 96]), sb(top, "l1_ts", [P, XT, 32]), sb(top, "l1_tk", [P, 2, AT, 32])
        tkn = sb(top, "l1_tkn", [P, 1, 64])
        of_layer_2 = ExitStack()
        mods = [[sb(c, f"{n}_gain", [P, AT, DK]), sb(c, f"{n}_shift", [P, AT, DK]), sb(c, f"{n}_gate", [P, conds, D])]
                for c, n, conds in ((top, "l1", 1), (of_layer_2, "l0", 2))][::-1]
        tabs_2 = sb(of_layer_2, "l0_tabs", [P, 4, AT, 64])
        rows = lambda v: v.rearrange("(t p) d -> p t d", p=P)
        tiles = lambda v, w: v.rearrange("p (t w) -> p t w", w=w)
        table = nc.dram_tensor("bias_rows", [CB, NA_HEADS, (2 * WIN_R - 1) * 3 * CB], F32).ap()
        slots = nc.dram_tensor("slots", [(MAX_BLOCKS + 2) * CAP, 4], I32).ap()
        xn = nc.dram_tensor("expert_in", [SEQ, D], F32).ap()
        ys = nc.dram_tensor("expert_out", [2 * SEQ + CAP, D], F32).ap()

        load(nc, "load", [(prm[:], A["params"]), (cst[:], A["consts"]),
                          (hx[:, 0:XT], rows(A["x"])), (hx[:, XT:AT], rows(A["ctx"]))])

        with ExitStack() as c:
            oT = sb(c, "mix_out", [P, DK, SEQ])
            with ExitStack() as cc:
                proj = sb(cc, "mix_proj", [P, XT, 3 * D])
                tabs = sb(cc, "mix_tabs", [P, 4, XT, 64])
                gains = sb(cc, "mix_gains", [P, 2, 1, NA_D])
                neg_lam = sb(cc, "neg_lam", [P, 1])
                ones = m["ones"][:, 0:64].unsqueeze(1)
                scale_a, scale_b, scale_2, scale_3 = 64 ** -0.5, NA_D ** -0.5, 64 ** -0.5, 96 ** -0.5
                scaled = [
                    (tabs[:, 0], tiles(m["full_cos"], 64), m["g_qa"], None, scale_a), (tabs[:, 1], tiles(m["full_sin"], 64), m["g_qa"], 1, scale_a),
                    (tabs[:, 2], tiles(m["full_cos"], 64), m["g_ka"], None, 1.0), (tabs[:, 3], tiles(m["full_sin"], 64), m["g_ka"], 1, 1.0),
                    (gains[:, 0], ones[:, :, 0:NA_D], m["g_qb"], None, scale_b), (gains[:, 1], ones[:, :, 0:NA_D], m["g_kb"], None, 1.0),
                    (tabs_2[:, 0], tiles(m["ax_cos"], 64), m["gqa_q"], None, scale_2), (tabs_2[:, 1], tiles(m["ax_sin"], 64), m["gqa_q"], 2, scale_2),
                    (tabs_2[:, 2], tiles(m["ax_cos"], 64), m["gqa_k"], None, 1.0), (tabs_2[:, 3], tiles(m["ax_sin"], 64), m["gqa_k"], 2, 1.0),
                    (tc[:, :, 0:64], ones.to_broadcast([P, XT, 64]), m["mla_q"][:, 0:64], None, scale_3),
                    (tc[:, :, 64:96], tiles(m["mla_cos"], 32)[:, 0:XT], m["mla_q"][:, 64:96], None, scale_3),
                    (tsn[:], tiles(m["mla_sin"], 32)[:, 0:XT], m["mla_q"][:, 64:96], 2, scale_3),
                    (tk[:, 0], tiles(m["mla_cos"], 32), m["mla_kr"], None, 1.0), (tk[:, 1], tiles(m["mla_sin"], 32), m["mla_kr"], 2, 1.0),
                    (tkn[:], ones, m["mla_kn"], None, 1.0)]
                with ExitStack() as ca:
                    aT = sb(ca, "mix_in", [P, DK, SEQ])
                    norm_transpose(nc, "mix_norm", m, lambda t: hx[:, t, :], DK, XT, m["g_mix"], None, aT)
                    with preparations(nc, "prep", m, A["rpb"], table, neg_lam[:], scaled) as beside:
                        dense(nc, "mix_in_w", tokens_of(aT), DK, XT, A["w_in"], 6, 512, store_to(proj, 512), beside=beside)
                def part(col, n, d):
                    return lambda t: proj[:, ds(t, 1), col:col + n * d].rearrange("p a (h d) -> p (a h) d", d=d)

                def row(tab):
                    return lambda t: tab[:, ds(t, 1), :].rearrange("p a d -> p (a d)")
                adaln = modulations(nc, "mod", m, [
                    (A["l0_w_mod"], m["l0_b"], A["l0_b_gate"], m["l0_norm"], *mods[0], 2),
                    (A["l1_w_mod"], m["l1_b"], A["l1_b_gate"], m["l1_norm"], *mods[1], 1)])
                with adaln as beside:
                    head_norms(nc, "mix_hn", m, XT, [
                        (part(0, 8, 64), 8, 64, row(tabs[:, 0]), (0, 1, 32, row(tabs[:, 1]))),
                        (part(512, 8, 64), 8, 64, row(tabs[:, 2]), (0, 1, 32, row(tabs[:, 3]))),
                        (part(1536, 16, 32), 16, 32, lambda t: gains[:, 0, 0], None),
                        (part(2048, 16, 32), 16, 32, lambda t: gains[:, 1, 0], None)], beside)

                def group(col):
                    return lambda i, p, dst: [(dst if len(dst.shape) == 3 else dst[:, 0], proj[:, :, ds(col + (2 * i + p) * P, P)])]
                attention(nc, "diff", m, 2, [(t, 0, XT) for t in range(XT)], 2, P, group(0), group(512), group(1024),
                          lambda i, p: oT[:, ds(2 * i + p, 1), :].rearrange("p a t -> p (a t)"), combine=neg_lam[:])
                sub_norm(nc, "subn", m, oT[:, 0:4], 4)
                attention(nc, "near", m, 2, [(t, max(t - 1, 0), min(t + 2, XT)) for t in range(XT)], 4, NA_D,
                          group(1536), group(2048), group(2560),
                          lambda i, p: oT[:, ds(4 + 2 * i + p, 1), :].rearrange("p a t -> p (a t)"), bias=table,
                          spare=proj[:, :, 0:4 * 3 * P])
            dense(nc, "mix_out_w", tokens_of(oT), DK, XT, A["w_out"], 2, 512, add_to(hx), by="dve")

        of_side = ExitStack()
        side = sb(of_side, "side", [P, XT, D])
        with ExitStack() as c:
            block_expert, n_pairs = sb(c, "block_expert", [P, MAX_BLOCKS], I32), sb(c, "n_pairs", [P, 1], I32)
            with ExitStack() as cc:
                aT = sb(cc, "ffn_in", [P, DK, SEQ])
                norm_transpose(nc, "ffn_norm", m, lambda t: hx[:, t, :], DK, XT, m["g_ffn"], None, aT,
                               spill=xn.rearrange("(t p) d -> t p d", p=P))
                pT = sb(cc, "side_in", [P, 2, SEQ])
                with route(nc, "route", m, aT, A["w_router"], A["slots_init"], A["slot_ids"], slots, block_expert[0:1, :], n_pairs[0:1, :],
                           (pT[:], A["p_t"].rearrange("(k p) t -> p k t", p=P))) as beside:
                    dense(nc, "side_w", tokens_of(pT), 2, XT, A["w_ple"], 2, 512, store_to(side, 512), by="act", beside=beside)
            expert_blocks(nc, "exp", m, block_expert[0:1, :], n_pairs[0:1, :], slots, A["halves"], xn, A["w1"], A["w3"], A["w2"], ys)
        add_experts(nc, "moe_add", ys, hx)

        with ExitStack() as c:
            sg = sb(c, "side_gate", [P, XT, D])
            with ExitStack() as cc:
                aT = sb(cc, "plg_in", [P, DK, SEQ])
                norm_transpose(nc, "plg_norm", m, lambda t: hx[:, t, :], DK, XT, m["g_plg"], None, aT)
                dense(nc, "plg_w", tokens_of(aT), DK, XT, A["w_plg"], 2, 512, by="act",
                      emit=lambda act, is_act, t, cidx, ps, tmp, chain: act.activation(sg[:, t, ds(cidx * 512, 512)], ps, ACT.Sigmoid))
            add_side(nc, "side_add", m, A["g_ple"], side, sg[:], hx)
        of_side.close()

        with ExitStack() as c:
            gain, shift, gate = mods[0]
            gT = sb(c, "l0_gT", [P, DK, AT * P])
            with ExitStack() as cc:
                proj = sb(cc, "l0_proj", [P, AT, 1536])
                def part2(col, n, d):
                    return lambda t: proj[:, ds(t, 1), col:col + n * d].rearrange("p a (h d) -> p (a h) d", d=d)

                def row2(tab):
                    return lambda t: tab[:, ds(t, 1), :].rearrange("p a d -> p (a d)")
                with ExitStack() as ca:
                    aT = sb(ca, "l0_in", [P, DK, AT * P])
                    norm_transpose(nc, "l0_n", m, lambda t: hx[:, t, :], DK, AT, gain, shift, aT)
                    dense(nc, "l0_w", tokens_of(aT), DK, AT, A["l0_w_in"], 3, 512, store_to(proj, 512))
                    with transposed_products(nc, "l0_g", aT, DK, AT * P, A["l0_w_in"], 1536, 2,
                                             lambda n, a, w: gT[:, n, a:a + w]) as beside:
                        head_norms(nc, "l0_hn", m, AT, [
                            (part2(512, 16, 64), 16, 64, row2(tabs_2[:, 0]), (0, 2, 16, row2(tabs_2[:, 1]))),
                            (part2(0, 4, 64), 4, 64, row2(tabs_2[:, 2]), (0, 2, 16, row2(tabs_2[:, 3])))], beside)
                attention(nc, "gqa", m, 4, [(t, 0, AT) for t in range(XT)] + [(t, XT, AT) for t in range(XT, AT)], 2, 64,
                          lambda i, p, dst: [(dst[:, 0], proj[:, :, ds(512 + (2 * i + p) * P, P)])],
                          lambda i, p, dst: [(dst[:, 0, :, x * 64:(x + 1) * 64], proj[:, :, ds(i * 64, 64)]) for x in range(2)],
                          lambda i, p, dst: [(dst[:, :, x * 64:(x + 1) * 64], proj[:, :, ds(256 + i * 64, 64)]) for x in range(2)],
                          lambda i, p: gT[:, ds(2 * i + p, 1), :].rearrange("p a t -> p (a t)"), gate=True,
                          tiles=AT, ktiles=AT)
            dense(nc, "l0_o", tokens_of(gT), DK, AT, A["l0_w_out"], 2, 512, add_gated(hx, gate), by="dve", links=1)
        of_layer_2.close()

        with ExitStack() as c:
            gain, shift, gate = mods[1]
            gT = sb(c, "l1_gT", [P, DK, SEQ])
            with ExitStack() as cc:
                latent, kv, q = sb(cc, "l1_latent", [P, AT, 288]), sb(cc, "l1_kv", [P, AT, 2048]), sb(cc, "l1_q", [P, XT, 1536])
                def row3(tab):
                    return lambda t: tab[:, ds(t, 1), :].rearrange("p a d -> p (a d)")
                with ExitStack() as ca:
                    aT = sb(ca, "l1_in", [P, DK, AT * P])
                    with ExitStack() as cd:
                        q_low = sb(cd, "l1_q_low", [P, XT, 384])
                        norm_transpose(nc, "l1_n", m, lambda t: hx[:, t, :], DK, AT, gain, shift, aT)
                        dense(nc, "l1_wk", tokens_of(aT), DK, AT, A["l1_w_in"], 1, 288, store_to(latent, 288))
                        dense(nc, "l1_wq", tokens_of(aT), DK, XT, A["l1_w_in"], 1, 384, store_to(q_low, 384), col0=288)
                        kvT, qaT = sb(cd, "l1_kvT", [P, 2, AT * P]), sb(cd, "l1_qaT", [P, 3, SEQ])
                        norm_transpose(nc, "l1_nkv", m, lambda t: latent[:, t, 0:256], 2, AT, m["kv_a_norm"], None, kvT)
                        norm_transpose(nc, "l1_nq", m, lambda t: q_low[:, t, :], 3, XT, m["q_a_norm"], None, qaT)
                        dense(nc, "l1_kvb", tokens_of(kvT), 2, AT, A["l1_w_kv_b"], 4, 512, store_to(kv, 512))
                        dense(nc, "l1_qb", tokens_of(qaT), 3, XT, A["l1_w_q_b"], 3, 512, store_to(q, 512))
                    gates = lambda z: transposed_products(nc, f"l1_g{z}", aT, DK, SEQ, A["l1_w_in"], 672 + z * 512, 1,
                                                          lambda n, a, w: gT[:, 4 * z + n, a:a + w])
                    with gates(0) as beside:
                        head_norms(nc, "l1_hq", m, XT, [
                            (lambda t: q[:, ds(t, 1), :].rearrange("p a (h d) -> p (a h) d", d=96), 16, 96, row3(tc), (64, 2, 8, row3(tsn)))], beside)
                    with gates(1) as beside:
                        head_norms(nc, "l1_hk", m, AT, [
                            (lambda t: kv[:, ds(t, 1), :].rearrange("p a (h d) -> p (a h) d", d=128)[:, :, 0:64], 16, 64, lambda t: tkn[:, 0], None),
                            (lambda t: latent[:, ds(t, 1), 256:288], 1, 32, row3(tk[:, 0]), (0, 2, 8, row3(tk[:, 1])))], beside)
                attention(nc, "mla", m, 4, [(t, 0, AT) for t in range(XT)], 2, 64,
                          lambda i, p, dst: [(dst[:, x], q[:, :, ds((4 * i + 2 * p + x) * 96, 96)]) for x in range(2)],
                          lambda i, p, dst: [e for x in range(2) for e in
                                             ((dst[:, x, :, 0:64], kv[:, :, ds((4 * i + 2 * p + x) * 128, 64)]), (dst[:, x, :, 64:96], latent[:, :, 256:288]))],
                          lambda i, p, dst: [(dst[:, :, x * 64:(x + 1) * 64], kv[:, :, ds((4 * i + 2 * p + x) * 128 + 64, 64)]) for x in range(2)],
                          lambda i, p: gT[:, ds(2 * i + p, 1), :].rearrange("p a t -> p (a t)"), gate=True, split=96,
                          tiles=XT, ktiles=AT)
            dense(nc, "l1_o", tokens_of(gT), DK, XT, A["l1_w_out"], 2, 512, add_gated(hx, gate), by="dve", links=1)
        load(nc, "store", [(rows(A["out"]), hx[:, 0:XT])])


def arrays(a):
    order = token_order()
    f = lambda k: np.ascontiguousarray(np.asarray(a[k]))
    prm_at, prm = parameters(a)
    const_at, cst = constants()
    init = slot_table()
    ins = dict(
        params=prm, consts=cst, x=f("x")[0][order], ctx=f("ctx_2")[0], p_t=f("p")[0, 0][order].T,
        rpb=f("rpb")[0], w_in=f("w_in")[0], w_out=f("w_out")[0],
        w_router=np.concatenate([f("w_rg")[0], f("w_re")[0]], 1),
        slots_init=np.concatenate([init, init[:2 * CAP]]), slot_ids=slot_ids(), halves=half_ids(),
        **wide_parameters(a), w1=f("w1")[0], w3=f("w3")[0], w2=f("w2")[0], w_plg=f("w_plg")[0], w_ple=f("w_ple")[0],
        l0_w_mod=f("l0_w_mod_2"), l0_w_in=f("l0_w_in_2"), l0_w_out=f("l0_w_out_2"),
        l1_w_mod=f("l1_w_mod_2"), l1_w_in=f("l1_w_in_2"), l1_w_kv_b=f("l1_w_kv_b_2"), l1_w_q_b=f("l1_w_q_b_2"),
        l1_w_out=f("l1_w_out_2"),
    )
    return {k: np.ascontiguousarray(v) for k, v in ins.items()}, prm_at, const_at


def kernel(**inputs):
    import concourse.bacc as bacc
    from concourse.bass_utils import run_bass_kernel_spmd

    ins, prm_at, const_at = arrays(inputs)
    nc = bacc.Bacc("TRN2", target_bir_lowering=False, num_devices=1)
    A = {k: nc.dram_tensor(f"in_{k}", v.shape, mybir.dt.from_np(v.dtype), kind="ExternalInput").ap() for k, v in ins.items()}
    A["out"] = nc.dram_tensor("out", (SEQ, D), F32, kind="ExternalOutput").ap()
    build(nc, A, prm_at, const_at)
    r = run_bass_kernel_spmd(nc, [{f"in_{k}": v for k, v in ins.items()}], core_ids=[0])
    got = np.asarray(r.results[0]["out"])
    out = np.empty_like(got)
    out[token_order()] = got
    return out.reshape(1, SEQ, D)
```
